# Optimizing a Trainium2 kernel written in Bass

```python
import math
import jax, jax.numpy as jnp
from jax import lax
import numpy as np

"""Hybrid decoder trunk with parallel head groups (Hymba-style).

Each layer: RMSNorm -> one combined input projection whose columns are partitioned among
  (A) differential attention (4 heads, two softmax maps per head, T5 relative bias),
  (B) Conformer convolution module (GLU -> causal depthwise conv w=31 -> LayerNorm -> swish),
  (C) S5-style complex-diagonal SSM (16 channel groups x 64 complex states, ZOH, associative scan, GLU),
concatenated over head groups -> one output projection -> residual add;
then RMSNorm -> hierarchical MoE (top-1 of 4 groups, top-2 of 8 experts in the group) -> residual add.
Final RMSNorm.
Input x: (BATCH, SEQ, D_MODEL) float32. Output: (BATCH, SEQ, D_MODEL).
"""

D_MODEL = 1024
BATCH = 1
SEQ = 1024
DEPTH = 1

ATTN_HEADS = 4
ATTN_QK_DIM = 64
ATTN_V_DIM = 2 * ATTN_QK_DIM
ATTN_WIDTH = ATTN_HEADS * ATTN_V_DIM
QK_COLS = ATTN_HEADS * ATTN_QK_DIM
Q_BLOCK = 128
CONV_WIDTH = D_MODEL // 4
CONV_KERNEL = 31
SSM_WIDTH = D_MODEL // 4
SSM_GROUP = 16
SSM_GROUPS = SSM_WIDTH // SSM_GROUP
SSM_STATE = 64
MIX_WIDTH = ATTN_WIDTH + CONV_WIDTH + SSM_WIDTH
IN_COLS = 4 * QK_COLS + ATTN_WIDTH + 2 * CONV_WIDTH + SSM_WIDTH
REL_BUCKETS = 32
REL_MAX_EXACT = REL_BUCKETS // 2
REL_MAX_DIST = 128
N_EXPERT_GROUPS = 4
EXPERTS_PER_GROUP = 8
N_EXPERTS = N_EXPERT_GROUPS * EXPERTS_PER_GROUP
TOP_K_IN_GROUP = 2
EXPERT_FF = D_MODEL // 2
MOE_BLOCK = 256
RMS_EPS = 1e-6
LN_EPS = 1e-5

kernel_name = "hymba_diffattn_conformer_s5_hmoe"

def rms_norm(x, g):
    xf = x.astype(jnp.float32)
    y = xf * lax.rsqrt(jnp.mean(xf * xf, axis=-1, keepdims=True) + RMS_EPS)
    return (y * g.astype(jnp.float32)).astype(x.dtype)

def layer_norm(x, g, b):
    xf = x.astype(jnp.float32)
    mu = jnp.mean(xf, axis=-1, keepdims=True)
    var = jnp.mean(jnp.square(xf - mu), axis=-1, keepdims=True)
    y = (xf - mu) * lax.rsqrt(var + LN_EPS)
    return (y * g.astype(jnp.float32) + b.astype(jnp.float32)).astype(x.dtype)

def rel_bucket(rel):
    n = jnp.maximum(rel, 0)
    nf = jnp.maximum(n, 1).astype(jnp.float32)
    large = REL_MAX_EXACT + (jnp.log(nf / REL_MAX_EXACT) / math.log(REL_MAX_DIST / REL_MAX_EXACT)
                             * (REL_BUCKETS - REL_MAX_EXACT)).astype(jnp.int32)
    large = jnp.minimum(large, REL_BUCKETS - 1)
    return jnp.where(n < REL_MAX_EXACT, n, large)

def diff_attention(q1, q2, k1, k2, v, lam, rel_table):
    B, L, H, dk = q1.shape
    n_blk = L // Q_BLOCK
    scale = dk ** -0.5
    kpos = jnp.arange(L)

    def block(i):
        start = i * Q_BLOCK
        q1b = lax.dynamic_slice_in_dim(q1, start, Q_BLOCK, axis=1)
        q2b = lax.dynamic_slice_in_dim(q2, start, Q_BLOCK, axis=1)
        rel = (start + jnp.arange(Q_BLOCK))[:, None] - kpos[None, :]
        bias = jnp.transpose(rel_table[rel_bucket(rel)], (2, 0, 1)).astype(jnp.float32)
        causal = rel >= 0

        def probs(qb, k):
            s = jnp.einsum('bqhd,bkhd->bhqk', qb, k).astype(jnp.float32) * scale + bias
            return jax.nn.softmax(jnp.where(causal, s, -1e30), axis=-1)

        p = probs(q1b, k1) - lam * probs(q2b, k2)
        return jnp.einsum('bhqk,bkhd->bqhd', p.astype(v.dtype), v)

    out = lax.map(block, jnp.arange(n_blk))
    return jnp.moveaxis(out, 0, 1).reshape(B, L, H, v.shape[-1])

def conformer_conv(u, conv_w, conv_b, ln_g, ln_b):
    a, gate = jnp.split(u, 2, axis=-1)
    h = a * jax.nn.sigmoid(gate)
    h = lax.conv_general_dilated(h, conv_w[:, None, :], window_strides=(1,),
                                 padding=[(CONV_KERNEL - 1, 0)],
                                 dimension_numbers=('NWC', 'WIO', 'NWC'),
                                 feature_group_count=CONV_WIDTH) + conv_b
    h = layer_norm(h, ln_g, ln_b)
    return jax.nn.silu(h)

def _ssm_combine(e1, e2):
    ar1, ai1, br1, bi1 = e1
    ar2, ai2, br2, bi2 = e2
    ar = ar2 * ar1 - ai2 * ai1
    ai = ar2 * ai1 + ai2 * ar1
    br = ar2 * br1 - ai2 * bi1 + br2
    bi = ar2 * bi1 + ai2 * br1 + bi2
    return (ar, ai, br, bi)

def s5_ssm(u, lam_re, lam_im, log_dt, b_re, b_im, c_re, c_im, d, glu_w, glu_b):
    f32 = jnp.float32
    Bsz, L, _ = u.shape
    uf = u.astype(f32).reshape(Bsz, L, SSM_GROUPS, SSM_GROUP)
    dt = jnp.exp(log_dt.astype(f32))[:, None]
    lr, li = lam_re.astype(f32), lam_im.astype(f32)
    mag = jnp.exp(lr * dt)
    ar, ai = mag * jnp.cos(li * dt), mag * jnp.sin(li * dt)
    den = lr * lr + li * li
    zr = ((ar - 1.0) * lr + ai * li) / den
    zi = (ai * lr - (ar - 1.0) * li) / den
    bre, bim = b_re.astype(f32), b_im.astype(f32)
    bbr = zr[..., None] * bre - zi[..., None] * bim
    bbi = zr[..., None] * bim + zi[..., None] * bre
    bu_re = jnp.einsum('blgh,gph->blgp', uf, bbr)
    bu_im = jnp.einsum('blgh,gph->blgp', uf, bbi)
    a_re = jnp.broadcast_to(ar, (1, L, SSM_GROUPS, SSM_STATE))
    a_im = jnp.broadcast_to(ai, (1, L, SSM_GROUPS, SSM_STATE))
    _, _, x_re, x_im = lax.associative_scan(_ssm_combine, (a_re, a_im, bu_re, bu_im), axis=1)
    y = (jnp.einsum('blgp,ghp->blgh', x_re, c_re.astype(f32))
         - jnp.einsum('blgp,ghp->blgh', x_im, c_im.astype(f32))
         + uf * d.astype(f32).reshape(SSM_GROUPS, SSM_GROUP))
    g = jax.nn.gelu(y.reshape(Bsz, L, SSM_WIDTH))
    out = g * jax.nn.sigmoid(g @ glu_w.astype(f32) + glu_b.astype(f32))
    return out.astype(u.dtype)

def hierarchical_moe(h, gw, gb, ew, eb, w_gate, w_up, w_down):
    f32 = jnp.float32
    T, D = h.shape
    g_logits = (h @ gw).astype(f32) + gb.astype(f32)
    g_prob = jax.nn.softmax(g_logits, axis=-1)
    g_idx = jnp.argmax(g_logits, axis=-1)
    g_p = jnp.take_along_axis(g_prob, g_idx[:, None], axis=1)
    e_logits = ((h @ ew).astype(f32) + eb.astype(f32)).reshape(T, N_EXPERT_GROUPS, EXPERTS_PER_GROUP)
    e_logits = jnp.take_along_axis(e_logits, g_idx[:, None, None], axis=1)[:, 0]
    top_v, top_i = lax.top_k(e_logits, TOP_K_IN_GROUP)
    gate = g_p * jax.nn.softmax(top_v, axis=-1)
    expert = g_idx[:, None].astype(jnp.int32) * EXPERTS_PER_GROUP + top_i.astype(jnp.int32)
    S = T * TOP_K_IN_GROUP
    flat_e = expert.reshape(S)
    flat_tok = jnp.repeat(jnp.arange(T, dtype=jnp.int32), TOP_K_IN_GROUP)
    flat_w = gate.reshape(S)
    order = jnp.argsort(flat_e)
    se, st, sw = flat_e[order], flat_tok[order], flat_w[order]
    counts = jnp.bincount(flat_e, length=N_EXPERTS)
    padded = (counts + MOE_BLOCK - 1) // MOE_BLOCK * MOE_BLOCK
    start = jnp.cumsum(counts) - counts
    pend = jnp.cumsum(padded)
    pstart = pend - padded
    dest = pstart[se] + jnp.arange(S) - start[se]
    n_blocks = -(-S // MOE_BLOCK) + N_EXPERTS
    P = n_blocks * MOE_BLOCK
    tok_pad = jnp.full((P,), T, jnp.int32).at[dest].set(st)
    w_pad = jnp.zeros((P,), f32).at[dest].set(sw)
    blk_e = jnp.minimum(jnp.searchsorted(pend, jnp.arange(n_blocks) * MOE_BLOCK, side='right'),
                        N_EXPERTS - 1)
    h_ext = jnp.concatenate([h, jnp.zeros((1, D), h.dtype)], axis=0)

    def expert_block(args):
        tok, e = args
        xb = h_ext[tok]
        act = jax.nn.silu(xb @ w_gate[e]) * (xb @ w_up[e])
        return act @ w_down[e]

    yb = lax.map(expert_block, (tok_pad.reshape(n_blocks, MOE_BLOCK), blk_e))
    yb = yb.reshape(P, D) * w_pad[:, None].astype(h.dtype)
    return jnp.zeros((T + 1, D), h.dtype).at[tok_pad].add(yb)[:T]

def setup_inputs(seed: int = 0) -> dict:
    key = jax.random.key(seed)
    ks = iter(jax.random.split(key, 48))
    f32 = jnp.float32

    def nrm(shape, scale):
        return scale * jax.random.normal(next(ks), shape, f32)

    G, P, H = SSM_GROUPS, SSM_STATE, SSM_GROUP
    n_idx = jnp.arange(P, dtype=f32)
    return {
        "x": nrm((BATCH, SEQ, D_MODEL), 1.0),
        "rel_bias": nrm((REL_BUCKETS, ATTN_HEADS), 0.1),
        "ln1_g": 1.0 + nrm((DEPTH, D_MODEL), 0.02),
        "w_in": nrm((DEPTH, D_MODEL, IN_COLS), D_MODEL ** -0.5),
        "lam_q1": nrm((DEPTH, ATTN_QK_DIM), 0.1),
        "lam_k1": nrm((DEPTH, ATTN_QK_DIM), 0.1),
        "lam_q2": nrm((DEPTH, ATTN_QK_DIM), 0.1),
        "lam_k2": nrm((DEPTH, ATTN_QK_DIM), 0.1),
        "subln_g": 1.0 + nrm((DEPTH, ATTN_V_DIM), 0.02),
        "conv_w": nrm((DEPTH, CONV_KERNEL, CONV_WIDTH), CONV_KERNEL ** -0.5),
        "conv_b": nrm((DEPTH, CONV_WIDTH), 0.02),
        "conv_ln_g": 1.0 + nrm((DEPTH, CONV_WIDTH), 0.02),
        "conv_ln_b": nrm((DEPTH, CONV_WIDTH), 0.02),
        "ssm_lam_re": -0.5 + nrm((DEPTH, G, P), 0.01),
        "ssm_lam_im": math.pi * n_idx + nrm((DEPTH, G, P), 0.01),
        "ssm_log_dt": jax.random.uniform(next(ks), (DEPTH, G), f32, math.log(1e-3), math.log(1e-1)),
        "ssm_b_re": nrm((DEPTH, G, P, H), (2 * H) ** -0.5),
        "ssm_b_im": nrm((DEPTH, G, P, H), (2 * H) ** -0.5),
        "ssm_c_re": nrm((DEPTH, G, H, P), P ** -0.5),
        "ssm_c_im": nrm((DEPTH, G, H, P), P ** -0.5),
        "ssm_d": nrm((DEPTH, SSM_WIDTH), 1.0),
        "ssm_glu_w": nrm((DEPTH, SSM_WIDTH, SSM_WIDTH), SSM_WIDTH ** -0.5),
        "ssm_glu_b": nrm((DEPTH, SSM_WIDTH), 0.02),
        "w_out": nrm((DEPTH, MIX_WIDTH, D_MODEL), MIX_WIDTH ** -0.5),
        "ln2_g": 1.0 + nrm((DEPTH, D_MODEL), 0.02),
        "group_router_w": nrm((DEPTH, D_MODEL, N_EXPERT_GROUPS), D_MODEL ** -0.5),
        "group_router_b": nrm((DEPTH, N_EXPERT_GROUPS), 0.01),
        "expert_router_w": nrm((DEPTH, D_MODEL, N_EXPERTS), D_MODEL ** -0.5),
        "expert_router_b": nrm((DEPTH, N_EXPERTS), 0.01),
        "w_gate": nrm((DEPTH, N_EXPERTS, D_MODEL, EXPERT_FF), D_MODEL ** -0.5),
        "w_up": nrm((DEPTH, N_EXPERTS, D_MODEL, EXPERT_FF), D_MODEL ** -0.5),
        "w_down": nrm((DEPTH, N_EXPERTS, EXPERT_FF, D_MODEL), EXPERT_FF ** -0.5),
        "final_g": 1.0 + nrm((D_MODEL,), 0.02),
    }

def reference(x, rel_bias, ln1_g, w_in, lam_q1, lam_k1, lam_q2, lam_k2, subln_g,
              conv_w, conv_b, conv_ln_g, conv_ln_b,
              ssm_lam_re, ssm_lam_im, ssm_log_dt, ssm_b_re, ssm_b_im, ssm_c_re, ssm_c_im,
              ssm_d, ssm_glu_w, ssm_glu_b, w_out, ln2_g,
              group_router_w, group_router_b, expert_router_w, expert_router_b,
              w_gate, w_up, w_down, final_g):
    B, L, D = x.shape
    splits = np.cumsum([QK_COLS, QK_COLS, QK_COLS, QK_COLS, ATTN_WIDTH, 2 * CONV_WIDTH]).tolist()
    for l in range(DEPTH):
        h = rms_norm(x, ln1_g[l])
        proj = h @ w_in[l]
        q1, q2, k1, k2, v, conv_in, ssm_in = jnp.split(proj, splits, axis=-1)
        q1, q2, k1, k2 = (t.reshape(B, L, ATTN_HEADS, ATTN_QK_DIM) for t in (q1, q2, k1, k2))
        v = v.reshape(B, L, ATTN_HEADS, ATTN_V_DIM)
        lam_init = 0.8 - 0.6 * math.exp(-0.3 * l)
        lam = (jnp.exp(jnp.sum(lam_q1[l].astype(jnp.float32) * lam_k1[l].astype(jnp.float32)))
               - jnp.exp(jnp.sum(lam_q2[l].astype(jnp.float32) * lam_k2[l].astype(jnp.float32)))
               + lam_init)
        a = diff_attention(q1, q2, k1, k2, v, lam, rel_bias)
        a = (rms_norm(a, subln_g[l]) * (1.0 - lam_init)).reshape(B, L, ATTN_WIDTH)
        c = conformer_conv(conv_in, conv_w[l], conv_b[l], conv_ln_g[l], conv_ln_b[l])
        s = s5_ssm(ssm_in, ssm_lam_re[l], ssm_lam_im[l], ssm_log_dt[l], ssm_b_re[l], ssm_b_im[l],
                   ssm_c_re[l], ssm_c_im[l], ssm_d[l], ssm_glu_w[l], ssm_glu_b[l])
        x = x + jnp.concatenate([a, c, s], axis=-1) @ w_out[l]
        h2 = rms_norm(x, ln2_g[l]).reshape(B * L, D)
        x = x + hierarchical_moe(h2, group_router_w[l], group_router_b[l], expert_router_w[l],
                                 expert_router_b[l], w_gate[l], w_up[l], w_down[l]).reshape(B, L, D)
    return rms_norm(x, final_g)


_drawn_inputs = setup_inputs


def setup_inputs(seed=0):
    import zlib

    import numpy as np

    out = dict(_drawn_inputs(seed))
    spreads = {}
    factors = {'subln_g': 9.376,
     'conv_b': 2.67,
     'conv_ln_g': 14.276,
     'conv_ln_b': 15.813,
     'ssm_lam_re': 200.0,
     'ssm_b_im': 88.424,
     'ssm_c_re': 101.4,
     'ssm_glu_b': 64.0,
     'group_router_b': 25.639,
     'expert_router_b': 19.473,
     'final_g': 20.889,
     'ssm_lam_im': 30.0,
     'ssm_log_dt': 35.192,
     'ssm_b_re': 64.0,
     'ssm_c_im': 64.0,
     'ln2_g': 4.487}
    for name, (base, spread) in spreads.items():
        noise = np.random.default_rng([zlib.crc32(name.encode()), seed]).standard_normal(out[name].shape)
        drawn = base * np.exp(spread * noise) if base else spread * noise
        out[name] = __import__('jax').numpy.asarray(drawn.astype(out[name].dtype))
    for name, factor in factors.items():
        out[name] = (out[name] * factor).astype(out[name].dtype)
    return out
```

```python
import math
from contextlib import ExitStack

import numpy as np

import concourse.bass as bass
import concourse.mybir as mybir
from concourse.mybir import ActivationFunctionType as ACT
from concourse.mybir import AluOpType as ALU
from concourse.mybir import AxisListType as AX

F32 = mybir.dt.float32
BF16 = mybir.dt.bfloat16
I32 = mybir.dt.int32
U32 = mybir.dt.uint32

P = 128
D = 1024
L = 1024
KD = D // P
NT = L // P
HEADS, DK, DV = 4, 64, 128
CH = 256
TAPS = 31
GROUPS, GCH, STATES = 16, 16, 64
PAIRS = GROUPS // 2
CHUNK = 8
NC = L // CHUNK
SCAN_STEPS = int(math.log2(NC))
COLS = 2304
WCH = 256
BUCKETS = 32
EXPERTS, EGROUPS, EPG, FF = 32, 4, 8, 512
FK = FF // P
NOVER = 2 * L // P - 1
NBLK = EXPERTS + NOVER
OOB = float(1 << 20)
RMS_EPS, LN_EPS = 1e-6, 1e-5
SCALE = DK ** -0.5
LAM_INIT = 0.8 - 0.6 * math.exp(0.0)
NEG = -1e30
TWO_PI = (6.28125, 0.0019350051879882812, 3.019915981956753e-07)
ROUND = 12582912.0
PI = 3.1415925

CHUNKS = [(2048, "ssm"), (1024, "v"), (1280, "v"), (1792, "gate"), (1536, "a"),
          (0, "qk"), (256, "qk"), (512, "qk"), (768, "qk")]


def units():
    out = []
    for c, (_, kind) in enumerate(CHUNKS):
        if kind in ("ssm", "v"):
            out += [(c, kind, i) for i in range(NT)]
        else:
            out += [(c, kind, i) for i in range(4)]
    return out


UNITS = units()
LAST_UNIT = {c: max(n for n, u in enumerate(UNITS) if u[0] == c) for c in range(len(CHUNKS))}

MISC_AT = {}
for _n, _job in enumerate([("conv_to_tok", i) for i in range(4)] + [("ssm_to_ch", i) for i in range(4)]
                          + [("conv_to_ch", i) for i in range(4)] + [("head", 0), ("head", 1)]
                          + [("glu", i) for i in range(4)]):
    MISC_AT.setdefault(_n, []).append(_job)
for _n, _job in ((20, 2), (21, 3), (28, 4), (29, 5)):
    MISC_AT.setdefault(_n, []).append(("head", _job))
ITEMS = [(h, i) for h in range(HEADS) for i in range(NT)]
NI = len(ITEMS)
ITERS = NI + 2
MISC_AT[ITERS + 1] = [("head", 6), ("head", 7)]
MISC_ORDER = [j for n in sorted(MISC_AT) for j in MISC_AT[n]]


def build(nc, t):
    with ExitStack() as ctx:
        def sb(name, shape, dt=F32):
            return ctx.enter_context(nc.sbuf_tensor(name, shape, dt))

        def sem(name):
            return ctx.enter_context(nc.semaphore(name))

        band_rows = nc.dram_tensor("band_rows", [HEADS, P, 384], F32, kind="Internal").ap()
        toep_rows = nc.dram_tensor("toep_rows", [GROUPS, GCH, 2 * P], F32, kind="Internal").ap()
        h2_dram = nc.dram_tensor("h2_rows", [L, D], F32, kind="Internal").ap()
        y2_dram = nc.dram_tensor("y2_rows", [2 * L, D], F32, kind="Internal").ap()

        RA = sb("RA", [P, 8192])
        RB = sb("RB", [P, 8192])
        RC = sb("RC", [P, 4096])
        RD = sb("RD", [P, 8192])
        RE = sb("RE", [P, 4096])
        RF = sb("RF", [P, 8192])
        RG = sb("RG", [P, 8192])

        hT = RA[:, :].rearrange("p (k n) -> p k n", k=KD)
        xt = RB[:, :].rearrange("p (t n) -> p t n", t=NT)
        qkT = RB[:, :].rearrange("p (c n) -> p c n", c=8)
        vtok = RC[:, :].rearrange("p (t n) -> p t n", t=NT)
        mixT = RD[:, :].rearrange("p (k n) -> p k n", k=KD)
        win = RF[:, 0:6144].rearrange("p (s k n) -> p s k n", s=3, k=KD)
        wout = RF[:, :].rearrange("p (k n) -> p k n", k=KD)
        x2 = RG[:, :].rearrange("p (t n) -> p t n", t=NT)

        convh = RF[:, 6144:8192].rearrange("p (c n) -> p c n", c=2)
        convt = RF[:, 6144:8192].rearrange("p (t n) -> p t n", t=NT)
        convo = RD[:, 4096:6144].rearrange("p (c n) -> p c n", c=2)
        ssmo = RD[:, 6144:8192].rearrange("p (c n) -> p c n", c=2)

        uc = RG[:, 0:2048].rearrange("p (g i h) -> p g i h", g=GROUPS, i=CHUNK)
        UT = RG[:, 2048:4096].rearrange("p (g c) -> p g c", g=GROUPS)
        XR = RG[:, 4096:5120].rearrange("p (a c) -> p a c", a=PAIRS)
        XI = RG[:, 5120:6144].rearrange("p (a c) -> p a c", a=PAIRS)
        yc = RG[:, 6144:8192].rearrange("p (j n) -> p j n", j=CHUNK)
        gT = RG[:, 4096:6144].rearrange("p (c n) -> p c n", c=2)
        glut = RG[:, 2048:4096].rearrange("p (c n) -> p c n", c=2)
        st = [RG[:, 6144:7168], RG[:, 7168:8192], RD[:, 6144:7168], RD[:, 7168:8192]]
        st = [s.rearrange("p (a c) -> p a c", a=PAIRS) for s in st]
        WinR = RE[:, 0:1024].rearrange("p (a s) -> p a s", a=PAIRS)
        WinI = RE[:, 1024:2048].rearrange("p (a s) -> p a s", a=PAIRS)
        TG = RE[:, 2048:4096].rearrange("p (g n) -> p g n", g=GROUPS)
        CAR = RD[:, 0:1152].rearrange("p (a t h) -> p a t h", a=PAIRS, t=9)
        CAI = RD[:, 1152:2304].rearrange("p (a t h) -> p a t h", a=PAIRS, t=9)
        VBR = RD[:, 6144:7168].rearrange("p (a i h) -> p a i h", a=PAIRS, i=CHUNK)
        VBI = RD[:, 7168:8192].rearrange("p (a i h) -> p a i h", a=PAIRS, i=CHUNK)
        s0 = 2304
        def scratch(n):
            nonlocal s0
            s0 += n
            assert s0 <= 4096
            return RD[:, s0 - n:s0]
        bre = scratch(128).rearrange("p (a h) -> p a h", a=PAIRS)
        bim = scratch(128).rearrange("p (a h) -> p a h", a=PAIRS)
        crow = scratch(256).rearrange("p (r s) -> p r s", r=2)
        BBR = scratch(128).rearrange("p (a h) -> p a h", a=PAIRS)
        BBI = scratch(128).rearrange("p (a h) -> p a h", a=PAIRS)
        PWR = scratch(72).rearrange("p (t a) -> p t a", a=PAIRS)
        PWI = scratch(72).rearrange("p (t a) -> p t a", a=PAIRS)
        RVR = scratch(64).rearrange("p (t a) -> p t a", a=PAIRS)
        RVI = scratch(64).rearrange("p (t a) -> p t a", a=PAIRS)
        sv = scratch(8 * 24).rearrange("p (n a) -> p n a", a=PAIRS)
        lrow = scratch(128)
        ctmp = scratch(256)
        lamv = RG[:, 6144:6400].rearrange("p (v n) -> p v n", v=4)
        onehot = RG[0:BUCKETS, 6400:6784]
        brow = RG[0:HEADS, 6784:7168]
        ksb = RG[:, 7168:8192].rearrange("p (q n) -> p q n", q=4)
        TMP4 = [RF[:, 6144:7168], RF[:, 7168:8192], RE[:, 2048:3072], RE[:, 3072:4096]]
        silu = RG[:, 0:2048].rearrange("p (i n) -> p i n", i=4)

        pexp = RE[:, :].rearrange("p (s n) -> p s n", s=4)
        xg = [RD[:, 0:1024], RD[:, 1024:2048]]
        xgT = RD[:, 2048:3072].rearrange("p (k n) -> p k n", k=KD)
        actb = RD[:, 4096:4608]
        actT = RD[:, 5120:5632].rearrange("p (k n) -> p k n", k=FK)
        yb = [RD[:, 6144:7168], RD[:, 7168:8192]]
        wgate = [RA[:, 0:4096].rearrange("p (k n) -> p k n", k=KD), RB[:, 0:4096].rearrange("p (k n) -> p k n", k=KD)]
        wup = [RA[:, 4096:8192].rearrange("p (k n) -> p k n", k=KD), RB[:, 4096:8192].rearrange("p (k n) -> p k n", k=KD)]
        wdown = [RE[:, :].rearrange("p (k n) -> p k n", k=FK), RC[:, :].rearrange("p (k n) -> p k n", k=FK)]
        r0 = 0
        def route(n):
            nonlocal r0
            r0 += n
            assert r0 <= 8192
            return RD[:, r0 - n:r0]
        slot1h = route(2048).rearrange("p (r n) -> p r n", r=16)
        blk1h = route(752).rearrange("p (r n) -> p r n", r=16)
        bval = route(2256).rearrange("p (r n v) -> p r n v", r=16, v=3)
        MM = route(512).rearrange("p (r n) -> p r n", r=16)
        MP = route(512).rearrange("p (r n) -> p r n", r=16)
        RK = route(256).rearrange("p (t n) -> p t n", t=NT)
        esel = route(256)
        rr = route(704)
        RR, _o = {}, 0
        for _name, _n in (("g8", 64), ("mx8", 64), ("e8", 64), ("me8", 64), ("gi8", 64), ("ei8", 64), ("gix", 8), ("goh", 32),
                          ("gsum", 8), ("den", 8), ("gp", 8), ("gexp", 32), ("gdif", 32), ("edif", 8), ("eexp", 8),
                          ("gate", 16), ("idx", 16), ("rk", 16), ("br_", 16), ("ovs", 16), ("blk", 16), ("dst", 16), ("tokm", 8)):
            RR[_name] = rr[:, _o:_o + _n]
            _o += _n
        assert _o <= 704

        def rrv(name, n=None):
            return RR[name]
        mbf = route(128).bitcast(BF16).rearrange("p (t n) -> p t n", t=NT)
        ovt = route(512)

        ident = sb("ident", [P, P])
        tri = sb("tri", [P, P], BF16)
        onesb = sb("onesb", [P, P], BF16)
        band = sb("band", [P, HEADS, 256])
        h2T = band[:, :, :].rearrange("p h n -> p (h n)").rearrange("p (k n) -> p k n", k=KD)
        xr = sb("xr", [P, 1024])
        pT = [xr[:, :].rearrange("p (k n) -> p k n", k=KD), RF[:, 5120:6144].rearrange("p (k n) -> p k n", k=KD)]
        g1 = sb("g1", [P, KD])
        g2k = sb("g2k", [P, KD])
        g2e = sb("g2e", [P, KD])
        rw = sb("rw", [P, KD, 36])
        rbias = sb("rbias", [P, 36])
        gluw = sb("gluw", [P, 2, CH])
        dbc = rw[:, :, :].rearrange("p k n -> p (k n)")[:, 0:CH]
        convw = sb("convw", [P, 2, TAPS])
        convb = sb("convb", [P, 2])
        lng = sb("lng", [P, 2])
        lnb = sb("lnb", [P, 2])
        glub = sb("glub", [P, 2])
        sg = sb("sg", [P, 1])
        b31 = sb("b31", [P, HEADS])
        relt = sb("relt", [BUCKETS, HEADS])
        nb31 = sb("nb31", [P, HEADS])
        lam = sb("lam", [P, 4])
        PDR = sb("PDR", [P, SCAN_STEPS, PAIRS])
        PDI = sb("PDI", [P, SCAN_STEPS, PAIRS])
        mhalf = sb("mhalf", [P, NT])
        ms = sb("ms", [P, NT])
        msv = sb("msv", [P, NT])
        rstd = sb("rstd", [P, NT])
        ms2 = sb("ms2", [P, NT])
        ms2v = sb("ms2v", [P, NT])
        rstd2 = sb("rstd2", [P, NT])
        ms3 = sb("ms3", [P, NT])
        ms3v = sb("ms3v", [P, NT])
        rstd3 = sb("rstd3", [P, NT])
        hss = sb("hss", [P, HEADS, NT])
        hssv = sb("hssv", [P, HEADS, NT])
        hrstd = sb("hrstd", [P, HEADS, NT])
        lnst = sb("lnst", [P, NT, 6])
        lnmv = sb("lnmv", [P, NT, 2])
        lnv = sb("lnv", [P, NT])
        lnr = sb("lnr", [P, NT])
        smx = sb("smx", [P, 2, 2, 8])
        logit = gluw[:, :, :].rearrange("p k n -> p (k n)")[:, 0:NT * 36].rearrange("p (t n) -> p t n", t=NT)
        iotai = RG[:, 0:128].bitcast(I32)
        iotaf = sb("iotaf", [P, P])
        thr = sb("thr", [P, 7])
        toki = RG[:, 128:136].bitcast(I32)
        tokf = sb("tokf", [P, NT])
        tabi = sb("tabi", [P, 2, NBLK], U32)
        tabg = sb("tabg", [P, NBLK])
        cur = sb("cur", [P, 4], U32)
        nov_i = sb("nov_i", [P, 16], I32)

        psum = ctx.enter_context(nc.psum_tensor("psum", [P, 8, 512], F32))
        def bank(i):
            return psum[:, i, :]
        def banks(i, n):
            return psum[:, i:i + n, :].rearrange("p b n -> p (b n)")

        x_in = [sem(f"x_in{i}") for i in range(NT)]
        win_in = [sem(f"win_in{i}") for i in range(3)]
        par_in = sem("par_in")
        set_in = sem("set_in")
        const_ok = sem("const_ok")
        act_c = sem("act_c")
        dve_c = sem("dve_c")
        pool_c = sem("pool_c")
        ms_ok = sem("ms_ok")
        msv_ok = sem("msv_ok")
        rstd_ok = sem("rstd_ok")
        xn_ok = sem("xn_ok")
        xT_ps = sem("xT_ps")
        hT_ok = sem("hT_ok")
        unit_ps = sem("unit_ps")
        unit_ev = sem("unit_ev")
        band_ps = sem("band_ps")
        band_row = sem("band_row")
        band_dram = sem("band_dram")
        band_in = sem("band_in")
        band_ok = sem("band_ok")
        lam_dot = sem("lam_dot")
        lam_exp = sem("lam_exp")
        lam_ok = sem("lam_ok")
        lrow_ps = sem("lrow_ps")
        ssm_dt = sem("ssm_dt")
        ssm_ang = sem("ssm_ang")
        ssm_sin = sem("ssm_sin")
        vb_ok = sem("vb_ok")
        ca_ok = sem("ca_ok")
        uT_ps = sem("uT_ps")
        uT_ev = sem("uT_ev")
        wi_ps = sem("wi_ps")
        wi_ev = sem("wi_ev")
        k_ps = sem("k_ps")
        k_ev = sem("k_ev")
        kz_ok = sem("kz_ok")
        toep_dram = sem("toep_dram")
        toep_in = sem("toep_in")
        vin_ps = sem("vin_ps")
        vin_ev = sem("vin_ev")
        scan_ok = sem("scan_ok")
        ud_ok = sem("ud_ok")
        y_ps = sem("y_ps")
        y_ev = sem("y_ev")
        gelu_ok = sem("gelu_ok")
        glu_half = sem("glu_half")
        ssm_ok = sem("ssm_ok")
        h_ok = sem("h_ok")
        tap_c = sem("tap_c")
        conv_ps = sem("conv_ps")
        conv_ev = sem("conv_ev")
        ln_var = sem("ln_var")
        ln_rstd = sem("ln_rstd")
        ln_ok = sem("ln_ok")
        silu_t = sem("silu_t")
        conv_ok = sem("conv_ok")
        s_ps = sem("s_ps")
        nm_ok = sem("nm_ok")
        e_ok = sem("e_ok")
        p_ok = sem("p_ok")
        pT_ps = sem("pT_ps")
        pT_ev = sem("pT_ev")
        o_ps = sem("o_ps")
        o_ev = sem("o_ev")
        misc_ps = sem("misc_ps")
        misc_ev = sem("misc_ev")
        head_ss = sem("head_ss")
        head_var = sem("head_var")
        head_rstd = sem("head_rstd")
        head_o = sem("head_o")
        rw_in = sem("rw_in")
        wout_in = [sem(f"wout_in{i}") for i in range(3)]
        xr_in = sem("xr_in")
        proj_ps = sem("proj_ps")
        x2_ok = sem("x2_ok")
        ms2_ok = sem("ms2_ok")
        ms2v_ok = sem("ms2v_ok")
        rstd2_ok = sem("rstd2_ok")
        h2_ok = sem("h2_ok")
        h2_out = sem("h2_out")
        h2T_ps = sem("h2T_ps")
        h2T_ok = sem("h2T_ok")
        lg_ps = sem("lg_ps")
        lg_ok = sem("lg_ok")
        gd_ok = sem("gd_ok")
        ge_ok = sem("ge_ok")
        mm_ok = sem("mm_ok")
        rank_ps = sem("rank_ps")
        tab_ok = sem("tab_ok")
        tab_ps = sem("tab_ps")
        idx_ok = sem("idx_ok")
        wgu_in = [sem(f"wgu_in{i}") for i in range(2)]
        wd_in = [sem(f"wd_in{i}") for i in range(2)]
        gather_in = [sem(f"gather_in{i}") for i in range(2)]
        cur_c = sem("cur_c")
        xg_z = sem("xg_z")
        ex_xT = sem("ex_xT")
        ex_xTe = sem("ex_xTe")
        ex_g = sem("ex_g")
        ex_u = sem("ex_u")
        ex_s = sem("ex_s")
        ex_a = sem("ex_a")
        ex_aT = sem("ex_aT")
        ex_aTe = sem("ex_aTe")
        ex_y = sem("ex_y")
        ex_y0 = sem("ex_y0")
        ex_y1 = sem("ex_y1")
        scat_out = [sem(f"scat_out{i}") for i in range(2)]
        ov_gu = sem("ov_gu")
        ov_d = sem("ov_d")
        ov_x = sem("ov_x")
        ov_cur = sem("ov_cur")
        ov_xT = sem("ov_xT")
        ov_xTe = sem("ov_xTe")
        ov_g = sem("ov_g")
        ov_u = sem("ov_u")
        ov_s = sem("ov_s")
        ov_a = sem("ov_a")
        ov_aT = sem("ov_aT")
        ov_aTe = sem("ov_aTe")
        ov_y = sem("ov_y")
        ov_y0 = sem("ov_y0")
        ov_y1 = sem("ov_y1")
        ov_out = sem("ov_out")
        moe_done = sem("moe_done")
        fg_in = sem("fg_in")
        y2_in = [sem(f"y2_in{i}") for i in range(4)]
        ya_ps = sem("ya_ps")
        x3_ok = sem("x3_ok")
        ms3_ok = sem("ms3_ok")
        ms3v_ok = sem("ms3v_ok")
        rstd3_ok = sem("rstd3_ok")
        fin_ok = sem("fin_ok")
        fin_c = sem("fin_c")
        fin_out = sem("fin_out")

        fgb = band[:, :, :].rearrange("p h n -> p (h n)")
        y2t = RF[:, :].rearrange("p (s r n) -> p s r n", s=4, r=2)

        def bc(ap, shape):
            return ap.to_broadcast(shape)

        def vec(name, **kw):
            return t[name].rearrange("o (k p) -> (o p) k", **kw)

        par_loads = [
            (g1[:, :], vec("ln1_g", p=P)),
            (relt[:, :], t["rel_bias"]),
            (onehot, t["bucket_onehot"]),
            (lrow[0:8, :], t["ssm_lam_re"][0].rearrange("(a q) s -> a (q s)", q=2)),
            (lrow[8:16, :], t["ssm_lam_im"][0].rearrange("(a q) s -> a (q s)", q=2)),
            (sv[0:64, 0, :], t["ssm_log_dt"].rearrange("o (a q) -> q (o a)", q=2)[0:1, :].to_broadcast([64, PAIRS])),
            (sv[64:128, 0, :], t["ssm_log_dt"].rearrange("o (a q) -> q (o a)", q=2)[1:2, :].to_broadcast([64, PAIRS])),
            (bre, t["ssm_b_re"][0].rearrange("(a q) s h -> (q s) a h", q=2)),
            (bim, t["ssm_b_im"][0].rearrange("(a q) s h -> (q s) a h", q=2)),
        ]
        for r, name in enumerate(("ssm_c_re", "ssm_c_im")):
            for a in range(PAIRS):
                par_loads.append((crow[GCH * a:GCH * (a + 1), r, :].rearrange("h (q s) -> h q s", q=2),
                                  t[name][0, 2 * a:2 * a + 2].rearrange("q h s -> h q s")))
        for v, name in enumerate(("lam_q1", "lam_k1", "lam_q2", "lam_k2")):
            par_loads.append((lamv[:, v, :], t[name].to_broadcast([P, DK])))
        set_loads = [
            (b31[:, :], t["rel_bias"][BUCKETS - 1:BUCKETS, :].to_broadcast([P, HEADS])),
            (dbc[:, :], t["ssm_d"].to_broadcast([P, CH])),
            (convb[:, :], vec("conv_b", p=P)),
            (lng[:, :], vec("conv_ln_g", p=P)),
            (lnb[:, :], vec("conv_ln_b", p=P)),
            (glub[:, :], vec("ssm_glu_b", p=P)),
            (sg[:, :], vec("subln_g", p=P)),
            (gluw[:, :, :], t["ssm_glu_w"][0].rearrange("(k p) n -> p k n", p=P)),
            (g2k[:, :], vec("ln2_g", p=P)),
            (g2e[:, :], t["ln2_g"].rearrange("o (p k) -> (o p) k", p=P)),
            (rbias[:, 0:4], t["group_router_b"].to_broadcast([P, EGROUPS])),
            (rbias[:, 4:36], t["expert_router_b"].to_broadcast([P, EXPERTS])),
        ]
        for c in range(2):
            set_loads.append((convw[:, c, :], t["conv_w"][0].rearrange("j (c p) -> p c j", p=P)[:, c, :]))
        SET_N = len(set_loads)
        PAR_N = len(par_loads)

        block = ctx.enter_context(nc.Block())

        @block.sync
        def _(sp):
            def load_chunk(c):
                src = t["w_in"][0, :, CHUNKS[c][0]:CHUNKS[c][0] + WCH].rearrange("(k p) n -> p k n", p=P)
                if c >= 3:
                    sp.wait_ge(unit_ps, LAST_UNIT[c - 3] + 1)
                sp.dma_start(win[:, c % 3], src).then_inc(win_in[c % 3], 16)

            for i in range(NT):
                sp.dma_start(xt[:, i, :], t["x"][0, i * P:(i + 1) * P, :]).then_inc(x_in[i], 16)
                if i in (1, 3, 5):
                    load_chunk(i // 2)
            sp.wait_ge(band_row, 1)
            sp.dma_start(band_rows, bc(brow[:, :].unsqueeze(1), [HEADS, P, 384])).then_inc(band_dram, 16)
            sp.wait_ge(band_dram, 16)
            sp.dma_start(band[:, :, :], bass.AP(tensor=band_rows.tensor, offset=P - 1,
                                                ap=[[383, P], [384 * P, HEADS], [1, 256]])).then_inc(band_in, 16)
            sp.wait_ge(k_ev, 1)
            sp.wait_ge(kz_ok, 1)
            for r in range(4):
                sp.dma_start(toep_rows.rearrange("(q r) h n -> r h q n", r=4)[r], ksb[32 * r:32 * r + GCH])\
                  .then_inc(toep_dram, 16)
            sp.wait_ge(toep_dram, 64)
            for i in range(CHUNK):
                src = bass.AP(tensor=toep_rows.tensor, offset=P - GCH * i,
                              ap=[[2 * P, GCH], [2 * P * GCH, GROUPS], [1, P]])
                sp.dma_start(TG[GCH * i:GCH * (i + 1)], src).then_inc(toep_in, 16)
            for c in range(3, len(CHUNKS)):
                load_chunk(c)
            sp.wait_ge(unit_ps, len(UNITS))
            wo = t["w_out"][0].rearrange("(k p) n -> p k n", p=P)
            sp.dma_start(wout[:, 0:5], wo[:, 0:5]).then_inc(wout_in[0], 16)

            def load_gu(s, e):
                sp.dma_start(wgate[s], t["w_gate"][0, e].rearrange("(p k) n -> p k n", p=P)).then_inc(wgu_in[s], 16)
                sp.dma_start(wup[s], t["w_up"][0, e].rearrange("(p k) n -> p k n", p=P)).then_inc(wgu_in[s], 16)

            def load_d(s, e):
                sp.dma_start(wdown[s], t["w_down"][0, e].rearrange("(p k) n -> p k n", p=P)).then_inc(wd_in[s], 16)

            load_gu(0, 0)
            sp.wait_ge(conv_ok, 4)
            sp.wait_ge(silu_t, 4)
            sp.dma_start(wout[:, 6:8], wo[:, 6:8]).then_inc(wout_in[2], 16)
            sp.wait_ge(o_ps, NI)
            sp.dma_start(wout[:, 5:6], wo[:, 5:6]).then_inc(wout_in[1], 16)
            load_d(0, 0)
            load_gu(1, 1)
            load_d(1, 1)
            wg = t["w_gate"][0].rearrange("e (p k) n -> e p k n", p=P)
            wu = t["w_up"][0].rearrange("e (p k) n -> e p k n", p=P)
            wd = t["w_down"][0].rearrange("e (p k) n -> e p k n", p=P)
            with sp.Fori(0, EXPERTS // 2 - 1) as j:
                for s in range(2):
                    e = sp.snap(j * 2 + 2 + s)
                    free = sp.snap(j * 2 + 1 + s)
                    sp.wait_ge(ex_u, free)
                    sp.dma_start(wgate[s], wg[bass.ds(e, 1)].rearrange("e p k n -> (e p) k n")).then_inc(wgu_in[s], 16)
                    sp.dma_start(wup[s], wu[bass.ds(e, 1)].rearrange("e p k n -> (e p) k n")).then_inc(wgu_in[s], 16)
                    sp.wait_ge(ex_y, free)
                    sp.dma_start(wdown[s], wd[bass.ds(e, 1)].rearrange("e p k n -> (e p) k n")).then_inc(wd_in[s], 16)
            sp.wait_ge(ex_y, EXPERTS)
            sp.wait_ge(idx_ok, 1)
            nov = sp.value_load(nov_i[0:1, 15:16], min_val=0, max_val=NOVER)
            for b in range(NOVER):
                with sp.If(nov > b):
                    e = sp.value_load(nov_i[0:1, b:b + 1], min_val=0, max_val=EXPERTS - 1)
                    sp.wait_ge(ex_y, EXPERTS)
                    if b:
                        sp.wait_ge(ov_y, b)
                    sp.dma_start(wgate[0], wg[bass.ds(e, 1)].rearrange("e p k n -> (e p) k n")).then_inc(ov_gu, 16)
                    sp.dma_start(wup[0], wu[bass.ds(e, 1)].rearrange("e p k n -> (e p) k n")).then_inc(ov_gu, 16)
                    sp.dma_start(wdown[0], wd[bass.ds(e, 1)].rearrange("e p k n -> (e p) k n")).then_inc(ov_d, 16)
            sp.wait_ge(moe_done, 1)
            y2 = y2_dram.rearrange("(n r) d -> n (r d)", r=2)
            for i in range(NT + 2):
                if i < NT:
                    if i >= 4:
                        sp.wait_ge(x3_ok, i - 3)
                    sp.dma_start(y2t[:, i % 4], y2[i * P:(i + 1) * P, :].rearrange("p (r d) -> p r d", r=2)).then_inc(y2_in[i % 4], 16)
                if i >= 2:
                    sp.wait_ge(fin_ok, i - 1)
                    sp.dma_start(t["out"][0, (i - 2) * P:(i - 1) * P, :], x2[:, i - 2, :]).then_inc(fin_out, 16)
            sp.wait_ge(fin_out, 16 * NT)

        @block.gpsimd
        def _(pool):
            n = [0]
            def link(ins):
                n[0] += 1
                ins.then_inc(pool_c, 1)
                pool.wait_ge(pool_c, n[0])

            link(pool.memset(ident[:, :], 0.0))
            pool.affine_select(out=ident[:, :], in_=ident[:, :], compare_op=ALU.not_equal, fill=1.0, base=0,
                               pattern=[[-1, P]], channel_multiplier=1).then_inc(const_ok, 1)
            pool.memset(mhalf[:, :], -0.5).then_inc(const_ok, 1)
            for r in range(4):
                pool.wait_ge(msv_ok, r + 1)
                if r == 0:
                    pool.wait_ge(const_ok, 2)
                pool.tensor_tensor(rstd[:, 2 * r:2 * r + 2], msv[:, 2 * r:2 * r + 2], mhalf[:, 0:2], ALU.pow)\
                    .then_inc(rstd_ok, 1)
            pool.memset(ksb[:, :, 0:P], 0.0).then_inc(kz_ok, 1)
            link(pool.memset(onesb[:, :], 1.0))
            link(pool.memset(tri[:, :], 1.0))
            pool.affine_select(out=tri[:, :], in_=tri[:, :], compare_op=ALU.is_gt, fill=0.0, base=0,
                               pattern=[[1, P]], channel_multiplier=-1).then_inc(const_ok, 1)
            link(pool.iota(iotai[:, :], pattern=[[1, P]], base=0, channel_multiplier=0))
            link(pool.iota(toki[:, :], pattern=[[P, NT]], base=0, channel_multiplier=1))
            link(pool.tensor_copy(iotaf[:, :], iotai[:, :]))
            link(pool.tensor_copy(tokf[:, :], toki[:, :]))
            pool.tensor_scalar(thr[:, :], iotaf[:, 1:8], float(P), None, ALU.mult).then_inc(const_ok, 1)
            pool.wait_ge(band_in, 16)
            for h in range(HEADS):
                pool.affine_select(out=band[:, h, :], in_=band[:, h, :], compare_op=ALU.is_ge, fill=NEG / SCALE,
                                   base=P, pattern=[[-1, 256]], channel_multiplier=1).then_inc(band_ok, 1)
            pool.wait_ge(set_in, SET_N * 16)
            pool.wait_ge(uT_ps, 4)
            pool.tensor_tensor(uc, uc, bc(dbc.rearrange("p (g h) -> p g h", h=GCH).unsqueeze(2), [P, GROUPS, CHUNK, GCH]), ALU.mult).then_inc(ud_ok, 1)
            pool.wait_ge(vin_ev, 4)
            pool.wait_ge(toep_dram, 64)
            pool.wait_ge(band_dram, 16)
            for k in range(SCAN_STEPS):
                d = 1 << k
                w = [P, PAIRS, NC - d]
                pr = bc(PDR[:, k, :].unsqueeze(2), w)
                pi = bc(PDI[:, k, :].unsqueeze(2), w)
                a = [s[:, :, 0:NC - d] for s in st]
                xrs, xis = XR[:, :, 0:NC - d], XI[:, :, 0:NC - d]
                pool.tensor_tensor(a[0], xrs, pr, ALU.mult)
                pool.tensor_tensor(a[1], xis, pi, ALU.mult)
                pool.tensor_tensor(a[2], xrs, pi, ALU.mult)
                link(pool.tensor_tensor(a[3], xis, pr, ALU.mult))
                pool.tensor_tensor(a[0], a[0], a[1], ALU.subtract)
                link(pool.tensor_tensor(a[2], a[2], a[3], ALU.add))
                pool.tensor_tensor(XR[:, :, d:NC], XR[:, :, d:NC], a[0], ALU.add)
                ins = pool.tensor_tensor(XI[:, :, d:NC], XI[:, :, d:NC], a[2], ALU.add)
                if k < SCAN_STEPS - 1:
                    link(ins)
                else:
                    ins.then_inc(scan_ok, 1)
            pool.wait_ge(ln_var, 1)
            pool.tensor_tensor(lnr[:, :], lnv[:, :], mhalf[:, :], ALU.pow).then_inc(ln_rstd, 1)
            for h in range(HEADS):
                pool.wait_ge(head_var, h + 1)
                pool.tensor_tensor(hrstd[:, h, :], hssv[:, h, :], mhalf[:, :], ALU.pow).then_inc(head_rstd, 1)
                pool.wait_ge(head_rstd, h + 1)
                o = mixT[:, h, :].rearrange("p (i v) -> p i v", i=NT)
                pool.tensor_tensor(o, o, bc(hrstd[:, h, :].unsqueeze(2), [P, NT, DV]), ALU.mult).then_inc(head_o, 1)
            for i in range(NT):
                pool.wait_ge(ms2v_ok, i + 1)
                pool.tensor_tensor(rstd2[:, i:i + 1], ms2v[:, i:i + 1], mhalf[:, 0:1], ALU.pow).then_inc(rstd2_ok, 1)

            pool.wait_ge(tab_ps, 1)
            pool.memset(xg[0], 0.0).then_inc(xg_z, 1)
            pool.memset(xg[1], 0.0).then_inc(xg_z, 1)
            pool.wait_ge(h2_out, 16 * NT)
            pool.wait_ge(xg_z, 2)

            def gather(b, s, done, cursem, curval):
                pool.tensor_copy(cur[:, 2 * s:2 * s + 1], tabi[:, 0, b:b + 1]).then_inc(cursem, 1)
                pool.tensor_copy(cur[:, 2 * s + 1:2 * s + 2], tabi[:, 1, b:b + 1]).then_inc(cursem, 1)
                pool.wait_ge(cursem, curval)
                pool.indirect_dma_start(xg[s], None, h2_dram,
                                        bass.IndirectOffsetOnAxis(ap=cur[:, 2 * s:2 * s + 1], axis=0),
                                        bounds_check=L - 1, oob_is_err=False).then_inc(done, 16)

            def scatter(s, done):
                pool.indirect_dma_start(y2_dram, bass.IndirectOffsetOnAxis(ap=cur[:, 2 * s + 1:2 * s + 2], axis=0),
                                        yb[s], None, bounds_check=2 * L - 1, oob_is_err=False).then_inc(done, 16)

            pool.wait_ge(idx_ok, 1)
            for e in range(2):
                gather(e, e, gather_in[e], cur_c, 2 * e + 2)
            for e in range(EXPERTS):
                s = e % 2
                pool.wait_ge(ex_y0, e + 1)
                pool.wait_ge(ex_y1, e + 1)
                scatter(s, scat_out[s])
                if e + 2 < EXPERTS:
                    pool.wait_ge(ex_xT, e + 1)
                    pool.wait_ge(scat_out[s], 16 * (e // 2 + 1))
                    gather(e + 2, s, gather_in[s], cur_c, 2 * e + 6)
            for s in range(2):
                pool.wait_ge(scat_out[s], 16 * (EXPERTS // 2))
            nov = pool.value_load(nov_i[0:1, 15:16], min_val=0, max_val=NOVER)
            for b in range(NOVER):
                with pool.If(nov > b):
                    pool.wait_ge(ex_xT, EXPERTS)
                    if b:
                        pool.wait_ge(ov_out, 16 * b)
                    gather(EXPERTS + b, 0, ov_x, ov_cur, 2 * b + 2)
                    pool.wait_ge(ov_y0, b + 1)
                    pool.wait_ge(ov_y1, b + 1)
                    scatter(0, ov_out)
                    pool.wait_ge(ov_out, 16 * (b + 1))
            pool.memset(cur[:, 0:1], 0).then_inc(moe_done, 1)
            for i in range(NT):
                pool.wait_ge(ms3v_ok, i + 1)
                pool.tensor_tensor(rstd3[:, i:i + 1], ms3v[:, i:i + 1], mhalf[:, 0:1], ALU.pow).then_inc(rstd3_ok, 1)

        @block.scalar
        def _(act):
            n = [0]
            def link(ins):
                n[0] += 1
                ins.then_inc(act_c, 1)
                act.wait_ge(act_c, n[0])

            for dst, src in par_loads:
                act.dma_start(dst, src, allow_slow_non_contiguous=True).then_inc(par_in, 16)
            for i in range(NT):
                act.wait_ge(x_in[i], 16)
                if i:
                    act.wait_ge(ms_ok, i)
                act.activation(xr[:, :], xt[:, i, :], ACT.Square, accum_out=ms[:, i:i + 1]).then_inc(ms_ok, 1)
            for dst, src in set_loads:
                act.dma_start(dst, src, allow_slow_non_contiguous=True).then_inc(set_in, 16)
            act.wait_ge(band_ps, 1)
            act.activation(brow[:, :], psum[0:HEADS, 6, 0:384], ACT.Copy, scale=1.0 / SCALE).then_inc(band_row, 1)
            act.wait_ge(lam_dot, 1)
            act.activation(lam[:, 2:4], lam[:, 0:2], ACT.Exp).then_inc(lam_exp, 1)
            act.wait_ge(par_in, 16 * PAR_N)
            act.activation(sv[:, 1, :], sv[:, 0, :], ACT.Exp).then_inc(ssm_dt, 1)
            act.wait_ge(ssm_ang, 1)
            act.activation(sv[:, 6, :], sv[:, 4, :], ACT.Exp)
            act.activation(sv[:, 7, :], sv[:, 5, :], ACT.Sin)
            act.activation(sv[:, 8, :], sv[:, 5, :], ACT.Sin, scale=0.5).then_inc(ssm_sin, 1)

            def evac(u):
                _, kind, i = UNITS[u]
                src = bank(4 + u % 4)
                act.wait_ge(unit_ps, u + 1)
                if kind == "ssm":
                    act.activation(uc[:, :, i, :], src[:, 0:CH].rearrange("p (g h) -> p g h", h=GCH), ACT.Copy).then_inc(unit_ev, 1)
                elif kind == "v":
                    c0 = CHUNKS[UNITS[u][0]][0] - 1024
                    act.activation(vtok[:, i, c0:c0 + WCH], src[:, 0:WCH], ACT.Copy).then_inc(unit_ev, 1)
                elif kind == "gate":
                    act.activation(convo[:, i // 2, 512 * (i % 2):512 * (i % 2) + 512], src, ACT.Sigmoid).then_inc(unit_ev, 1)
                elif kind == "a":
                    act.activation(convh[:, i // 2, 512 * (i % 2):512 * (i % 2) + 512], src, ACT.Copy).then_inc(unit_ev, 1)
                else:
                    c = 2 * (UNITS[u][0] - 5) + i // 2
                    if u == LAST_UNIT[4] + 1:
                        act.wait_ge(xT_ps, NT)
                    act.activation(qkT[:, c, 512 * (i % 2):512 * (i % 2) + 512], src, ACT.Copy).then_inc(unit_ev, 1)

            act.wait_ge(const_ok, 4)
            for u in range(0, 16):
                evac(u)
            for i in range(4):
                act.wait_ge(uT_ps, i + 1)
                act.activation(UT[:, 4 * i:4 * i + 4, :].rearrange("p g c -> p (g c)"), bank(i), ACT.Copy).then_inc(uT_ev, 1)
            for i in range(4):
                act.wait_ge(wi_ps, i + 1)
                dst = (WinR, WinI)[i // 2]
                act.activation(dst[:, 4 * (i % 2):4 * (i % 2) + 4, :].rearrange("p a s -> p (a s)"), bank(i), ACT.Copy).then_inc(wi_ev, 1)
            act.wait_ge(k_ps, 1)
            act.wait_ge(kz_ok, 1)
            for r in range(4):
                ins = act.activation(ksb[32 * r:32 * r + GCH, :, P:2 * P],
                                     psum[32 * r:32 * r + GCH, 0, :].rearrange("p (q n) -> p q n", q=4), ACT.Copy)
            ins.then_inc(k_ev, 1)
            for u in range(16, LAST_UNIT[3] + 1):
                evac(u)
            act.memzero(XR[:, :, 0:1])
            act.memzero(XI[:, :, 0:1])
            for i in range(4):
                act.wait_ge(vin_ps, i + 1)
                dst = (XR, XI)[i // 2]
                act.activation(dst[:, 4 * (i % 2):4 * (i % 2) + 4, 1:NC],
                               bank(i % 2).rearrange("p (a c) -> p a c", a=4)[:, :, 0:NC - 1], ACT.Copy).then_inc(vin_ev, 1)
            for u in range(LAST_UNIT[3] + 1, len(UNITS)):
                evac(u)
            act.wait_ge(set_in, 16 * SET_N)
            for c in range(2):
                act.wait_ge(conv_ps, c + 1)
                act.activation(convo[:, c, :], banks(2 - 2 * c, 2), ACT.Identity, bias=convb[:, c:c + 1]).then_inc(conv_ev, 1)
            act.wait_ge(y_ev, 4)
            act.activation(RG[:, 6144:8192], RG[:, 6144:8192], ACT.Gelu_apprx_tanh).then_inc(gelu_ok, 1)

            act.dma_start(rw[:, :, 0:4], t["group_router_w"][0].rearrange("(k p) n -> p k n", p=P)).then_inc(rw_in, 16)
            act.dma_start(rw[:, :, 4:36], t["expert_router_w"][0].rearrange("(k p) n -> p k n", p=P)).then_inc(rw_in, 16)
            link(act.activation(sg[:, :], sg[:, :], ACT.Copy, scale=1.0 - LAM_INIT))
            nm = [0]

            def misc(job):
                kind, i = job
                nm[0] += 1
                act.wait_ge(misc_ps, nm[0])
                src = bank(7)
                if kind == "conv_to_tok":
                    ins = act.activation(convt[:, 2 * i:2 * i + 2, :].rearrange("p t n -> p (t n)"), src, ACT.Copy)
                elif kind == "ssm_to_ch":
                    c, jh = i // 2, i % 2
                    dst = gT[:, c, :].rearrange("p (n j) -> p j n", j=CHUNK)[:, 4 * jh:4 * jh + 4, :]
                    ins = act.activation(dst, src.rearrange("p (j n) -> p j n", j=4), ACT.Copy)
                elif kind == "conv_to_ch":
                    c, half = i // 2, i % 2
                    z = convo[:, c, 512 * half:512 * half + 512]
                    link(act.activation(z, src, ACT.Identity, bias=lnb[:, c:c + 1], scale=lng[:, c:c + 1]))
                    act.activation(silu[:, i, :], z, ACT.Tanh, scale=0.5).then_inc(silu_t, 1)
                    ins = None
                elif kind == "glu":
                    c, half = i // 2, i % 2
                    ins = act.activation(glut[:, c, 512 * half:512 * half + 512], src, ACT.Tanh,
                                         bias=glub[:, c:c + 1], scale=0.5)
                else:
                    h, half = i // 2, i % 2
                    ins = act.activation(mixT[:, h, 512 * half:512 * half + 512], src, ACT.Copy, scale=sg[:, 0:1])
                return ins

            link(act.activation(glub[:, :], glub[:, :], ACT.Copy, scale=0.5))

            def exps(k):
                h, i = ITEMS[k]
                nk = (i + 1) * P
                far = max(nk - 256, 0)
                for m in range(2):
                    act.wait_ge(nm_ok, 2 * k + m + 1)
                    sl = 2 * (k % 2) + m
                    st_ = smx[:, k % 2, m, :]
                    ins = act.activation(pexp[:, sl, far:nk], pexp[:, sl, far:nk], ACT.Exp,
                                         bias=st_[:, 2:3], accum_out=st_[:, 4:5])
                    if far:
                        ins = act.activation(pexp[:, sl, 0:far], banks(2 * m, 2)[:, 0:far], ACT.Exp,
                                             bias=st_[:, 3:4], scale=SCALE, accum_out=st_[:, 5:6])
                    ins.then_inc(e_ok, 1)

            def p_evac(k):
                h, i = ITEMS[k]
                act.wait_ge(pT_ps, k + 1)
                act.activation(pT[k % 2][:, 0:i + 1, :].rearrange("p k n -> p (k n)"),
                               banks(4, 2)[:, 0:(i + 1) * P], ACT.Copy).then_inc(pT_ev, 1)

            def o_evac(k):
                h, i = ITEMS[k]
                act.wait_ge(o_ps, k + 1)
                o = mixT[:, h, i * P:(i + 1) * P]
                act.activation(o, psum[:, 6, 0:P], ACT.Copy).then_inc(o_ev, 1)
                act.activation(psum[:, 6, P:2 * P], psum[:, 6, 0:P], ACT.Square, accum_out=hss[:, h, i:i + 1]).then_inc(head_ss, 1)

            for k in range(ITERS + 2):
                if k < NI:
                    exps(k)
                if 1 <= k <= NI:
                    p_evac(k - 1)
                if 2 <= k < NI + 2:
                    if k >= 3:
                        act.wait_ge(head_ss, k - 2)
                    o_evac(k - 2)
                for job in MISC_AT.get(k, []):
                    ins = misc(job)
                    if ins is not None:
                        ins.then_inc(misc_ev, 1)

            def reload(i):
                if i:
                    act.wait_ge(x2_ok, i)
                act.dma_start(xr[:, :], t["x"][0, i * P:(i + 1) * P, :]).then_inc(xr_in, 16)

            act.wait_ge(head_ss, NI)
            reload(0)
            for i in range(NT):
                act.wait_ge(x2_ok, i + 1)
                if i + 1 < NT:
                    reload(i + 1)
                if i:
                    act.wait_ge(ms2_ok, i)
                act.activation(banks(6, 2), x2[:, i, :], ACT.Square, accum_out=ms2[:, i:i + 1]).then_inc(ms2_ok, 1)
                act.wait_ge(h2_ok, i + 1)
                act.dma_start(h2_dram[i * P:(i + 1) * P, :].rearrange("p (k n) -> p k n", k=KD),
                              mixT[:, :, i * P:(i + 1) * P]).then_inc(h2_out, 16)
            act.wait_ge(gd_ok, 1)
            act.activation(rrv("gexp"), rrv("gdif"), ACT.Exp)
            act.activation(rrv("eexp"), rrv("edif"), ACT.Exp).then_inc(ge_ok, 1)

            def expert(s, g, u, a, aT, yv, S, scat):
                act.wait_ge(S["g"], g)
                act.activation(actb, bank(2), ACT.Silu).then_inc(S["s"], 1)
                act.wait_ge(S["aT"], aT)
                act.activation(actT[:, :, :].rearrange("p k n -> p (k n)"), bank(4), ACT.Copy).then_inc(S["aTe"], 1)
                act.wait_ge(S["y"], yv)
                if scat is not None:
                    act.wait_ge(scat[0], scat[1])

            EX = dict(g=ex_g, s=ex_s, aT=ex_aT, aTe=ex_aTe, y=ex_y)
            OV = dict(g=ov_g, s=ov_s, aT=ov_aT, aTe=ov_aTe, y=ov_y)
            act.wait_ge(idx_ok, 1)

            def y_half(s, b):
                gate = tabg[:, b:b + 1] if isinstance(b, int) else tabg[:, bass.ds(b, 1)]
                return act.activation(yb[s][:, 0:512], bank(5), ACT.Copy, scale=gate)

            for e in range(2):
                expert(e, e + 1, 0, 0, e + 1, e + 1, EX, None)
                y_half(e, e).then_inc(ex_y0, 1)
            with act.Fori(1, EXPERTS // 2) as j:
                for s in range(2):
                    e = act.snap(j * 2 + s)
                    e1 = act.snap(j * 2 + s + 1)
                    expert(s, e1, 0, 0, e1, e1, EX, (scat_out[s], j * 16))
                    y_half(s, e).then_inc(ex_y0, 1)
            nov = act.value_load(nov_i[0:1, 15:16], min_val=0, max_val=NOVER)
            for b in range(NOVER):
                with act.If(nov > b):
                    act.wait_ge(ex_y, EXPERTS)
                    for s in range(2):
                        act.wait_ge(scat_out[s], 16 * (EXPERTS // 2))
                    expert(0, b + 1, 0, 0, b + 1, b + 1, OV, (ov_out, 16 * b) if b else None)
                    y_half(0, EXPERTS + b).then_inc(ov_y0, 1)
            act.dma_start(fgb, t["final_g"].rearrange("(o d) -> o d", o=1).to_broadcast([P, D])).then_inc(fg_in, 16)
            act.wait_ge(moe_done, 1)
            for i in range(NT + 1):
                if i < NT:
                    act.wait_ge(y2_in[i % 4], 16 * (i // 4 + 1))
                    if i >= 3:
                        act.wait_ge(fin_ok, i - 2)
                    act.activation(banks(2 * (i % 3), 2), y2t[:, i % 4, 0, :], ACT.Copy).then_inc(ya_ps, 1)
                if i >= 1:
                    act.wait_ge(x3_ok, i)
                    if i >= 2:
                        act.wait_ge(ms3_ok, i - 1)
                    act.activation(banks(6, 2), banks(2 * ((i - 1) % 3), 2), ACT.Square,
                                   accum_out=ms3[:, i - 1:i]).then_inc(ms3_ok, 1)

        @block.tensor
        def _(pe):
            pe.wait_ge(const_ok, 1)
            pe.wait_ge(par_in, 16 * PAR_N)
            pe.matmul(psum[0:HEADS, 6, 0:384], relt[:, :], onehot, start=True, stop=True).then_inc(band_ps, 1)
            pe.transpose(psum[:, 7, 0:16], lrow[0:16, :], ident[0:16, 0:16])
            pe.transpose(psum[:, 7, 128:256], crow[:, 0, :], ident[:, :])
            pe.transpose(psum[:, 7, 256:384], crow[:, 1, :], ident[:, :]).then_inc(lrow_ps, 1)
            for i in range(NT):
                pe.wait_ge(xn_ok, i + 1)
                if i >= 2:
                    pe.wait_ge(hT_ok, 2 * (i - 1))
                for k in range(KD):
                    ins = pe.transpose(psum[:, 2 * (i % 2) + k // 4, P * (k % 4):P * (k % 4) + P],
                                       xt[:, i, k * P:(k + 1) * P], ident[:, :])
                ins.then_inc(xT_ps, 1)
            pe.wait_ge(hT_ok, 2 * NT)
            pe.wait_ge(band_row, 1)
            pe.wait_ge(lam_ok, 1)
            chunk_seen = [-1]

            def unit(u):
                c, kind, i = UNITS[u]
                if chunk_seen[0] != c:
                    chunk_seen[0] = c
                    pe.wait_ge(win_in[c % 3], 16 * (c // 3 + 1))
                if u >= 4:
                    pe.wait_ge(unit_ev, u - 3)
                w = win[:, c % 3]
                for k in range(KD):
                    first, last = k == 0, k == KD - 1
                    if kind == "ssm":
                        ins = pe.matmul(bank(4 + u % 4)[:, 0:WCH], hT[:, k, i:L:CHUNK], w[:, k, :], start=first, stop=last)
                    elif kind == "v":
                        ins = pe.matmul(bank(4 + u % 4)[:, 0:WCH], hT[:, k, i * P:(i + 1) * P], w[:, k, :], start=first, stop=last)
                    else:
                        ct, half = i // 2, i % 2
                        ins = pe.matmul(bank(4 + u % 4), w[:, k, ct * P:(ct + 1) * P],
                                        hT[:, k, 512 * half:512 * half + 512], start=first, stop=last)
                ins.then_inc(unit_ps, 1)

            for u in range(16):
                unit(u)
            pe.wait_ge(unit_ev, 8)
            for g in range(GROUPS):
                ins = pe.transpose(psum[:, g // 4, P * (g % 4):P * (g % 4) + P],
                                   uc[:, g].rearrange("p i h -> p (i h)"), ident[:, :])
                if g % 4 == 3:
                    ins.then_inc(uT_ps, 1)
            pe.wait_ge(vb_ok, 1)
            for r, vb in enumerate((VBR, VBI)):
                for a in range(PAIRS):
                    b = 2 * r + a // 4
                    if a % 4 == 0:
                        pe.wait_ge(uT_ev, b + 1)
                    ins = pe.transpose(psum[:, b, P * (a % 4):P * (a % 4) + P],
                                       vb[:, a].rearrange("p i h -> p (i h)"), ident[:, :])
                    if a % 4 == 3:
                        ins.then_inc(wi_ps, 1)
            pe.wait_ge(ca_ok, 1)
            pe.wait_ge(wi_ev, 1)
            for g in range(GROUPS):
                a, q = g // 2, STATES * (g % 2)
                out = psum[32 * (g % 4):32 * (g % 4) + GCH, 0, P * (g // 4):P * (g // 4) + P]
                pe.matmul(out, BBR[q:q + STATES, a, :], CAR[q:q + STATES, a, 0:CHUNK, :].rearrange("p t h -> p (t h)"),
                          start=True, stop=False)
                ins = pe.matmul(out, BBI[q:q + STATES, a, :], CAI[q:q + STATES, a, 0:CHUNK, :].rearrange("p t h -> p (t h)"),
                                start=False, stop=True)
            ins.then_inc(k_ps, 1)
            for u in range(16, LAST_UNIT[3] + 1):
                unit(u)
            pe.wait_ge(k_ev, 1)
            pe.wait_ge(wi_ev, 4)
            for r, win_ in enumerate((WinR, WinI)):
                for a in range(PAIRS):
                    b = a // 4
                    if r == 1 and a % 4 == 0:
                        pe.wait_ge(vin_ev, b + 1)
                    for q in range(2):
                        ins = pe.matmul(psum[STATES * q:STATES * (q + 1), b, P * (a % 4):P * (a % 4) + P],
                                        win_[:, a, STATES * q:STATES * (q + 1)], UT[:, 2 * a + q, :], start=True, stop=True)
                    if a % 4 == 3:
                        ins.then_inc(vin_ps, 1)
            for u in range(LAST_UNIT[3] + 1, len(UNITS)):
                unit(u)
            pe.wait_ge(scan_ok, 1)
            pe.wait_ge(toep_in, 16 * CHUNK)
            pe.wait_ge(conv_ev, 2)
            for g in range(GROUPS):
                a, q = g // 2, STATES * (g % 2)
                b, c = 2 * (g % 2) + g // 8, (g // 2) % 4
                out = psum[:, b, P * c:P * c + P]
                pe.matmul(out, XR[q:q + STATES, a, :], CAR[q:q + STATES, a, 1:CHUNK + 1, :].rearrange("p t h -> p (t h)"),
                          start=True, stop=False)
                pe.matmul(out, XI[q:q + STATES, a, :], CAI[q:q + STATES, a, 1:CHUNK + 1, :].rearrange("p t h -> p (t h)"),
                          start=False, stop=False)
                ins = pe.matmul(out, UT[:, g, :], TG[:, g, :], start=False, stop=True)
                if g % 8 == 7:
                    ins.then_inc(y_ps, 1)

            nm = [0]

            def misc(job):
                kind, i = job
                if nm[0] and MISC_ORDER[nm[0] - 1][0] != "conv_to_ch":
                    pe.wait_ge(misc_ev, sum(1 for j in MISC_ORDER[:nm[0]] if j[0] != "conv_to_ch"))
                elif nm[0]:
                    pe.wait_ge(silu_t, sum(1 for j in MISC_ORDER[:nm[0]] if j[0] == "conv_to_ch"))
                nm[0] += 1
                if kind == "conv_to_tok":
                    for k in range(4):
                        tt, c = 2 * i + k // 2, k % 2
                        ins = pe.transpose(psum[:, 7, P * k:P * k + P], convo[:, c, tt * P:(tt + 1) * P], ident[:, :])
                elif kind == "ssm_to_ch":
                    pe.wait_ge(gelu_ok, 1)
                    c, jh = i // 2, i % 2
                    for k in range(4):
                        ins = pe.transpose(psum[:, 7, P * k:P * k + P], yc[:, 4 * jh + k, c * P:(c + 1) * P], ident[:, :])
                elif kind == "conv_to_ch":
                    pe.wait_ge(ln_ok, 1)
                    c, half = i // 2, i % 2
                    for k in range(4):
                        ins = pe.transpose(psum[:, 7, P * k:P * k + P], convt[:, 4 * half + k, c * P:(c + 1) * P], ident[:, :])
                elif kind == "glu":
                    c, half = i // 2, i % 2
                    for k in range(2):
                        ins = pe.matmul(bank(7), gluw[:, k, c * P:(c + 1) * P], gT[:, k, 512 * half:512 * half + 512],
                                        start=k == 0, stop=k == 1)
                else:
                    h, half = i // 2, i % 2
                    pe.wait_ge(head_o, h + 1)
                    for k in range(4):
                        ins = pe.transpose(psum[:, 7, P * k:P * k + P],
                                           mixT[:, h, (4 * half + k) * P:(4 * half + k + 1) * P], ident[:, :])
                ins.then_inc(misc_ps, 1)

            pe.wait_ge(set_in, 16 * SET_N)
            pe.wait_ge(unit_ev, len(UNITS))
            pe.wait_ge(y_ev, 4)
            for k in range(ITERS + 2):
                if k < NI:
                    h, i = ITEMS[k]
                    q = DK * (h % 2)
                    nk = (i + 1) * P
                    for m in range(2):
                        if k:
                            pe.wait_ge(e_ok, 2 * (k - 1) + m + 1)
                        for b in range(0, nk, 512):
                            w = min(512, nk - b)
                            ins = pe.matmul(psum[:, 2 * m + b // 512, 0:w],
                                            qkT[q:q + DK, 2 * m + h // 2, i * P:(i + 1) * P],
                                            qkT[q:q + DK, 4 + 2 * m + h // 2, b:b + w], start=True, stop=True)
                        ins.then_inc(s_ps, 1)
                if 1 <= k <= NI:
                    i = ITEMS[k - 1][1]
                    pe.wait_ge(p_ok, k)
                    if k >= 2:
                        pe.wait_ge(pT_ev, k - 1)
                    for c in range(i + 1):
                        ins = pe.transpose(psum[:, 4 + c // 4, P * (c % 4):P * (c % 4) + P],
                                           pexp[:, 2 * ((k - 1) % 2), c * P:(c + 1) * P], ident[:, :])
                    ins.then_inc(pT_ps, 1)
                if 2 <= k < NI + 2:
                    h, i = ITEMS[k - 2]
                    pe.wait_ge(pT_ev, k - 1)
                    if k >= 3:
                        pe.wait_ge(head_ss, k - 2)
                    for c in range(i + 1):
                        ins = pe.matmul(psum[:, 6, 0:P], pT[k % 2][:, c, :], vtok[:, c, h * DV:(h + 1) * DV],
                                        start=c == 0, stop=c == i)
                    ins.then_inc(o_ps, 1)
                for job in MISC_AT.get(k, []):
                    misc(job)

            for s in range(3):
                pe.wait_ge(wout_in[s], 16)
            pe.wait_ge(rw_in, 32)
            pe.wait_ge(misc_ev, sum(1 for j in MISC_ORDER if j[0] != "conv_to_ch"))
            pe.wait_ge(conv_ok, 4)
            pe.wait_ge(ssm_ok, 1)
            for k in range(NT + 2):
                if k < NT:
                    if k >= 2:
                        pe.wait_ge(x2_ok, k - 1)
                    for half in range(2):
                        for c in range(KD):
                            ins = pe.matmul(bank(2 * (k % 2) + half), mixT[:, c, k * P:(k + 1) * P],
                                            wout[:, c, 512 * half:512 * half + 512], start=c == 0, stop=c == KD - 1)
                    ins.then_inc(proj_ps, 1)
                if k >= 2:
                    pe.wait_ge(h2T_ok, k - 1)
                    if k >= 3:
                        pe.wait_ge(lg_ok, k - 2)
                    for c in range(KD):
                        ins = pe.matmul(psum[:, 4, 0:36], h2T[:, c, :], rw[:, c, :], start=c == 0, stop=c == KD - 1)
                    ins.then_inc(lg_ps, 1)
                if 1 <= k <= NT:
                    pe.wait_ge(h2_ok, k)
                    if k >= 2:
                        pe.wait_ge(lg_ok, k - 1)
                    for c in range(4):
                        pe.transpose(psum[:, 4, P * c:P * c + P], mixT[:, c, (k - 1) * P:k * P], ident[:, :])
                    for c in range(4):
                        ins = pe.transpose(psum[:, 5, P * c:P * c + P], mixT[:, 4 + c, (k - 1) * P:k * P], ident[:, :])
                    ins.then_inc(h2T_ps, 1)

            pe.wait_ge(mm_ok, 1)
            pe.wait_ge(const_ok, 3)
            pe.matmul(bank(0)[:, 0:256], tri[:, :], mbf[:, :, :].rearrange("p t n -> p (t n)"), start=True, stop=False)
            for s in range(1, NT):
                pe.matmul(bank(0)[:, 32 * s:256], onesb[:, :], mbf[:, 0:NT - s, :].rearrange("p t n -> p (t n)"),
                          start=False, stop=s == NT - 1)
            for i in range(NT):
                ins = pe.matmul(bank(1)[:, 0:32], onesb[:, :], mbf[:, i, :], start=i == 0, stop=i == NT - 1)
            ins.then_inc(rank_ps, 1)
            pe.wait_ge(tab_ok, 1)
            for r in range(16):
                ins = pe.matmul(bank(2)[:, 0:3 * NBLK], slot1h[:, r, :], bval[:, r].rearrange("p n v -> p (n v)"),
                                start=r == 0, stop=r == 15)
            ins.then_inc(tab_ps, 1)

            def xT(s, got, S):
                pe.wait_ge(*got)
                for k in range(KD):
                    ins = pe.transpose(psum[:, k // 4, P * (k % 4):P * (k % 4) + P],
                                       xg[s].rearrange("p (n k) -> p k n", k=KD)[:, k, :], ident[:, :])
                ins.then_inc(S["xT"], 1)

            def gate_up(s, xTe, wsem, wval, S):
                pe.wait_ge(S["xTe"], xTe)
                pe.wait_ge(wsem, wval)
                for b, w, done in ((2, wgate[s], S["g"]), (3, wup[s], S["u"])):
                    for k in range(KD):
                        ins = pe.matmul(bank(b), xgT[:, k, :], w[:, k, :], start=k == 0, stop=k == KD - 1)
                    ins.then_inc(done, 1)

            def down(s, a, aTe, wsem, wval, S):
                pe.wait_ge(S["a"], a)
                for k in range(FK):
                    ins = pe.transpose(psum[:, 4, P * k:P * k + P],
                                       actb.rearrange("p (n k) -> p k n", k=FK)[:, k, :], ident[:, :])
                ins.then_inc(S["aT"], 1)
                pe.wait_ge(S["aTe"], aTe)
                pe.wait_ge(wsem, wval)
                for half in range(2):
                    for k in range(FK):
                        ins = pe.matmul(bank(5 + half), actT[:, k, :], wdown[s][:, k, 512 * half:512 * half + 512],
                                        start=k == 0, stop=k == FK - 1)
                ins.then_inc(S["y"], 1)

            EX = dict(xT=ex_xT, xTe=ex_xTe, g=ex_g, u=ex_u, a=ex_a, aT=ex_aT, aTe=ex_aTe, y=ex_y)
            OV = dict(xT=ov_xT, xTe=ov_xTe, g=ov_g, u=ov_u, a=ov_a, aT=ov_aT, aTe=ov_aTe, y=ov_y)
            pe.wait_ge(idx_ok, 1)

            def expert(j, s, first=False, last=False):
                e1 = j * 2 + s + 1
                gate_up(s, e1 if isinstance(e1, int) else pe.snap(e1), wgu_in[s], (j + 1) * 32, EX)
                if not last:
                    xT(1 - s, (gather_in[1 - s], (j + 1 + s) * 16), EX)
                if not first:
                    pe.wait_ge(ex_y0, e1 - 1)
                    pe.wait_ge(ex_y1, e1 - 1)
                down(s, e1, e1, wd_in[s], (j + 1) * 16, EX)

            xT(0, (gather_in[0], 16), EX)
            expert(0, 0, first=True)
            expert(0, 1)
            with pe.Fori(1, EXPERTS // 2 - 1) as j:
                for s in range(2):
                    expert(j, s)
            expert(EXPERTS // 2 - 1, 0)
            expert(EXPERTS // 2 - 1, 1, last=True)
            nov = pe.value_load(nov_i[0:1, 15:16], min_val=0, max_val=NOVER)
            for b in range(NOVER):
                with pe.If(nov > b):
                    pe.wait_ge(ex_y0, EXPERTS)
                    pe.wait_ge(ex_y1, EXPERTS)
                    if b:
                        pe.wait_ge(ov_y0, b)
                        pe.wait_ge(ov_y1, b)
                    xT(0, (ov_x, 16 * (b + 1)), OV)
                    gate_up(0, b + 1, ov_gu, 32 * (b + 1), OV)
                    down(0, b + 1, b + 1, ov_d, 16 * (b + 1), OV)

        @block.vector
        def _(dve):
            n = [0]
            def link(ins):
                n[0] += 1
                ins.then_inc(dve_c, 1)
                dve.wait_ge(dve_c, n[0])

            def norm_pair(r):
                dve.wait_ge(ms_ok, 2 * r + 2)
                dve.tensor_scalar(msv[:, 2 * r:2 * r + 2], ms[:, 2 * r:2 * r + 2], 1.0 / D, RMS_EPS, ALU.mult, ALU.add)\
                   .then_inc(msv_ok, 1)
                dve.wait_ge(rstd_ok, r + 1)
                for i in (2 * r, 2 * r + 1):
                    dve.tensor_scalar(xt[:, i, :], xt[:, i, :], rstd[:, i:i + 1], None, ALU.mult).then_inc(xn_ok, 1)

            def hT_evac(i):
                dve.wait_ge(xT_ps, i + 1)
                if i == 0:
                    dve.wait_ge(par_in, 16 * PAR_N)
                for b in range(2):
                    dve.tensor_tensor(hT[:, 4 * b:4 * b + 4, i * P:(i + 1) * P],
                                      bank(2 * (i % 2) + b).rearrange("p (k n) -> p k n", k=4),
                                      bc(g1[:, 4 * b:4 * b + 4].unsqueeze(2), [P, 4, P]), ALU.mult).then_inc(hT_ok, 1)

            norm_pair(0)
            for r in range(1, 4):
                norm_pair(r)
                hT_evac(2 * r - 2)
                hT_evac(2 * r - 1)
            hT_evac(6)
            hT_evac(7)

            dve.wait_ge(par_in, 16 * PAR_N)
            for v in range(2):
                ins = dve.tensor_tensor_reduce(out=ctmp[:, 64 * v:64 * v + DK], in0=lamv[:, 2 * v, :], in1=lamv[:, 2 * v + 1, :],
                                               scale=1.0, scalar=0.0, op0=ALU.mult, op1=ALU.add, accum_out=lam[:, v:v + 1])
            ins.then_inc(lam_dot, 1)
            dve.wait_ge(lrow_ps, 1)
            dve.tensor_copy(sv[:, 2:4, :].rearrange("p n a -> p (n a)"), psum[:, 7, 0:16])
            c4 = psum[:, 7, 128:384].rearrange("p (r a h) -> p r a h", r=2, a=PAIRS)
            dve.tensor_copy(CAR[:, :, 0, :], c4[:, 0])
            link(dve.tensor_scalar(CAI[:, :, 0, :], c4[:, 1], -1.0, None, ALU.mult))
            dve.wait_ge(lam_exp, 1)
            link(dve.tensor_tensor(lam[:, 0:1], lam[:, 3:4], lam[:, 2:3], ALU.subtract))
            dve.tensor_scalar(lam[:, 1:2], lam[:, 0:1], LAM_INIT, None, ALU.subtract).then_inc(lam_ok, 1)
            dve.wait_ge(ssm_dt, 1)
            dve.tensor_tensor(sv[:, 4, :], sv[:, 2, :], sv[:, 1, :], ALU.mult)
            link(dve.tensor_tensor(sv[:, 9, :], sv[:, 3, :], sv[:, 1, :], ALU.mult))
            link(dve.tensor_scalar(sv[:, 10, :], sv[:, 9, :], 1.0 / (2.0 * math.pi), ROUND, ALU.mult, ALU.add))
            link(dve.tensor_scalar(sv[:, 10, :], sv[:, 10, :], ROUND, None, ALU.subtract))
            for c in TWO_PI:
                link(dve.scalar_tensor_tensor(sv[:, 9, :], sv[:, 10, :], -c, sv[:, 9, :], ALU.mult, ALU.add))
            dve.tensor_scalar(sv[:, 5, :], sv[:, 9, :], PI, -PI, ALU.min, ALU.max).then_inc(ssm_ang, 1)
            dve.tensor_tensor(sv[:, 11, :], sv[:, 2, :], sv[:, 2, :], ALU.mult)
            link(dve.tensor_tensor(sv[:, 12, :], sv[:, 3, :], sv[:, 3, :], ALU.mult))
            link(dve.tensor_tensor(sv[:, 11, :], sv[:, 11, :], sv[:, 12, :], ALU.add))
            link(dve.reciprocal(sv[:, 13, :], sv[:, 11, :]))
            dve.wait_ge(ssm_sin, 1)
            link(dve.scalar_tensor_tensor(sv[:, 14, :], sv[:, 8, :], -2.0, sv[:, 8, :], ALU.mult, ALU.mult))
            dve.scalar_tensor_tensor(PWR[:, 1, :], sv[:, 14, :], 1.0, sv[:, 6, :], ALU.add, ALU.mult)
            dve.tensor_tensor(PWI[:, 1, :], sv[:, 6, :], sv[:, 7, :], ALU.mult)
            dve.memset(PWR[:, 0, :], 1.0)
            link(dve.memset(PWI[:, 0, :], 0.0))
            link(dve.tensor_scalar(sv[:, 15, :], PWR[:, 1, :], 1.0, None, ALU.subtract))
            dve.tensor_tensor(sv[:, 16, :], sv[:, 15, :], sv[:, 2, :], ALU.mult)
            dve.tensor_tensor(sv[:, 17, :], PWI[:, 1, :], sv[:, 3, :], ALU.mult)
            dve.tensor_tensor(sv[:, 18, :], PWI[:, 1, :], sv[:, 2, :], ALU.mult)
            link(dve.tensor_tensor(sv[:, 19, :], sv[:, 15, :], sv[:, 3, :], ALU.mult))
            dve.tensor_tensor(sv[:, 20, :], sv[:, 16, :], sv[:, 17, :], ALU.add)
            link(dve.tensor_tensor(sv[:, 21, :], sv[:, 18, :], sv[:, 19, :], ALU.subtract))
            dve.tensor_tensor(sv[:, 22, :], sv[:, 20, :], sv[:, 13, :], ALU.mult)
            link(dve.tensor_tensor(sv[:, 23, :], sv[:, 21, :], sv[:, 13, :], ALU.mult))

            def cmul(outr, outi, ar, ai, br, bi, t1, t2, t3, t4, neg=False):
                dve.tensor_tensor(t1, ar, br, ALU.mult)
                dve.tensor_tensor(t2, ai, bi, ALU.mult)
                dve.tensor_tensor(t3, ar, bi, ALU.mult)
                link(dve.tensor_tensor(t4, ai, br, ALU.mult))
                dve.tensor_tensor(outr, t1, t2, ALU.add if neg else ALU.subtract)
                link(dve.tensor_tensor(outi, t3, t4, ALU.subtract if neg else ALU.add))

            tm = [ctmp[:, 64 * q:64 * q + 32] for q in range(4)]

            def small(q, k):
                return tm[q][:, 0:8 * k].rearrange("p (t a) -> p t a", a=PAIRS)

            for base in (1, 2, 4):
                w = [P, base, PAIRS]
                cmul(PWR[:, base + 1:2 * base + 1, :], PWI[:, base + 1:2 * base + 1, :],
                     bc(PWR[:, base:base + 1, :], w), bc(PWI[:, base:base + 1, :], w),
                     PWR[:, 1:base + 1, :], PWI[:, 1:base + 1, :], *[small(q, base) for q in range(4)])
            dve.tensor_copy(PDR[:, 0, :], PWR[:, 8, :])
            link(dve.tensor_copy(PDI[:, 0, :], PWI[:, 8, :]))
            for k in range(SCAN_STEPS - 1):
                cmul(PDR[:, k + 1:k + 2, :], PDI[:, k + 1:k + 2, :], PDR[:, k:k + 1, :], PDI[:, k:k + 1, :],
                     PDR[:, k:k + 1, :], PDI[:, k:k + 1, :], *[small(q, 1) for q in range(4)])
            w = [P, PAIRS, GCH]
            tb = [st4[:, 0:128].rearrange("p (a h) -> p a h", a=PAIRS) for st4 in TMP4]
            cmul(BBR, BBI, bc(sv[:, 22, :].unsqueeze(2), w), bc(sv[:, 23, :].unsqueeze(2), w), bre, bim, *tb)
            for i in range(CHUNK):
                dve.tensor_copy(RVR[:, i, :], PWR[:, CHUNK - 1 - i, :])
                ins = dve.tensor_copy(RVI[:, i, :], PWI[:, CHUNK - 1 - i, :])
            link(ins)
            w = [P, PAIRS, CHUNK, GCH]
            tv = [st4[:, 0:1024].rearrange("p (a i h) -> p a i h", a=PAIRS, i=CHUNK) for st4 in TMP4]
            cmul(VBR, VBI, bc(RVR.rearrange("p t a -> p a t").unsqueeze(3), w), bc(RVI.rearrange("p t a -> p a t").unsqueeze(3), w),
                 bc(BBR.unsqueeze(2), w), bc(BBI.unsqueeze(2), w), *tv)
            dve.tensor_copy(sv[:, 20, :], sv[:, 22, :]).then_inc(vb_ok, 1)
            cmul(CAR[:, :, 1:9, :], CAI[:, :, 1:9, :],
                 bc(PWR[:, 1:9, :].rearrange("p t a -> p a t").unsqueeze(3), w),
                 bc(PWI[:, 1:9, :].rearrange("p t a -> p a t").unsqueeze(3), w),
                 bc(CAR[:, :, 0:1, :], w), bc(CAI[:, :, 0:1, :], w), *tv, neg=True)
            dve.tensor_copy(sv[:, 21, :], sv[:, 22, :]).then_inc(ca_ok, 1)
            dve.wait_ge(set_in, 16 * SET_N)
            link(dve.tensor_scalar(nb31[:, :], b31[:, :], -1.0, None, ALU.mult))

            dve.wait_ge(unit_ev, LAST_UNIT[4] + 1)
            for c in range(2):
                dve.tensor_tensor(convh[:, c, :], convh[:, c, :], convo[:, c, :], ALU.mult).then_inc(h_ok, 1)
            dve.wait_ge(vin_ev, 4)
            dve.wait_ge(h_ok, 2)
            for j in range(TAPS - 1, -1, -1):
                s = TAPS - 1 - j
                for c in range(2):
                    acc = banks(2 - 2 * c, 2)
                    if s == 0:
                        ins = dve.tensor_scalar(acc, convh[:, c, :], convw[:, c, j:j + 1], None, ALU.mult)
                    else:
                        dve.wait_ge(tap_c, 2 * s - 1 + c)
                        ins = dve.scalar_tensor_tensor(acc[:, s:L], convh[:, c, 0:L - s], convw[:, c, j:j + 1],
                                                       acc[:, s:L], ALU.mult, ALU.add)
                    ins.then_inc(tap_c if s < TAPS - 1 else conv_ps, 1)
            dve.wait_ge(ud_ok, 1)
            for half in range(2):
                dve.wait_ge(y_ps, half + 1)
                for r in range(2):
                    src = bank(2 * r + half).rearrange("p (g j h) -> p j g h", g=4, j=CHUNK)
                    yv = yc[:, :, P * half:P * half + P].rearrange("p j (g r h) -> p r j g h", g=4, r=2)[:, r]
                    uv = uc[:, 8 * half:8 * half + 8].rearrange("p (g r) j h -> p r j g h", r=2)[:, r]
                    dve.tensor_tensor(yv, src, uv, ALU.add).then_inc(y_ev, 1)

            dve.wait_ge(band_ok, HEADS)

            def stats(k, m):
                h, i = ITEMS[k]
                nk = (i + 1) * P
                far = max(nk - 256, 0)
                sl = 2 * (k % 2) + m
                st_ = smx[:, k % 2, m, :]
                S = banks(2 * m, 2)
                dve.wait_ge(s_ps, 2 * k + m + 1)
                if k >= 2:
                    dve.wait_ge(pT_ps, k - 1)
                ins = dve.tensor_tensor_reduce(out=pexp[:, sl, far:nk], in0=S[:, far:nk], in1=band[:, h, 256 - (nk - far):256],
                                               scale=SCALE, scalar=-3e38, op0=ALU.add, op1=ALU.max, accum_out=st_[:, 0:1])
                if far:
                    link(dve.tensor_reduce(st_[:, 1:2], S[:, 0:far], AX.X, ALU.max))
                    link(dve.tensor_scalar(st_[:, 1:2], st_[:, 1:2], -SCALE, nb31[:, h:h + 1], ALU.mult, ALU.add))
                    link(dve.scalar_tensor_tensor(st_[:, 2:3], st_[:, 0:1], -1.0, st_[:, 1:2], ALU.mult, ALU.min))
                    dve.tensor_tensor(st_[:, 3:4], st_[:, 2:3], b31[:, h:h + 1], ALU.add).then_inc(nm_ok, 1)
                else:
                    link(ins)
                    dve.tensor_scalar(st_[:, 2:3], st_[:, 0:1], -1.0, None, ALU.mult).then_inc(nm_ok, 1)

            def combine(k):
                h, i = ITEMS[k]
                nk = (i + 1) * P
                far = nk > 256
                a, b = smx[:, k % 2, 0, :], smx[:, k % 2, 1, :]
                dve.wait_ge(e_ok, 2 * k + 2)
                if far:
                    dve.tensor_tensor(a[:, 4:5], a[:, 4:5], a[:, 5:6], ALU.add)
                    link(dve.tensor_tensor(b[:, 4:5], b[:, 4:5], b[:, 5:6], ALU.add))
                dve.reciprocal(a[:, 6:7], a[:, 4:5])
                link(dve.reciprocal(b[:, 6:7], b[:, 4:5]))
                dve.tensor_tensor(b[:, 7:8], b[:, 6:7], lam[:, 1:2], ALU.mult)
                p1, p2 = pexp[:, 2 * (k % 2), 0:nk], pexp[:, 2 * (k % 2) + 1, 0:nk]
                link(dve.tensor_scalar(p1, p1, a[:, 6:7], None, ALU.mult))
                dve.scalar_tensor_tensor(p1, p2, b[:, 7:8], p1, ALU.mult, ALU.add).then_inc(p_ok, 1)

            for k in range(ITERS + 2):
                if k < NI:
                    stats(k, 0)
                    stats(k, 1)
                if 1 <= k <= NI:
                    combine(k - 1)
                if k == 4:
                    dve.wait_ge(misc_ev, 4)
                    for i in range(NT):
                        ins = dve.bn_stats(lnst[:, i, :], convt[:, i, :])
                    link(ins)
                    for i in range(NT):
                        ins = dve.bn_aggr(lnmv[:, i, :], lnst[:, i, :])
                    link(ins)
                    dve.tensor_scalar(lnv[:, :], lnmv[:, :, 1], LN_EPS, None, ALU.add).then_inc(ln_var, 1)
                if k == 6:
                    dve.wait_ge(ln_rstd, 1)
                    for i in range(NT):
                        ins = dve.tensor_scalar(convt[:, i, :], convt[:, i, :], lnmv[:, i, 0:1], lnr[:, i:i + 1],
                                                ALU.subtract, ALU.mult)
                    ins.then_inc(ln_ok, 1)
                if 13 <= k < 17:
                    i = k - 13
                    c, half = i // 2, i % 2
                    dve.wait_ge(silu_t, i + 1)
                    link(dve.tensor_scalar(silu[:, i, :], silu[:, i, :], 0.5, 0.5, ALU.mult, ALU.add))
                    z = convo[:, c, 512 * half:512 * half + 512]
                    dve.tensor_tensor(z, z, silu[:, i, :], ALU.mult).then_inc(conv_ok, 1)
                if k == 19:
                    dve.wait_ge(misc_ev, 4 + 4 + 2 + 4)
                    gl = RG[:, 2048:4096]
                    link(dve.tensor_scalar(gl, gl, 0.5, 0.5, ALU.mult, ALU.add))
                    dve.tensor_tensor(RD[:, 6144:8192], RG[:, 4096:6144], gl, ALU.mult).then_inc(ssm_ok, 1)
                if k >= 10 and (k - 10) % NT == 0:
                    h = (k - 10) // NT
                    dve.wait_ge(head_ss, (h + 1) * NT)
                    dve.tensor_scalar(hssv[:, h, :], hss[:, h, :], 1.0 / DV, RMS_EPS, ALU.mult, ALU.add).then_inc(head_var, 1)

            for k in range(NT + 2):
                if k < NT:
                    dve.wait_ge(proj_ps, k + 1)
                    dve.wait_ge(xr_in, 16 * (k + 1))
                    if k == 0:
                        dve.wait_ge(ssm_ok, 1)
                    dve.tensor_tensor(x2[:, k, :], banks(2 * (k % 2), 2), xr[:, :], ALU.add).then_inc(x2_ok, 1)
                    dve.wait_ge(ms2_ok, k + 1)
                    dve.tensor_scalar(ms2v[:, k:k + 1], ms2[:, k:k + 1], 1.0 / D, RMS_EPS, ALU.mult, ALU.add).then_inc(ms2v_ok, 1)
                    dve.wait_ge(rstd2_ok, k + 1)
                    dve.tensor_scalar(mixT[:, :, k * P:(k + 1) * P], x2[:, k, :].rearrange("p (c n) -> p c n", c=KD),
                                      rstd2[:, k:k + 1], None, ALU.mult).then_inc(h2_ok, 1)
                if k >= 2:
                    dve.wait_ge(lg_ps, k - 1)
                    dve.tensor_tensor(logit[:, k - 2, :], psum[:, 4, 0:36], rbias[:, :], ALU.add).then_inc(lg_ok, 1)
                if 1 <= k <= NT:
                    dve.wait_ge(h2T_ps, k)
                    for b in range(2):
                        ins = dve.tensor_tensor(h2T[:, 4 * b:4 * b + 4, :], bank(4 + b).rearrange("p (k n) -> p k n", k=4),
                                                bc(g2k[:, 4 * b:4 * b + 4].unsqueeze(2), [P, 4, P]), ALU.mult)
                    ins.then_inc(h2T_ok, 1)

            dve.wait_ge(lg_ok, NT)
            dve.wait_ge(h2_out, 16 * NT)
            dve.wait_ge(const_ok, 4)
            T8 = [P, NT, 8]
            g8, mx8, e8, me8 = (rrv(x, 64).rearrange("p (t n) -> p t n", t=NT) for x in ("g8", "mx8", "e8", "me8"))
            gi8 = rrv("gi8", 64).bitcast(U32).rearrange("p (t n) -> p t n", t=NT)
            ei8 = rrv("ei8", 64).bitcast(U32).rearrange("p (t n) -> p t n", t=NT)
            gix = rrv("gix", 8)
            goh = rrv("goh", 32).rearrange("p (t n) -> p t n", t=NT)
            gsum, den, gp = rrv("gsum", 8), rrv("den", 8), rrv("gp", 8)
            gexp = rrv("gexp", 32).rearrange("p (t n) -> p t n", t=NT)
            gdif = rrv("gdif", 32).rearrange("p (t n) -> p t n", t=NT)
            edif, eexp = rrv("edif", 8), rrv("eexp", 8)
            gate = rrv("gate", 16).rearrange("p (r t) -> p r t", r=2)
            idx = rrv("idx", 16).rearrange("p (r t) -> p r t", r=2)
            rk, br_, ovs, blk, dst = (rrv(x, 16) for x in ("rk", "br_", "ovs", "blk", "dst"))
            tokm = rrv("tokm", 8)
            link(dve.memset(g8, -3e38))
            link(dve.tensor_copy(g8[:, :, 0:4], logit[:, :, 0:4]))
            for i in range(NT):
                ins = dve.max(mx8[:, i, :], g8[:, i, :])
            link(ins)
            for i in range(NT):
                ins = dve.max_index(gi8[:, i, :], mx8[:, i, :], g8[:, i, :])
            dve.tensor_tensor(gdif, logit[:, :, 0:4], bc(mx8[:, :, 0:1], [P, NT, 4]), ALU.subtract)
            link(dve.tensor_copy(tokm, tokf[:, :]))
            link(dve.tensor_copy(gix.unsqueeze(2), gi8[:, :, 0:1]))
            link(dve.tensor_tensor(goh, bc(gix.unsqueeze(2), [P, NT, 4]), bc(iotaf[:, 0:4].unsqueeze(1), [P, NT, 4]), ALU.is_equal))
            es4 = esel.rearrange("p (t g n) -> p t g n", t=NT, g=4)
            link(dve.tensor_tensor(es4, logit[:, :, 4:36].rearrange("p t (g n) -> p t g n", g=4),
                                   bc(goh.unsqueeze(3), [P, NT, 4, 8]), ALU.mult))
            link(dve.tensor_reduce(e8, es4.rearrange("p t g n -> p t n g"), AX.X, ALU.add))
            for i in range(NT):
                ins = dve.max(me8[:, i, :], e8[:, i, :])
            link(ins)
            for i in range(NT):
                dve.max_index(ei8[:, i, :], me8[:, i, :], e8[:, i, :])
            dve.tensor_tensor(edif.unsqueeze(2), me8[:, :, 1:2], me8[:, :, 0:1], ALU.subtract).then_inc(gd_ok, 1)
            link(dve.memset(dst, 0.0))
            for r in range(2):
                link(dve.tensor_copy(idx[:, r, :].unsqueeze(2), ei8[:, :, r:r + 1]))
                link(dve.scalar_tensor_tensor(idx[:, r, :], gix, float(EPG), idx[:, r, :], ALU.mult, ALU.add))
            idx16 = idx.rearrange("p r t -> p (r t)")
            link(dve.tensor_tensor(MM, bc(idx16.unsqueeze(2), [P, 16, 32]), bc(iotaf[:, 0:32].unsqueeze(1), [P, 16, 32]), ALU.is_equal))
            dve.tensor_tensor(mbf, MM[:, 0:8, :], MM[:, 8:16, :], ALU.add).then_inc(mm_ok, 1)
            dve.wait_ge(ge_ok, 1)
            dve.tensor_reduce(gsum, gexp, AX.X, ALU.add)
            link(dve.tensor_scalar(den, eexp, 1.0, None, ALU.add))
            link(dve.tensor_tensor(den, den, gsum, ALU.mult))
            link(dve.reciprocal(gate[:, 0, :], den))
            link(dve.tensor_tensor(gate[:, 1, :], gate[:, 0, :], eexp, ALU.mult))
            dve.wait_ge(rank_ps, 1)
            dve.tensor_copy(RK[:, :, :].rearrange("p t n -> p (t n)"), bank(0)[:, 0:256])
            cnt = ovt[:, 0:32]
            link(dve.tensor_copy(cnt, bank(1)[:, 0:32]))
            for r in range(2):
                dve.tensor_tensor(MP[:, 8 * r:8 * r + 8, :], MM[:, 8 * r:8 * r + 8, :], RK, ALU.mult)
            nvt = ovt[:, 64:64 + 224].rearrange("p (n j) -> p n j", j=7)
            link(dve.tensor_tensor(nvt, bc(cnt.unsqueeze(2), [P, 32, 7]), bc(thr[:, :].unsqueeze(1), [P, 32, 7]), ALU.is_gt))
            dve.tensor_reduce(rk, MP, AX.X, ALU.add)
            nov_e, ovend, ovstart = ovt[:, 32:64], ovt[:, 288:320], ovt[:, 320:352]
            link(dve.tensor_reduce(nov_e, nvt, AX.X, ALU.add))
            jt = ovt[:, 352:464].rearrange("p (n j) -> p n j", j=7)
            dve.tensor_tensor(jt, bc(rk.unsqueeze(2), [P, 16, 7]), bc(thr[:, :].unsqueeze(1), [P, 16, 7]), ALU.is_ge)
            link(dve.memset(ovt[:, 464:496], 1.0))
            link(dve.tensor_tensor_scan(ovend, ovt[:, 464:496], nov_e, 0.0, ALU.mult, ALU.add))
            dve.tensor_reduce(br_, jt, AX.X, ALU.add)
            link(dve.tensor_tensor(ovstart, ovend, nov_e, ALU.subtract))
            link(dve.tensor_tensor(MP, MM, bc(ovstart.unsqueeze(1), [P, 16, 32]), ALU.mult))
            dve.scalar_tensor_tensor(rk, br_, -float(P), rk, ALU.mult, ALU.add)
            link(dve.tensor_reduce(ovs, MP, AX.X, ALU.add))
            link(dve.tensor_tensor(blk, ovs, br_, ALU.add))
            link(dve.scalar_tensor_tensor(blk, blk, float(EXPERTS - 1), idx16, ALU.add, ALU.subtract))
            link(dve.scalar_tensor_tensor(blk, br_, 0.5, blk, ALU.is_gt, ALU.mult))
            link(dve.tensor_tensor(blk, blk, idx16, ALU.add))
            dve.tensor_tensor(slot1h, bc(rk.unsqueeze(2), [P, 16, P]), bc(iotaf[:, :].unsqueeze(1), [P, 16, P]), ALU.is_equal)
            dve.tensor_scalar(tokm, tokf[:, :], OOB, None, ALU.subtract)
            dve.tensor_scalar(dst[:, 0:8], tokf[:, :], 2.0, OOB, ALU.mult, ALU.subtract)
            dve.tensor_scalar(dst[:, 8:16], tokf[:, :], 2.0, OOB - 1.0, ALU.mult, ALU.subtract)
            link(dve.tensor_tensor(blk1h, bc(blk.unsqueeze(2), [P, 16, NBLK]), bc(iotaf[:, 0:NBLK].unsqueeze(1), [P, 16, NBLK]), ALU.is_equal))
            for r in range(2):
                dve.tensor_tensor(bval[:, 8 * r:8 * r + 8, :, 0], blk1h[:, 8 * r:8 * r + 8, :], bc(tokm.unsqueeze(2), [P, 8, NBLK]), ALU.mult)
            dve.tensor_tensor(bval[:, :, :, 1], blk1h, bc(dst.unsqueeze(2), [P, 16, NBLK]), ALU.mult)
            dve.tensor_tensor(bval[:, :, :, 2], blk1h, bc(gate.rearrange("p r t -> p (r t)").unsqueeze(2), [P, 16, NBLK]), ALU.mult)\
               .then_inc(tab_ok, 1)
            ovx = ovt[:, 0:16]
            ovc = MP.rearrange("p r n -> p (r n)")[:, 0:480].rearrange("p (b n) -> p b n", b=NOVER)
            link(dve.tensor_tensor(ovc, bc(ovend.unsqueeze(1), [P, NOVER, 32]), bc(iotaf[:, 0:NOVER].unsqueeze(2), [P, NOVER, 32]), ALU.is_le))
            link(dve.tensor_reduce(ovx[:, 0:NOVER], ovc, AX.X, ALU.add))
            link(dve.tensor_scalar(nov_i[:, 0:NOVER], ovx[:, 0:NOVER], float(EXPERTS - 1), None, ALU.min))
            link(dve.tensor_copy(nov_i[:, 15:16], ovend[:, 31:32]))
            dve.wait_ge(tab_ps, 1)
            tab = bank(2)[:, 0:3 * NBLK].rearrange("p (n v) -> p v n", v=3)
            dve.tensor_scalar(tabi[:, :, :], tab[:, 0:2, :], OOB, None, ALU.add)
            dve.tensor_copy(tabg[:, :], tab[:, 2, :]).then_inc(idx_ok, 1)

            def xT_evac(v, S):
                dve.wait_ge(S["xT"], v)
                for b in range(2):
                    ins = dve.tensor_tensor(xgT[:, 4 * b:4 * b + 4, :], bank(b).rearrange("p (k n) -> p k n", k=4),
                                            bc(g2e[:, 4 * b:4 * b + 4].unsqueeze(2), [P, 4, P]), ALU.mult)
                ins.then_inc(S["xTe"], 1)

            def act_mul(v, S):
                dve.wait_ge(S["u"], v)
                dve.wait_ge(S["s"], v)
                dve.tensor_tensor(actb, bank(3), actb, ALU.mult).then_inc(S["a"], 1)

            def y_half(s, b, v, S):
                g = tabg[:, b:b + 1] if isinstance(b, int) else tabg[:, bass.ds(b, 1)]
                dve.wait_ge(S["y"], v)
                dve.tensor_scalar(yb[s][:, 512:1024], bank(6), g, None, ALU.mult).then_inc(S["y1"], 1)

            EX = dict(xT=ex_xT, xTe=ex_xTe, u=ex_u, s=ex_s, a=ex_a, y=ex_y, y1=ex_y1)
            OV = dict(xT=ov_xT, xTe=ov_xTe, u=ov_u, s=ov_s, a=ov_a, y=ov_y, y1=ov_y1)
            dve.wait_ge(xg_z, 2)
            xT_evac(1, EX)

            def expert(j, s, scat, last=False):
                e1 = j * 2 + s + 1
                e0 = j * 2 + s
                if not isinstance(e1, int):
                    e0, e1 = dve.snap(e0), dve.snap(e1)
                act_mul(e1, EX)
                if not last:
                    xT_evac(e1 + 1, EX)
                if scat is not None:
                    dve.wait_ge(scat_out[s], scat)
                y_half(s, e0, e1, EX)

            expert(0, 0, None)
            expert(0, 1, None)
            with dve.Fori(1, EXPERTS // 2 - 1) as j:
                for s in range(2):
                    expert(j, s, j * 16)
            expert(EXPERTS // 2 - 1, 0, 16 * (EXPERTS // 2 - 1))
            expert(EXPERTS // 2 - 1, 1, 16 * (EXPERTS // 2 - 1), last=True)
            nov = dve.value_load(nov_i[0:1, 15:16], min_val=0, max_val=NOVER)
            for b in range(NOVER):
                with dve.If(nov > b):
                    for s in range(2):
                        dve.wait_ge(scat_out[s], 16 * (EXPERTS // 2))
                    if b:
                        dve.wait_ge(ov_out, 16 * b)
                    xT_evac(b + 1, OV)
                    act_mul(b + 1, OV)
                    y_half(0, EXPERTS + b, b + 1, OV)
            for i in range(NT + 1):
                if i < NT:
                    x3 = banks(2 * (i % 3), 2)
                    dve.wait_ge(ya_ps, i + 1)
                    dve.tensor_tensor(x3, x3, y2t[:, i % 4, 1, :], ALU.add).then_inc(fin_c, 1)
                    dve.wait_ge(fin_c, i + 1)
                    dve.tensor_tensor(x3, x3, x2[:, i, :], ALU.add).then_inc(x3_ok, 1)
                if i >= 1:
                    if i == 1:
                        dve.wait_ge(fg_in, 16)
                    dve.wait_ge(ms3_ok, i)
                    dve.tensor_scalar(ms3v[:, i - 1:i], ms3[:, i - 1:i], 1.0 / D, RMS_EPS, ALU.mult, ALU.add).then_inc(ms3v_ok, 1)
                    dve.wait_ge(rstd3_ok, i)
                    dve.scalar_tensor_tensor(x2[:, i - 1, :], banks(2 * ((i - 1) % 3), 2), rstd3[:, i - 1:i], fgb,
                                             ALU.mult, ALU.mult).then_inc(fin_ok, 1)


_INS = ["x", "rel_bias", "ln1_g", "w_in", "lam_q1", "lam_k1", "lam_q2", "lam_k2", "subln_g", "conv_w", "conv_b",
        "conv_ln_g", "conv_ln_b", "ssm_lam_re", "ssm_lam_im", "ssm_log_dt", "ssm_b_re", "ssm_b_im", "ssm_c_re",
        "ssm_c_im", "ssm_d", "ssm_glu_w", "ssm_glu_b", "w_out", "ln2_g", "group_router_w", "group_router_b",
        "expert_router_w", "expert_router_b", "w_gate", "w_up", "w_down", "final_g"]


def bucket_onehot():
    rel = 255 - np.arange(384)
    n = np.maximum(rel, 0)
    exact = BUCKETS // 2
    nf = np.maximum(n, 1).astype(np.float32)
    large = exact + (np.log(nf / np.float32(exact)) / np.float32(math.log(128 / exact))
                     * np.float32(BUCKETS - exact)).astype(np.int32)
    bucket = np.where(n < exact, n, np.minimum(large, BUCKETS - 1))
    return ((bucket[None, :] == np.arange(BUCKETS)[:, None]) & (rel >= 0)[None, :]).astype(np.float32)


def kernel(**inputs):
    import concourse.bacc as bacc
    from concourse.bass_utils import run_bass_kernel_spmd

    nc = bacc.Bacc("TRN2", target_bir_lowering=False, num_devices=1)
    arrays, t = {}, {}
    for name in _INS:
        arrays[f"in_{name}"] = np.ascontiguousarray(inputs[name])
    arrays["in_bucket_onehot"] = bucket_onehot()
    for key, a in arrays.items():
        t[key[3:]] = nc.dram_tensor(key, a.shape, mybir.dt.from_np(a.dtype), kind="ExternalInput").ap()
    t["out"] = nc.dram_tensor("out", (1, L, D), F32, kind="ExternalOutput").ap()
    build(nc, t)
    r = run_bass_kernel_spmd(nc, [arrays], core_ids=[0])
    return r.results[0]["out"]
```

```python
import math
from contextlib import ExitStack

import numpy as np

import concourse.bass as bass
import concourse.mybir as mybir
from concourse.mybir import ActivationFunctionType as ACT
from concourse.mybir import AluOpType as ALU
from concourse.mybir import AxisListType as AX

F32 = mybir.dt.float32
BF16 = mybir.dt.bfloat16
I32 = mybir.dt.int32
U32 = mybir.dt.uint32

P = 128
D = 1024
L = 1024
KD = D // P
NT = L // P
HEADS, DK, DV = 4, 64, 128
CH = 256
TAPS = 31
GROUPS, GCH, STATES = 16, 16, 64
PAIRS = GROUPS // 2
CHUNK = 8
NC = L // CHUNK
SCAN_STEPS = int(math.log2(NC))
COLS = 2304
WCH = 256
BUCKETS = 32
EXPERTS, EGROUPS, EPG, FF = 32, 4, 8, 512
FK = FF // P
NOVER = 2 * L // P
NBLK = EXPERTS + NOVER + 2
OOB = float(1 << 20)
RMS_EPS, LN_EPS = 1e-6, 1e-5
SCALE = DK ** -0.5
LAM_INIT = 0.8 - 0.6 * math.exp(0.0)
NEG = -1e30
TWO_PI = (6.28125, 0.0019350051879882812, 3.019915981956753e-07)
ROUND = 12582912.0
PI = 3.1415925

CHUNKS = [(2048, "ssm"), (1024, "v"), (1280, "v"), (1792, "gate"), (1536, "a"),
          (0, "qk"), (256, "qk"), (512, "qk"), (768, "qk")]


def units():
    out = []
    for c, (_, kind) in enumerate(CHUNKS):
        if kind in ("ssm", "v"):
            out += [(c, kind, i) for i in range(NT)]
        else:
            out += [(c, kind, i) for i in range(4)]
    return out


UNITS = units()
LAST_UNIT = {c: max(n for n, u in enumerate(UNITS) if u[0] == c) for c in range(len(CHUNKS))}

MISC_AT = {}
for _n, _job in enumerate([("conv_to_tok", i) for i in range(4)] + [("ssm_to_ch", i) for i in range(4)]
                          + [("conv_to_ch", i) for i in range(4)] + [("head", 0), ("head", 1)]
                          + [("glu", i) for i in range(4)]):
    MISC_AT.setdefault(_n, []).append(_job)
for _n, _job in ((20, 2), (21, 3), (28, 4), (29, 5)):
    MISC_AT.setdefault(_n, []).append(("head", _job))
ITEMS = [(h, i) for h in range(HEADS) for i in range(NT)]
NI = len(ITEMS)
ITERS = NI + 2
MISC_AT[ITERS + 1] = [("head", 6), ("head", 7)]
MISC_ORDER = [j for n in sorted(MISC_AT) for j in MISC_AT[n]]


def build(nc, t):
    with ExitStack() as ctx:
        def sb(name, shape, dt=F32):
            return ctx.enter_context(nc.sbuf_tensor(name, shape, dt))

        def sem(name):
            return ctx.enter_context(nc.semaphore(name))

        band_rows = nc.dram_tensor("band_rows", [HEADS, P, 384], F32, kind="Internal").ap()
        toep_rows = nc.dram_tensor("toep_rows", [GROUPS, GCH, 2 * P], F32, kind="Internal").ap()
        h2_dram = nc.dram_tensor("h2_rows", [L, D], F32, kind="Internal").ap()
        y2_dram = nc.dram_tensor("y2_rows", [2 * L, D], F32, kind="Internal").ap()

        RA = sb("RA", [P, 8192])
        RB = sb("RB", [P, 8192])
        RC = sb("RC", [P, 4096])
        RD = sb("RD", [P, 8192])
        RE = sb("RE", [P, 4096])
        RF = sb("RF", [P, 8192])
        RG = sb("RG", [P, 8192])

        hT = RA[:, :].rearrange("p (k n) -> p k n", k=KD)
        xt = RB[:, :].rearrange("p (t n) -> p t n", t=NT)
        qkT = RB[:, :].rearrange("p (c n) -> p c n", c=8)
        vtok = RC[:, :].rearrange("p (t n) -> p t n", t=NT)
        mixT = RD[:, :].rearrange("p (k n) -> p k n", k=KD)
        win = RF[:, 0:6144].rearrange("p (s k n) -> p s k n", s=3, k=KD)
        wout = RF[:, :].rearrange("p (k n) -> p k n", k=KD)
        x2 = RG[:, :].rearrange("p (t n) -> p t n", t=NT)

        convh = RF[:, 6144:8192].rearrange("p (c n) -> p c n", c=2)
        convt = RF[:, 6144:8192].rearrange("p (t n) -> p t n", t=NT)
        convo = RD[:, 4096:6144].rearrange("p (c n) -> p c n", c=2)
        ssmo = RD[:, 6144:8192].rearrange("p (c n) -> p c n", c=2)

        uc = RG[:, 0:2048].rearrange("p (g i h) -> p g i h", g=GROUPS, i=CHUNK)
        UT = RG[:, 2048:4096].rearrange("p (g c) -> p g c", g=GROUPS)
        XR = RG[:, 4096:5120].rearrange("p (a c) -> p a c", a=PAIRS)
        XI = RG[:, 5120:6144].rearrange("p (a c) -> p a c", a=PAIRS)
        yc = RG[:, 6144:8192].rearrange("p (j n) -> p j n", j=CHUNK)
        gT = RG[:, 4096:6144].rearrange("p (c n) -> p c n", c=2)
        glut = RG[:, 2048:4096].rearrange("p (c n) -> p c n", c=2)
        st = [RG[:, 6144:7168], RG[:, 7168:8192], RD[:, 6144:7168], RD[:, 7168:8192]]
        st = [s.rearrange("p (a c) -> p a c", a=PAIRS) for s in st]
        WinR = RE[:, 0:1024].rearrange("p (a s) -> p a s", a=PAIRS)
        WinI = RE[:, 1024:2048].rearrange("p (a s) -> p a s", a=PAIRS)
        TG = RE[:, 2048:4096].rearrange("p (g n) -> p g n", g=GROUPS)
        CAR = RD[:, 0:1152].rearrange("p (a t h) -> p a t h", a=PAIRS, t=9)
        CAI = RD[:, 1152:2304].rearrange("p (a t h) -> p a t h", a=PAIRS, t=9)
        VBR = RD[:, 6144:7168].rearrange("p (a i h) -> p a i h", a=PAIRS, i=CHUNK)
        VBI = RD[:, 7168:8192].rearrange("p (a i h) -> p a i h", a=PAIRS, i=CHUNK)
        s0 = 2304
        def scratch(n):
            nonlocal s0
            s0 += n
            assert s0 <= 4096
            return RD[:, s0 - n:s0]
        bre = scratch(128).rearrange("p (a h) -> p a h", a=PAIRS)
        bim = scratch(128).rearrange("p (a h) -> p a h", a=PAIRS)
        crow = scratch(256).rearrange("p (r s) -> p r s", r=2)
        BBR = scratch(128).rearrange("p (a h) -> p a h", a=PAIRS)
        BBI = scratch(128).rearrange("p (a h) -> p a h", a=PAIRS)
        PWR = scratch(72).rearrange("p (t a) -> p t a", a=PAIRS)
        PWI = scratch(72).rearrange("p (t a) -> p t a", a=PAIRS)
        RVR = scratch(64).rearrange("p (t a) -> p t a", a=PAIRS)
        RVI = scratch(64).rearrange("p (t a) -> p t a", a=PAIRS)
        sv = scratch(8 * 24).rearrange("p (n a) -> p n a", a=PAIRS)
        lrow = scratch(128)
        ctmp = scratch(256)
        lamv = RG[:, 6144:6400].rearrange("p (v n) -> p v n", v=4)
        onehot = RG[0:BUCKETS, 6400:6784]
        brow = RG[0:HEADS, 6784:7168]
        ksb = RG[:, 7168:8192].rearrange("p (q n) -> p q n", q=4)
        TMP4 = [RF[:, 6144:7168], RF[:, 7168:8192], RE[:, 2048:3072], RE[:, 3072:4096]]
        silu = RG[:, 0:2048].rearrange("p (i n) -> p i n", i=4)

        pexp = RE[:, :].rearrange("p (s n) -> p s n", s=4)
        xg = [RD[:, 0:1024], RD[:, 1024:2048]]
        xgT = RD[:, 2048:3072].rearrange("p (k n) -> p k n", k=KD)
        actb = RD[:, 4096:4608]
        actT = RD[:, 5120:5632].rearrange("p (k n) -> p k n", k=FK)
        yb = [RD[:, 6144:7168], RD[:, 7168:8192]]
        wgate = [RA[:, 0:4096].rearrange("p (k n) -> p k n", k=KD), RB[:, 0:4096].rearrange("p (k n) -> p k n", k=KD)]
        wup = [RA[:, 4096:8192].rearrange("p (k n) -> p k n", k=KD), RB[:, 4096:8192].rearrange("p (k n) -> p k n", k=KD)]
        wdown = [RE[:, :].rearrange("p (k n) -> p k n", k=FK), RC[:, :].rearrange("p (k n) -> p k n", k=FK)]
        r0 = 0
        def route(n):
            nonlocal r0
            r0 += n
            assert r0 <= 8192
            return RD[:, r0 - n:r0]
        slot1h = route(2048).rearrange("p (r n) -> p r n", r=16)
        blk1h = route(16 * NBLK).rearrange("p (r n) -> p r n", r=16)
        bval = route(48 * NBLK).rearrange("p (r n v) -> p r n v", r=16, v=3)
        MM = route(512).rearrange("p (r n) -> p r n", r=16)
        MP = route(512).rearrange("p (r n) -> p r n", r=16)
        RK = route(256).rearrange("p (t n) -> p t n", t=NT)
        esel = route(256)
        rr = route(704)
        RR, _o = {}, 0
        for _name, _n in (("g8", 64), ("mx8", 64), ("e8", 64), ("me8", 64), ("gi8", 64), ("ei8", 64), ("gix", 8), ("goh", 32),
                          ("gsum", 8), ("den", 8), ("gp", 8), ("gexp", 32), ("gdif", 32), ("edif", 8), ("eexp", 8),
                          ("gate", 16), ("idx", 16), ("rk", 16), ("br_", 16), ("ovs", 16), ("blk", 16), ("dst", 16), ("tokm", 8)):
            RR[_name] = rr[:, _o:_o + _n]
            _o += _n
        assert _o <= 704

        def rrv(name, n=None):
            return RR[name]
        mbf = route(128).bitcast(BF16).rearrange("p (t n) -> p t n", t=NT)
        ovt = route(512)

        ident = sb("ident", [P, P])
        tri = sb("tri", [P, P], BF16)
        onesb = sb("onesb", [P, P], BF16)
        band = sb("band", [P, HEADS, 256])
        h2T = band[:, :, :].rearrange("p h n -> p (h n)").rearrange("p (k n) -> p k n", k=KD)
        xr = sb("xr", [P, 1024])
        pT = [xr[:, :].rearrange("p (k n) -> p k n", k=KD), RF[:, 5120:6144].rearrange("p (k n) -> p k n", k=KD)]
        g1 = sb("g1", [P, KD])
        g2k = sb("g2k", [P, KD])
        g2e = sb("g2e", [P, KD])
        rw = sb("rw", [P, KD, 36])
        rbias = sb("rbias", [P, 36])
        gluw = sb("gluw", [P, 2, CH])
        dbc = rw[:, :, :].rearrange("p k n -> p (k n)")[:, 0:CH]
        convw = sb("convw", [P, 2, TAPS])
        convb = sb("convb", [P, 2])
        lng = sb("lng", [P, 2])
        lnb = sb("lnb", [P, 2])
        glub = sb("glub", [P, 2])
        sg = sb("sg", [P, 1])
        b31 = sb("b31", [P, HEADS])
        relt = sb("relt", [BUCKETS, HEADS])
        nb31 = sb("nb31", [P, HEADS])
        lam = sb("lam", [P, 4])
        PDR = sb("PDR", [P, SCAN_STEPS, PAIRS])
        PDI = sb("PDI", [P, SCAN_STEPS, PAIRS])
        mhalf = sb("mhalf", [P, NT])
        ms = sb("ms", [P, NT])
        msv = sb("msv", [P, NT])
        rstd = sb("rstd", [P, NT])
        ms2 = sb("ms2", [P, NT])
        ms2v = sb("ms2v", [P, NT])
        rstd2 = sb("rstd2", [P, NT])
        ms3 = sb("ms3", [P, NT])
        ms3v = sb("ms3v", [P, NT])
        rstd3 = sb("rstd3", [P, NT])
        hss = sb("hss", [P, HEADS, NT])
        hssv = sb("hssv", [P, HEADS, NT])
        hrstd = sb("hrstd", [P, HEADS, NT])
        lnst = sb("lnst", [P, NT, 6])
        lnmv = sb("lnmv", [P, NT, 2])
        lnv = sb("lnv", [P, NT])
        lnr = sb("lnr", [P, NT])
        smx = sb("smx", [P, 2, 2, 8])
        logit = gluw[:, :, :].rearrange("p k n -> p (k n)")[:, 0:NT * 36].rearrange("p (t n) -> p t n", t=NT)
        iotai = RG[:, 0:128].bitcast(I32)
        iotaf = sb("iotaf", [P, P])
        thr = sb("thr", [P, 7])
        toki = RG[:, 128:136].bitcast(I32)
        tokf = sb("tokf", [P, NT])
        tabi = sb("tabi", [P, 2, NBLK], U32)
        tabg = sb("tabg", [P, NBLK])
        cur = sb("cur", [P, 1], U32)
        pdump = sb("pdump", [P, 4])
        nov_i = sb("nov_i", [P, NOVER + 1], I32)

        psum = ctx.enter_context(nc.psum_tensor("psum", [P, 8, 512], F32))
        def bank(i):
            return psum[:, i, :]
        def banks(i, n):
            return psum[:, i:i + n, :].rearrange("p b n -> p (b n)")

        x_in = [sem(f"x_in{i}") for i in range(NT)]
        win_in = [sem(f"win_in{i}") for i in range(3)]
        par_in = sem("par_in")
        set_in = sem("set_in")
        const_ok = sem("const_ok")
        act_c = sem("act_c")
        dve_c = sem("dve_c")
        pool_c = sem("pool_c")
        ms_ok = sem("ms_ok")
        msv_ok = sem("msv_ok")
        rstd_ok = sem("rstd_ok")
        xn_ok = sem("xn_ok")
        xT_ps = sem("xT_ps")
        hT_ok = sem("hT_ok")
        unit_ps = sem("unit_ps")
        unit_ev = sem("unit_ev")
        band_ps = sem("band_ps")
        band_row = sem("band_row")
        band_dram = sem("band_dram")
        band_in = sem("band_in")
        band_ok = sem("band_ok")
        lam_dot = sem("lam_dot")
        lam_exp = sem("lam_exp")
        lam_ok = sem("lam_ok")
        lrow_ps = sem("lrow_ps")
        ssm_dt = sem("ssm_dt")
        ssm_ang = sem("ssm_ang")
        ssm_sin = sem("ssm_sin")
        vb_ok = sem("vb_ok")
        ca_ok = sem("ca_ok")
        uT_ps = sem("uT_ps")
        uT_ev = sem("uT_ev")
        wi_ps = sem("wi_ps")
        wi_ev = sem("wi_ev")
        k_ps = sem("k_ps")
        k_ev = sem("k_ev")
        kz_ok = sem("kz_ok")
        toep_dram = sem("toep_dram")
        toep_in = sem("toep_in")
        vin_ps = sem("vin_ps")
        vin_ev = sem("vin_ev")
        scan_ok = sem("scan_ok")
        ud_ok = sem("ud_ok")
        y_ps = sem("y_ps")
        y_ev = sem("y_ev")
        gelu_ok = sem("gelu_ok")
        glu_half = sem("glu_half")
        ssm_ok = sem("ssm_ok")
        h_ok = sem("h_ok")
        tap_c = sem("tap_c")
        conv_ps = sem("conv_ps")
        conv_ev = sem("conv_ev")
        ln_var = sem("ln_var")
        ln_rstd = sem("ln_rstd")
        ln_ok = sem("ln_ok")
        silu_t = sem("silu_t")
        conv_ok = sem("conv_ok")
        s_ps = sem("s_ps")
        nm_ok = sem("nm_ok")
        e_ok = sem("e_ok")
        p_ok = sem("p_ok")
        pT_ps = sem("pT_ps")
        pT_ev = sem("pT_ev")
        o_ps = sem("o_ps")
        o_ev = sem("o_ev")
        misc_ps = sem("misc_ps")
        misc_ev = sem("misc_ev")
        head_ss = sem("head_ss")
        head_var = sem("head_var")
        head_rstd = sem("head_rstd")
        head_o = sem("head_o")
        rw_in = sem("rw_in")
        wout_in = [sem(f"wout_in{i}") for i in range(3)]
        xr_in = sem("xr_in")
        proj_ps = sem("proj_ps")
        x2_ok = sem("x2_ok")
        ms2_ok = sem("ms2_ok")
        ms2v_ok = sem("ms2v_ok")
        rstd2_ok = sem("rstd2_ok")
        h2_ok = sem("h2_ok")
        h2_out = sem("h2_out")
        h2T_ps = sem("h2T_ps")
        h2T_ok = sem("h2T_ok")
        lg_ps = sem("lg_ps")
        lg_ok = sem("lg_ok")
        gd_ok = sem("gd_ok")
        ge_ok = sem("ge_ok")
        mm_ok = sem("mm_ok")
        rank_ps = sem("rank_ps")
        tab_ok = sem("tab_ok")
        tab_ps = sem("tab_ps")
        idx_ok = sem("idx_ok")
        wgu_in = [sem(f"wgu_in{i}") for i in range(2)]
        wd_in = [sem(f"wd_in{i}") for i in range(2)]
        gather_in = [sem(f"gather_in{i}") for i in range(2)]
        cur_c = sem("cur_c")
        xg_z = sem("xg_z")
        ex_xT = sem("ex_xT")
        ex_xTe = sem("ex_xTe")
        ex_g = sem("ex_g")
        ex_u = sem("ex_u")
        ex_s = sem("ex_s")
        ex_a = sem("ex_a")
        ex_aT = sem("ex_aT")
        ex_aTe = sem("ex_aTe")
        ex_y = sem("ex_y")
        ex_y0 = sem("ex_y0")
        ex_y1 = sem("ex_y1")
        tail_y = sem("tail_y")
        scat_out = [sem(f"scat_out{i}") for i in range(2)]
        moe_done = sem("moe_done")
        fg_in = sem("fg_in")
        y2_in = [sem(f"y2_in{i}") for i in range(4)]
        ya_ps = sem("ya_ps")
        x3_ok = sem("x3_ok")
        ms3_ok = sem("ms3_ok")
        ms3v_ok = sem("ms3v_ok")
        rstd3_ok = sem("rstd3_ok")
        fin_ok = sem("fin_ok")
        fin_c = sem("fin_c")
        fin_out = sem("fin_out")

        fgb = band[:, :, :].rearrange("p h n -> p (h n)")
        y2t = RF[:, :].rearrange("p (s r n) -> p s r n", s=4, r=2)

        def bc(ap, shape):
            return ap.to_broadcast(shape)

        def vec(name, **kw):
            return t[name].rearrange("o (k p) -> (o p) k", **kw)

        par_loads = [
            (g1[:, :], vec("ln1_g", p=P)),
            (relt[:, :], t["rel_bias"]),
            (onehot, t["bucket_onehot"]),
            (lrow[0:8, :], t["ssm_lam_re"][0].rearrange("(a q) s -> a (q s)", q=2)),
            (lrow[8:16, :], t["ssm_lam_im"][0].rearrange("(a q) s -> a (q s)", q=2)),
            (sv[0:64, 0, :], t["ssm_log_dt"].rearrange("o (a q) -> q (o a)", q=2)[0:1, :].to_broadcast([64, PAIRS])),
            (sv[64:128, 0, :], t["ssm_log_dt"].rearrange("o (a q) -> q (o a)", q=2)[1:2, :].to_broadcast([64, PAIRS])),
            (bre, t["ssm_b_re"][0].rearrange("(a q) s h -> (q s) a h", q=2)),
            (bim, t["ssm_b_im"][0].rearrange("(a q) s h -> (q s) a h", q=2)),
        ]
        for r, name in enumerate(("ssm_c_re", "ssm_c_im")):
            for a in range(PAIRS):
                par_loads.append((crow[GCH * a:GCH * (a + 1), r, :].rearrange("h (q s) -> h q s", q=2),
                                  t[name][0, 2 * a:2 * a + 2].rearrange("q h s -> h q s")))
        for v, name in enumerate(("lam_q1", "lam_k1", "lam_q2", "lam_k2")):
            par_loads.append((lamv[:, v, :], t[name].to_broadcast([P, DK])))
        set_loads = [
            (b31[:, :], t["rel_bias"][BUCKETS - 1:BUCKETS, :].to_broadcast([P, HEADS])),
            (dbc[:, :], t["ssm_d"].to_broadcast([P, CH])),
            (convb[:, :], vec("conv_b", p=P)),
            (lng[:, :], vec("conv_ln_g", p=P)),
            (lnb[:, :], vec("conv_ln_b", p=P)),
            (glub[:, :], vec("ssm_glu_b", p=P)),
            (sg[:, :], vec("subln_g", p=P)),
            (gluw[:, :, :], t["ssm_glu_w"][0].rearrange("(k p) n -> p k n", p=P)),
            (g2k[:, :], vec("ln2_g", p=P)),
            (g2e[:, :], t["ln2_g"].rearrange("o (p k) -> (o p) k", p=P)),
            (rbias[:, 0:4], t["group_router_b"].to_broadcast([P, EGROUPS])),
            (rbias[:, 4:36], t["expert_router_b"].to_broadcast([P, EXPERTS])),
        ]
        for c in range(2):
            set_loads.append((convw[:, c, :], t["conv_w"][0].rearrange("j (c p) -> p c j", p=P)[:, c, :]))
        SET_N = len(set_loads)
        PAR_N = len(par_loads)

        block = ctx.enter_context(nc.Block())

        @block.sync
        def _(sp):
            def load_chunk(c):
                src = t["w_in"][0, :, CHUNKS[c][0]:CHUNKS[c][0] + WCH].rearrange("(k p) n -> p k n", p=P)
                if c >= 3:
                    sp.wait_ge(unit_ps, LAST_UNIT[c - 3] + 1)
                sp.dma_start(win[:, c % 3], src).then_inc(win_in[c % 3], 16)

            for i in range(NT):
                sp.dma_start(xt[:, i, :], t["x"][0, i * P:(i + 1) * P, :]).then_inc(x_in[i], 16)
                if i in (1, 3, 5):
                    load_chunk(i // 2)
            sp.wait_ge(band_row, 1)
            sp.dma_start(band_rows, bc(brow[:, :].unsqueeze(1), [HEADS, P, 384])).then_inc(band_dram, 16)
            sp.wait_ge(band_dram, 16)
            sp.dma_start(band[:, :, :], bass.AP(tensor=band_rows.tensor, offset=P - 1,
                                                ap=[[383, P], [384 * P, HEADS], [1, 256]])).then_inc(band_in, 16)
            sp.wait_ge(k_ev, 1)
            sp.wait_ge(kz_ok, 1)
            for r in range(4):
                sp.dma_start(toep_rows.rearrange("(q r) h n -> r h q n", r=4)[r], ksb[32 * r:32 * r + GCH])\
                  .then_inc(toep_dram, 16)
            sp.wait_ge(toep_dram, 64)
            for i in range(CHUNK):
                src = bass.AP(tensor=toep_rows.tensor, offset=P - GCH * i,
                              ap=[[2 * P, GCH], [2 * P * GCH, GROUPS], [1, P]])
                sp.dma_start(TG[GCH * i:GCH * (i + 1)], src).then_inc(toep_in, 16)
            for c in range(3, len(CHUNKS)):
                load_chunk(c)
            sp.wait_ge(unit_ps, len(UNITS))
            wo = t["w_out"][0].rearrange("(k p) n -> p k n", p=P)
            sp.dma_start(wout[:, 0:5], wo[:, 0:5]).then_inc(wout_in[0], 16)

            def load_gu(s, e):
                sp.dma_start(wgate[s], t["w_gate"][0, e].rearrange("(p k) n -> p k n", p=P)).then_inc(wgu_in[s], 16)
                sp.dma_start(wup[s], t["w_up"][0, e].rearrange("(p k) n -> p k n", p=P)).then_inc(wgu_in[s], 16)

            def load_d(s, e):
                sp.dma_start(wdown[s], t["w_down"][0, e].rearrange("(p k) n -> p k n", p=P)).then_inc(wd_in[s], 16)

            load_gu(0, 0)
            sp.wait_ge(conv_ok, 4)
            sp.wait_ge(silu_t, 4)
            sp.dma_start(wout[:, 6:8], wo[:, 6:8]).then_inc(wout_in[2], 16)
            sp.wait_ge(o_ps, NI)
            sp.dma_start(wout[:, 5:6], wo[:, 5:6]).then_inc(wout_in[1], 16)
            load_d(0, 0)
            load_gu(1, 1)
            load_d(1, 1)
            wg = t["w_gate"][0].rearrange("e (p k) n -> e p k n", p=P)
            wu = t["w_up"][0].rearrange("e (p k) n -> e p k n", p=P)
            wd = t["w_down"][0].rearrange("e (p k) n -> e p k n", p=P)

            def reload_gu(s, e, left):
                sp.wait_ge(ex_u, left)
                sp.dma_start(wgate[s], wg[bass.ds(e, 1)].rearrange("e p k n -> (e p) k n")).then_inc(wgu_in[s], 16)
                sp.dma_start(wup[s], wu[bass.ds(e, 1)].rearrange("e p k n -> (e p) k n")).then_inc(wgu_in[s], 16)

            def reload_d(s, e, left):
                sp.wait_ge(ex_y, left)
                sp.dma_start(wdown[s], wd[bass.ds(e, 1)].rearrange("e p k n -> (e p) k n")).then_inc(wd_in[s], 16)

            reload_gu(0, 2, 1)
            with sp.Fori(1, EXPERTS // 2 - 1) as j:
                for s in range(2):
                    e, nxt = sp.snap(j * 2 + s), sp.snap(j * 2 + s + 1)
                    left, nxt_left = sp.snap(j * 2 + s - 1), sp.snap(j * 2 + s)
                    reload_gu(1 - s, nxt, nxt_left)
                    reload_d(s, e, left)
            reload_gu(1, EXPERTS - 1, EXPERTS - 2)
            reload_d(0, EXPERTS - 2, EXPERTS - 3)
            reload_d(1, EXPERTS - 1, EXPERTS - 2)
            sp.wait_ge(idx_ok, 1)
            nov = sp.value_load(nov_i[0:1, NOVER:NOVER + 1], min_val=0, max_val=NOVER)
            for b in range(0, NOVER, 2):
                with sp.If(nov > b):
                    for s in range(2):
                        e = sp.value_load(nov_i[0:1, b + s:b + s + 1], min_val=0, max_val=EXPERTS - 1)
                        reload_gu(s, e, EXPERTS + b + s - 1)
                        reload_d(s, e, EXPERTS + b + s - 1)
            sp.wait_ge(moe_done, 4)
            y2 = y2_dram.rearrange("(n r) d -> n (r d)", r=2)
            for i in range(NT + 2):
                if i < NT:
                    if i >= 4:
                        sp.wait_ge(x3_ok, i - 3)
                    sp.dma_start(y2t[:, i % 4], y2[i * P:(i + 1) * P, :].rearrange("p (r d) -> p r d", r=2)).then_inc(y2_in[i % 4], 16)
                if i >= 2:
                    sp.wait_ge(fin_ok, i - 1)
                    sp.dma_start(t["out"][0, (i - 2) * P:(i - 1) * P, :], x2[:, i - 2, :]).then_inc(fin_out, 16)
            sp.wait_ge(fin_out, 16 * NT)

        @block.gpsimd
        def _(pool):
            n = [0]
            def link(ins):
                n[0] += 1
                ins.then_inc(pool_c, 1)
                pool.wait_ge(pool_c, n[0])

            link(pool.memset(ident[:, :], 0.0))
            pool.affine_select(out=ident[:, :], in_=ident[:, :], compare_op=ALU.not_equal, fill=1.0, base=0,
                               pattern=[[-1, P]], channel_multiplier=1).then_inc(const_ok, 1)
            pool.memset(mhalf[:, :], -0.5).then_inc(const_ok, 1)
            for r in range(4):
                pool.wait_ge(msv_ok, r + 1)
                if r == 0:
                    pool.wait_ge(const_ok, 2)
                pool.tensor_tensor(rstd[:, 2 * r:2 * r + 2], msv[:, 2 * r:2 * r + 2], mhalf[:, 0:2], ALU.pow)\
                    .then_inc(rstd_ok, 1)
            pool.memset(ksb[:, :, 0:P], 0.0).then_inc(kz_ok, 1)
            link(pool.memset(onesb[:, :], 1.0))
            link(pool.memset(tri[:, :], 1.0))
            pool.affine_select(out=tri[:, :], in_=tri[:, :], compare_op=ALU.is_gt, fill=0.0, base=0,
                               pattern=[[1, P]], channel_multiplier=-1).then_inc(const_ok, 1)
            link(pool.iota(iotai[:, :], pattern=[[1, P]], base=0, channel_multiplier=0))
            link(pool.iota(toki[:, :], pattern=[[P, NT]], base=0, channel_multiplier=1))
            link(pool.tensor_copy(iotaf[:, :], iotai[:, :]))
            link(pool.tensor_copy(tokf[:, :], toki[:, :]))
            pool.tensor_scalar(thr[:, :], iotaf[:, 1:8], float(P), None, ALU.mult).then_inc(const_ok, 1)
            pool.wait_ge(band_in, 16)
            for h in range(HEADS):
                pool.affine_select(out=band[:, h, :], in_=band[:, h, :], compare_op=ALU.is_ge, fill=NEG / SCALE,
                                   base=P, pattern=[[-1, 256]], channel_multiplier=1).then_inc(band_ok, 1)
            pool.wait_ge(set_in, SET_N * 16)
            pool.wait_ge(uT_ps, 4)
            pool.tensor_tensor(uc, uc, bc(dbc.rearrange("p (g h) -> p g h", h=GCH).unsqueeze(2), [P, GROUPS, CHUNK, GCH]), ALU.mult).then_inc(ud_ok, 1)
            pool.wait_ge(vin_ev, 4)
            pool.wait_ge(toep_dram, 64)
            pool.wait_ge(band_dram, 16)
            for k in range(SCAN_STEPS):
                d = 1 << k
                w = [P, PAIRS, NC - d]
                pr = bc(PDR[:, k, :].unsqueeze(2), w)
                pi = bc(PDI[:, k, :].unsqueeze(2), w)
                a = [s[:, :, 0:NC - d] for s in st]
                xrs, xis = XR[:, :, 0:NC - d], XI[:, :, 0:NC - d]
                pool.tensor_tensor(a[0], xrs, pr, ALU.mult)
                pool.tensor_tensor(a[1], xis, pi, ALU.mult)
                pool.tensor_tensor(a[2], xrs, pi, ALU.mult)
                link(pool.tensor_tensor(a[3], xis, pr, ALU.mult))
                pool.tensor_tensor(a[0], a[0], a[1], ALU.subtract)
                link(pool.tensor_tensor(a[2], a[2], a[3], ALU.add))
                pool.tensor_tensor(XR[:, :, d:NC], XR[:, :, d:NC], a[0], ALU.add)
                ins = pool.tensor_tensor(XI[:, :, d:NC], XI[:, :, d:NC], a[2], ALU.add)
                if k < SCAN_STEPS - 1:
                    link(ins)
                else:
                    ins.then_inc(scan_ok, 1)
            pool.wait_ge(ln_var, 1)
            pool.tensor_tensor(lnr[:, :], lnv[:, :], mhalf[:, :], ALU.pow).then_inc(ln_rstd, 1)
            for h in range(HEADS):
                pool.wait_ge(head_var, h + 1)
                pool.tensor_tensor(hrstd[:, h, :], hssv[:, h, :], mhalf[:, :], ALU.pow).then_inc(head_rstd, 1)
                pool.wait_ge(head_rstd, h + 1)
                o = mixT[:, h, :].rearrange("p (i v) -> p i v", i=NT)
                pool.tensor_tensor(o, o, bc(hrstd[:, h, :].unsqueeze(2), [P, NT, DV]), ALU.mult).then_inc(head_o, 1)
            for i in range(NT):
                pool.wait_ge(ms2v_ok, i + 1)
                pool.tensor_tensor(rstd2[:, i:i + 1], ms2v[:, i:i + 1], mhalf[:, 0:1], ALU.pow).then_inc(rstd2_ok, 1)

            pool.wait_ge(tab_ps, 1)
            pool.memset(xg[0], 0.0).then_inc(xg_z, 1)
            pool.memset(xg[1], 0.0).then_inc(xg_z, 1)
            pool.wait_ge(h2_out, 16 * NT)
            pool.wait_ge(xg_z, 2)

            def gather(b):
                pool.indirect_dma_start(xg[b % 2], None, h2_dram,
                                        bass.IndirectOffsetOnAxis(ap=tabi[:, 0, b:b + 1], axis=0),
                                        bounds_check=L - 1, oob_is_err=False).then_inc(gather_in[b % 2], 16)

            def scatter(rows, s):
                pool.indirect_dma_start(y2_dram, bass.IndirectOffsetOnAxis(ap=rows, axis=0),
                                        yb[s], None, bounds_check=2 * L - 1, oob_is_err=False).then_inc(scat_out[s], 16)

            def block_io(b):
                pool.wait_ge(ex_xT, b + 1)
                gather(b + 2)
                if b:
                    pool.wait_ge(ex_y0, b)
                    pool.wait_ge(ex_y1, b)
                    scatter(tabi[:, 1, b - 1:b], (b - 1) % 2)

            pool.wait_ge(idx_ok, 1)
            gather(0)
            gather(1)
            for b in range(EXPERTS):
                block_io(b)
            nov = pool.value_load(nov_i[0:1, NOVER:NOVER + 1], min_val=0, max_val=NOVER)
            for b in range(EXPERTS, EXPERTS + NOVER, 2):
                with pool.If(nov > b - EXPERTS):
                    block_io(b)
                    block_io(b + 1)
            pool.tensor_copy(cur[:, 0:1], tabi[:, 1, bass.ds(nov + (EXPERTS - 1), 1)]).then_inc(cur_c, 1)
            pool.wait_ge(tail_y, 2)
            pool.wait_ge(cur_c, 1)
            scatter(cur[:, 0:1], 1)
            scat_all = pool.snap(nov * 8 + 16 * (EXPERTS // 2))
            gath_all = pool.snap(nov * 8 + 16 * (EXPERTS // 2 + 1))
            for n, (done, val) in enumerate(((scat_out[0], scat_all), (scat_out[1], scat_all),
                                             (gather_in[0], gath_all), (gather_in[1], gath_all))):
                pool.wait_ge(done, val)
                pool.tensor_tensor(pdump[:, n:n + 1], mhalf[:, 0:1], mhalf[:, 0:1], ALU.add).then_inc(moe_done, 1)
            for i in range(NT):
                pool.wait_ge(ms3v_ok, i + 1)
                pool.tensor_tensor(rstd3[:, i:i + 1], ms3v[:, i:i + 1], mhalf[:, 0:1], ALU.pow).then_inc(rstd3_ok, 1)

        @block.scalar
        def _(act):
            n = [0]
            def link(ins):
                n[0] += 1
                ins.then_inc(act_c, 1)
                act.wait_ge(act_c, n[0])

            for dst, src in par_loads:
                act.dma_start(dst, src, allow_slow_non_contiguous=True).then_inc(par_in, 16)
            for i in range(NT):
                act.wait_ge(x_in[i], 16)
                if i:
                    act.wait_ge(ms_ok, i)
                act.activation(xr[:, :], xt[:, i, :], ACT.Square, accum_out=ms[:, i:i + 1]).then_inc(ms_ok, 1)
            for dst, src in set_loads:
                act.dma_start(dst, src, allow_slow_non_contiguous=True).then_inc(set_in, 16)
            act.wait_ge(band_ps, 1)
            act.activation(brow[:, :], psum[0:HEADS, 6, 0:384], ACT.Copy, scale=1.0 / SCALE).then_inc(band_row, 1)
            act.wait_ge(lam_dot, 1)
            act.activation(lam[:, 2:4], lam[:, 0:2], ACT.Exp).then_inc(lam_exp, 1)
            act.wait_ge(par_in, 16 * PAR_N)
            act.activation(sv[:, 1, :], sv[:, 0, :], ACT.Exp).then_inc(ssm_dt, 1)
            act.wait_ge(ssm_ang, 1)
            act.activation(sv[:, 6, :], sv[:, 4, :], ACT.Exp)
            act.activation(sv[:, 7, :], sv[:, 5, :], ACT.Sin)
            act.activation(sv[:, 8, :], sv[:, 5, :], ACT.Sin, scale=0.5).then_inc(ssm_sin, 1)

            def evac(u):
                _, kind, i = UNITS[u]
                src = bank(4 + u % 4)
                act.wait_ge(unit_ps, u + 1)
                if kind == "ssm":
                    act.activation(uc[:, :, i, :], src[:, 0:CH].rearrange("p (g h) -> p g h", h=GCH), ACT.Copy).then_inc(unit_ev, 1)
                elif kind == "v":
                    c0 = CHUNKS[UNITS[u][0]][0] - 1024
                    act.activation(vtok[:, i, c0:c0 + WCH], src[:, 0:WCH], ACT.Copy).then_inc(unit_ev, 1)
                elif kind == "gate":
                    act.activation(convo[:, i // 2, 512 * (i % 2):512 * (i % 2) + 512], src, ACT.Sigmoid).then_inc(unit_ev, 1)
                elif kind == "a":
                    act.activation(convh[:, i // 2, 512 * (i % 2):512 * (i % 2) + 512], src, ACT.Copy).then_inc(unit_ev, 1)
                else:
                    c = 2 * (UNITS[u][0] - 5) + i // 2
                    if u == LAST_UNIT[4] + 1:
                        act.wait_ge(xT_ps, NT)
                    act.activation(qkT[:, c, 512 * (i % 2):512 * (i % 2) + 512], src, ACT.Copy).then_inc(unit_ev, 1)

            act.wait_ge(const_ok, 4)
            for u in range(0, 16):
                evac(u)
            for i in range(4):
                act.wait_ge(uT_ps, i + 1)
                act.activation(UT[:, 4 * i:4 * i + 4, :].rearrange("p g c -> p (g c)"), bank(i), ACT.Copy).then_inc(uT_ev, 1)
            for i in range(4):
                act.wait_ge(wi_ps, i + 1)
                dst = (WinR, WinI)[i // 2]
                act.activation(dst[:, 4 * (i % 2):4 * (i % 2) + 4, :].rearrange("p a s -> p (a s)"), bank(i), ACT.Copy).then_inc(wi_ev, 1)
            act.wait_ge(k_ps, 1)
            act.wait_ge(kz_ok, 1)
            for r in range(4):
                ins = act.activation(ksb[32 * r:32 * r + GCH, :, P:2 * P],
                                     psum[32 * r:32 * r + GCH, 0, :].rearrange("p (q n) -> p q n", q=4), ACT.Copy)
            ins.then_inc(k_ev, 1)
            for u in range(16, LAST_UNIT[3] + 1):
                evac(u)
            act.memzero(XR[:, :, 0:1])
            act.memzero(XI[:, :, 0:1])
            for i in range(4):
                act.wait_ge(vin_ps, i + 1)
                dst = (XR, XI)[i // 2]
                act.activation(dst[:, 4 * (i % 2):4 * (i % 2) + 4, 1:NC],
                               bank(i % 2).rearrange("p (a c) -> p a c", a=4)[:, :, 0:NC - 1], ACT.Copy).then_inc(vin_ev, 1)
            for u in range(LAST_UNIT[3] + 1, len(UNITS)):
                evac(u)
            act.wait_ge(set_in, 16 * SET_N)
            for c in range(2):
                act.wait_ge(conv_ps, c + 1)
                act.activation(convo[:, c, :], banks(2 - 2 * c, 2), ACT.Identity, bias=convb[:, c:c + 1]).then_inc(conv_ev, 1)
            act.wait_ge(y_ev, 4)
            act.activation(RG[:, 6144:8192], RG[:, 6144:8192], ACT.Gelu_apprx_tanh).then_inc(gelu_ok, 1)

            act.dma_start(rw[:, :, 0:4], t["group_router_w"][0].rearrange("(k p) n -> p k n", p=P)).then_inc(rw_in, 16)
            act.dma_start(rw[:, :, 4:36], t["expert_router_w"][0].rearrange("(k p) n -> p k n", p=P)).then_inc(rw_in, 16)
            link(act.activation(sg[:, :], sg[:, :], ACT.Copy, scale=1.0 - LAM_INIT))
            nm = [0]

            def misc(job):
                kind, i = job
                nm[0] += 1
                act.wait_ge(misc_ps, nm[0])
                src = bank(7)
                if kind == "conv_to_tok":
                    ins = act.activation(convt[:, 2 * i:2 * i + 2, :].rearrange("p t n -> p (t n)"), src, ACT.Copy)
                elif kind == "ssm_to_ch":
                    c, jh = i // 2, i % 2
                    dst = gT[:, c, :].rearrange("p (n j) -> p j n", j=CHUNK)[:, 4 * jh:4 * jh + 4, :]
                    ins = act.activation(dst, src.rearrange("p (j n) -> p j n", j=4), ACT.Copy)
                elif kind == "conv_to_ch":
                    c, half = i // 2, i % 2
                    z = convo[:, c, 512 * half:512 * half + 512]
                    link(act.activation(z, src, ACT.Identity, bias=lnb[:, c:c + 1], scale=lng[:, c:c + 1]))
                    act.activation(silu[:, i, :], z, ACT.Tanh, scale=0.5).then_inc(silu_t, 1)
                    ins = None
                elif kind == "glu":
                    c, half = i // 2, i % 2
                    ins = act.activation(glut[:, c, 512 * half:512 * half + 512], src, ACT.Tanh,
                                         bias=glub[:, c:c + 1], scale=0.5)
                else:
                    h, half = i // 2, i % 2
                    ins = act.activation(mixT[:, h, 512 * half:512 * half + 512], src, ACT.Copy, scale=sg[:, 0:1])
                return ins

            link(act.activation(glub[:, :], glub[:, :], ACT.Copy, scale=0.5))

            def exps(k):
                h, i = ITEMS[k]
                nk = (i + 1) * P
                far = max(nk - 256, 0)
                for m in range(2):
                    act.wait_ge(nm_ok, 2 * k + m + 1)
                    sl = 2 * (k % 2) + m
                    st_ = smx[:, k % 2, m, :]
                    ins = act.activation(pexp[:, sl, far:nk], pexp[:, sl, far:nk], ACT.Exp,
                                         bias=st_[:, 2:3], accum_out=st_[:, 4:5])
                    if far:
                        ins = act.activation(pexp[:, sl, 0:far], banks(2 * m, 2)[:, 0:far], ACT.Exp,
                                             bias=st_[:, 3:4], scale=SCALE, accum_out=st_[:, 5:6])
                    ins.then_inc(e_ok, 1)

            def p_evac(k):
                h, i = ITEMS[k]
                act.wait_ge(pT_ps, k + 1)
                act.activation(pT[k % 2][:, 0:i + 1, :].rearrange("p k n -> p (k n)"),
                               banks(4, 2)[:, 0:(i + 1) * P], ACT.Copy).then_inc(pT_ev, 1)

            def o_evac(k):
                h, i = ITEMS[k]
                act.wait_ge(o_ps, k + 1)
                o = mixT[:, h, i * P:(i + 1) * P]
                act.activation(o, psum[:, 6, 0:P], ACT.Copy).then_inc(o_ev, 1)
                act.activation(psum[:, 6, P:2 * P], psum[:, 6, 0:P], ACT.Square, accum_out=hss[:, h, i:i + 1]).then_inc(head_ss, 1)

            for k in range(ITERS + 2):
                if k < NI:
                    exps(k)
                if 1 <= k <= NI:
                    p_evac(k - 1)
                if 2 <= k < NI + 2:
                    if k >= 3:
                        act.wait_ge(head_ss, k - 2)
                    o_evac(k - 2)
                for job in MISC_AT.get(k, []):
                    ins = misc(job)
                    if ins is not None:
                        ins.then_inc(misc_ev, 1)

            def reload(i):
                if i:
                    act.wait_ge(x2_ok, i)
                act.dma_start(xr[:, :], t["x"][0, i * P:(i + 1) * P, :]).then_inc(xr_in, 16)

            act.wait_ge(head_ss, NI)
            reload(0)
            for i in range(NT):
                act.wait_ge(x2_ok, i + 1)
                if i + 1 < NT:
                    reload(i + 1)
                if i:
                    act.wait_ge(ms2_ok, i)
                act.activation(banks(6, 2), x2[:, i, :], ACT.Square, accum_out=ms2[:, i:i + 1]).then_inc(ms2_ok, 1)
                act.wait_ge(h2_ok, i + 1)
                act.dma_start(h2_dram[i * P:(i + 1) * P, :].rearrange("p (k n) -> p k n", k=KD),
                              mixT[:, :, i * P:(i + 1) * P]).then_inc(h2_out, 16)
            act.wait_ge(gd_ok, 1)
            act.activation(rrv("gexp"), rrv("gdif"), ACT.Exp)
            act.activation(rrv("eexp"), rrv("edif"), ACT.Exp).then_inc(ge_ok, 1)

            def actT_evac(done):
                act.wait_ge(ex_aT, done)
                act.activation(actT[:, :, :].rearrange("p k n -> p (k n)"), bank(4), ACT.Copy).then_inc(ex_aTe, 1)

            def silu_gate(done):
                act.wait_ge(ex_g, done)
                act.activation(actb, bank(2), ACT.Silu).then_inc(ex_s, 1)

            def y_half(s, b, down, scat, done):
                gate = tabg[:, b:b + 1] if isinstance(b, int) else tabg[:, bass.ds(b, 1)]
                act.wait_ge(ex_y, down)
                if scat is not None:
                    act.wait_ge(scat_out[s], scat)
                act.activation(yb[s][:, 0:512], bank(5), ACT.Copy, scale=gate).then_inc(done, 1)

            def step(j, s):
                b = j * 2 + s
                prev, b1 = j * 2 + s - 1, j * 2 + s + 1
                scat = (j - 1 + s) * 16
                if not isinstance(b, int):
                    b, prev, b1, scat = act.snap(b), act.snap(prev), act.snap(b1), act.snap(scat)
                actT_evac(b)
                silu_gate(b1)
                y_half(1 - s, prev, b, None if isinstance(scat, int) and scat == 0 else scat, ex_y0)

            act.wait_ge(idx_ok, 1)
            silu_gate(1)
            step(0, 1)
            step(1, 0)
            step(1, 1)
            with act.Fori(2, EXPERTS // 2) as j:
                for s in range(2):
                    step(j, s)
            nov = act.value_load(nov_i[0:1, NOVER:NOVER + 1], min_val=0, max_val=NOVER)
            for b in range(0, NOVER, 2):
                with act.If(nov > b):
                    for s in range(2):
                        step((EXPERTS + b) // 2, s)
            blocks, last = act.snap(nov + EXPERTS), act.snap(nov + (EXPERTS - 1))
            scat = act.snap(nov * 8 + 16 * (EXPERTS // 2 - 1))
            actT_evac(blocks)
            y_half(1, last, blocks, scat, tail_y)
            act.dma_start(fgb, t["final_g"].rearrange("(o d) -> o d", o=1).to_broadcast([P, D])).then_inc(fg_in, 16)
            act.wait_ge(moe_done, 4)
            for i in range(NT + 1):
                if i < NT:
                    act.wait_ge(y2_in[i % 4], 16 * (i // 4 + 1))
                    if i >= 3:
                        act.wait_ge(fin_ok, i - 2)
                    act.activation(banks(2 * (i % 3), 2), y2t[:, i % 4, 0, :], ACT.Copy).then_inc(ya_ps, 1)
                if i >= 1:
                    act.wait_ge(x3_ok, i)
                    if i >= 2:
                        act.wait_ge(ms3_ok, i - 1)
                    act.activation(banks(6, 2), banks(2 * ((i - 1) % 3), 2), ACT.Square,
                                   accum_out=ms3[:, i - 1:i]).then_inc(ms3_ok, 1)

        @block.tensor
        def _(pe):
            pe.wait_ge(const_ok, 1)
            pe.wait_ge(par_in, 16 * PAR_N)
            pe.matmul(psum[0:HEADS, 6, 0:384], relt[:, :], onehot, start=True, stop=True).then_inc(band_ps, 1)
            pe.transpose(psum[:, 7, 0:16], lrow[0:16, :], ident[0:16, 0:16])
            pe.transpose(psum[:, 7, 128:256], crow[:, 0, :], ident[:, :])
            pe.transpose(psum[:, 7, 256:384], crow[:, 1, :], ident[:, :]).then_inc(lrow_ps, 1)
            for i in range(NT):
                pe.wait_ge(xn_ok, i + 1)
                if i >= 2:
                    pe.wait_ge(hT_ok, 2 * (i - 1))
                for k in range(KD):
                    ins = pe.transpose(psum[:, 2 * (i % 2) + k // 4, P * (k % 4):P * (k % 4) + P],
                                       xt[:, i, k * P:(k + 1) * P], ident[:, :])
                ins.then_inc(xT_ps, 1)
            pe.wait_ge(hT_ok, 2 * NT)
            pe.wait_ge(band_row, 1)
            pe.wait_ge(lam_ok, 1)
            chunk_seen = [-1]

            def unit(u):
                c, kind, i = UNITS[u]
                if chunk_seen[0] != c:
                    chunk_seen[0] = c
                    pe.wait_ge(win_in[c % 3], 16 * (c // 3 + 1))
                if u >= 4:
                    pe.wait_ge(unit_ev, u - 3)
                w = win[:, c % 3]
                for k in range(KD):
                    first, last = k == 0, k == KD - 1
                    if kind == "ssm":
                        ins = pe.matmul(bank(4 + u % 4)[:, 0:WCH], hT[:, k, i:L:CHUNK], w[:, k, :], start=first, stop=last)
                    elif kind == "v":
                        ins = pe.matmul(bank(4 + u % 4)[:, 0:WCH], hT[:, k, i * P:(i + 1) * P], w[:, k, :], start=first, stop=last)
                    else:
                        ct, half = i // 2, i % 2
                        ins = pe.matmul(bank(4 + u % 4), w[:, k, ct * P:(ct + 1) * P],
                                        hT[:, k, 512 * half:512 * half + 512], start=first, stop=last)
                ins.then_inc(unit_ps, 1)

            for u in range(16):
                unit(u)
            pe.wait_ge(unit_ev, 8)
            for g in range(GROUPS):
                ins = pe.transpose(psum[:, g // 4, P * (g % 4):P * (g % 4) + P],
                                   uc[:, g].rearrange("p i h -> p (i h)"), ident[:, :])
                if g % 4 == 3:
                    ins.then_inc(uT_ps, 1)
            pe.wait_ge(vb_ok, 1)
            for r, vb in enumerate((VBR, VBI)):
                for a in range(PAIRS):
                    b = 2 * r + a // 4
                    if a % 4 == 0:
                        pe.wait_ge(uT_ev, b + 1)
                    ins = pe.transpose(psum[:, b, P * (a % 4):P * (a % 4) + P],
                                       vb[:, a].rearrange("p i h -> p (i h)"), ident[:, :])
                    if a % 4 == 3:
                        ins.then_inc(wi_ps, 1)
            pe.wait_ge(ca_ok, 1)
            pe.wait_ge(wi_ev, 1)
            for g in range(GROUPS):
                a, q = g // 2, STATES * (g % 2)
                out = psum[32 * (g % 4):32 * (g % 4) + GCH, 0, P * (g // 4):P * (g // 4) + P]
                pe.matmul(out, BBR[q:q + STATES, a, :], CAR[q:q + STATES, a, 0:CHUNK, :].rearrange("p t h -> p (t h)"),
                          start=True, stop=False)
                ins = pe.matmul(out, BBI[q:q + STATES, a, :], CAI[q:q + STATES, a, 0:CHUNK, :].rearrange("p t h -> p (t h)"),
                                start=False, stop=True)
            ins.then_inc(k_ps, 1)
            for u in range(16, LAST_UNIT[3] + 1):
                unit(u)
            pe.wait_ge(k_ev, 1)
            pe.wait_ge(wi_ev, 4)
            for r, win_ in enumerate((WinR, WinI)):
                for a in range(PAIRS):
                    b = a // 4
                    if r == 1 and a % 4 == 0:
                        pe.wait_ge(vin_ev, b + 1)
                    for q in range(2):
                        ins = pe.matmul(psum[STATES * q:STATES * (q + 1), b, P * (a % 4):P * (a % 4) + P],
                                        win_[:, a, STATES * q:STATES * (q + 1)], UT[:, 2 * a + q, :], start=True, stop=True)
                    if a % 4 == 3:
                        ins.then_inc(vin_ps, 1)
            for u in range(LAST_UNIT[3] + 1, len(UNITS)):
                unit(u)
            pe.wait_ge(scan_ok, 1)
            pe.wait_ge(toep_in, 16 * CHUNK)
            pe.wait_ge(conv_ev, 2)
            for g in range(GROUPS):
                a, q = g // 2, STATES * (g % 2)
                b, c = 2 * (g % 2) + g // 8, (g // 2) % 4
                out = psum[:, b, P * c:P * c + P]
                pe.matmul(out, XR[q:q + STATES, a, :], CAR[q:q + STATES, a, 1:CHUNK + 1, :].rearrange("p t h -> p (t h)"),
                          start=True, stop=False)
                pe.matmul(out, XI[q:q + STATES, a, :], CAI[q:q + STATES, a, 1:CHUNK + 1, :].rearrange("p t h -> p (t h)"),
                          start=False, stop=False)
                ins = pe.matmul(out, UT[:, g, :], TG[:, g, :], start=False, stop=True)
                if g % 8 == 7:
                    ins.then_inc(y_ps, 1)

            nm = [0]

            def misc(job):
                kind, i = job
                if nm[0] and MISC_ORDER[nm[0] - 1][0] != "conv_to_ch":
                    pe.wait_ge(misc_ev, sum(1 for j in MISC_ORDER[:nm[0]] if j[0] != "conv_to_ch"))
                elif nm[0]:
                    pe.wait_ge(silu_t, sum(1 for j in MISC_ORDER[:nm[0]] if j[0] == "conv_to_ch"))
                nm[0] += 1
                if kind == "conv_to_tok":
                    for k in range(4):
                        tt, c = 2 * i + k // 2, k % 2
                        ins = pe.transpose(psum[:, 7, P * k:P * k + P], convo[:, c, tt * P:(tt + 1) * P], ident[:, :])
                elif kind == "ssm_to_ch":
                    pe.wait_ge(gelu_ok, 1)
                    c, jh = i // 2, i % 2
                    for k in range(4):
                        ins = pe.transpose(psum[:, 7, P * k:P * k + P], yc[:, 4 * jh + k, c * P:(c + 1) * P], ident[:, :])
                elif kind == "conv_to_ch":
                    pe.wait_ge(ln_ok, 1)
                    c, half = i // 2, i % 2
                    for k in range(4):
                        ins = pe.transpose(psum[:, 7, P * k:P * k + P], convt[:, 4 * half + k, c * P:(c + 1) * P], ident[:, :])
                elif kind == "glu":
                    c, half = i // 2, i % 2
                    for k in range(2):
                        ins = pe.matmul(bank(7), gluw[:, k, c * P:(c + 1) * P], gT[:, k, 512 * half:512 * half + 512],
                                        start=k == 0, stop=k == 1)
                else:
                    h, half = i // 2, i % 2
                    pe.wait_ge(head_o, h + 1)
                    for k in range(4):
                        ins = pe.transpose(psum[:, 7, P * k:P * k + P],
                                           mixT[:, h, (4 * half + k) * P:(4 * half + k + 1) * P], ident[:, :])
                ins.then_inc(misc_ps, 1)

            pe.wait_ge(set_in, 16 * SET_N)
            pe.wait_ge(unit_ev, len(UNITS))
            pe.wait_ge(y_ev, 4)
            for k in range(ITERS + 2):
                if k < NI:
                    h, i = ITEMS[k]
                    q = DK * (h % 2)
                    nk = (i + 1) * P
                    for m in range(2):
                        if k:
                            pe.wait_ge(e_ok, 2 * (k - 1) + m + 1)
                        for b in range(0, nk, 512):
                            w = min(512, nk - b)
                            ins = pe.matmul(psum[:, 2 * m + b // 512, 0:w],
                                            qkT[q:q + DK, 2 * m + h // 2, i * P:(i + 1) * P],
                                            qkT[q:q + DK, 4 + 2 * m + h // 2, b:b + w], start=True, stop=True)
                        ins.then_inc(s_ps, 1)
                if 1 <= k <= NI:
                    i = ITEMS[k - 1][1]
                    pe.wait_ge(p_ok, k)
                    if k >= 2:
                        pe.wait_ge(pT_ev, k - 1)
                    for c in range(i + 1):
                        ins = pe.transpose(psum[:, 4 + c // 4, P * (c % 4):P * (c % 4) + P],
                                           pexp[:, 2 * ((k - 1) % 2), c * P:(c + 1) * P], ident[:, :])
                    ins.then_inc(pT_ps, 1)
                if 2 <= k < NI + 2:
                    h, i = ITEMS[k - 2]
                    pe.wait_ge(pT_ev, k - 1)
                    if k >= 3:
                        pe.wait_ge(head_ss, k - 2)
                    for c in range(i + 1):
                        ins = pe.matmul(psum[:, 6, 0:P], pT[k % 2][:, c, :], vtok[:, c, h * DV:(h + 1) * DV],
                                        start=c == 0, stop=c == i)
                    ins.then_inc(o_ps, 1)
                for job in MISC_AT.get(k, []):
                    misc(job)

            for s in range(3):
                pe.wait_ge(wout_in[s], 16)
            pe.wait_ge(rw_in, 32)
            pe.wait_ge(misc_ev, sum(1 for j in MISC_ORDER if j[0] != "conv_to_ch"))
            pe.wait_ge(conv_ok, 4)
            pe.wait_ge(ssm_ok, 1)
            for k in range(NT + 2):
                if k < NT:
                    if k >= 2:
                        pe.wait_ge(x2_ok, k - 1)
                    for half in range(2):
                        for c in range(KD):
                            ins = pe.matmul(bank(2 * (k % 2) + half), mixT[:, c, k * P:(k + 1) * P],
                                            wout[:, c, 512 * half:512 * half + 512], start=c == 0, stop=c == KD - 1)
                    ins.then_inc(proj_ps, 1)
                if k >= 2:
                    pe.wait_ge(h2T_ok, k - 1)
                    if k >= 3:
                        pe.wait_ge(lg_ok, k - 2)
                    for c in range(KD):
                        ins = pe.matmul(psum[:, 4, 0:36], h2T[:, c, :], rw[:, c, :], start=c == 0, stop=c == KD - 1)
                    ins.then_inc(lg_ps, 1)
                if 1 <= k <= NT:
                    pe.wait_ge(h2_ok, k)
                    if k >= 2:
                        pe.wait_ge(lg_ok, k - 1)
                    for c in range(4):
                        pe.transpose(psum[:, 4, P * c:P * c + P], mixT[:, c, (k - 1) * P:k * P], ident[:, :])
                    for c in range(4):
                        ins = pe.transpose(psum[:, 5, P * c:P * c + P], mixT[:, 4 + c, (k - 1) * P:k * P], ident[:, :])
                    ins.then_inc(h2T_ps, 1)

            pe.wait_ge(mm_ok, 1)
            pe.wait_ge(const_ok, 3)
            pe.matmul(bank(0)[:, 0:256], tri[:, :], mbf[:, :, :].rearrange("p t n -> p (t n)"), start=True, stop=False)
            for s in range(1, NT):
                pe.matmul(bank(0)[:, 32 * s:256], onesb[:, :], mbf[:, 0:NT - s, :].rearrange("p t n -> p (t n)"),
                          start=False, stop=s == NT - 1)
            for i in range(NT):
                ins = pe.matmul(bank(1)[:, 0:32], onesb[:, :], mbf[:, i, :], start=i == 0, stop=i == NT - 1)
            ins.then_inc(rank_ps, 1)
            pe.wait_ge(tab_ok, 1)
            for r in range(16):
                ins = pe.matmul(bank(2)[:, 0:3 * NBLK], slot1h[:, r, :], bval[:, r].rearrange("p n v -> p (n v)"),
                                start=r == 0, stop=r == 15)
            ins.then_inc(tab_ps, 1)

            def xT(s, got):
                pe.wait_ge(gather_in[s], got)
                for k in range(KD):
                    ins = pe.transpose(psum[:, k // 4, P * (k % 4):P * (k % 4) + P],
                                       xg[s].rearrange("p (n k) -> p k n", k=KD)[:, k, :], ident[:, :])
                ins.then_inc(ex_xT, 1)

            def product(b, w, done):
                for k in range(KD):
                    ins = pe.matmul(bank(b), xgT[:, k, :], w[:, k, :], start=k == 0, stop=k == KD - 1)
                ins.then_inc(done, 1)

            def aT(a, freed):
                pe.wait_ge(ex_a, a)
                if freed is not None:
                    pe.wait_ge(ex_aTe, freed)
                for k in range(FK):
                    ins = pe.transpose(psum[:, 4, P * k:P * k + P],
                                       actb.rearrange("p (n k) -> p k n", k=FK)[:, k, :], ident[:, :])
                ins.then_inc(ex_aT, 1)

            def down(s, aTe, loaded, freed):
                pe.wait_ge(ex_aTe, aTe)
                pe.wait_ge(wd_in[s], loaded)
                if freed is not None:
                    pe.wait_ge(ex_y0, freed)
                    pe.wait_ge(ex_y1, freed)
                for half in range(2):
                    for k in range(FK):
                        ins = pe.matmul(bank(5 + half), actT[:, k, :], wdown[s][:, k, 512 * half:512 * half + 512],
                                        start=k == 0, stop=k == FK - 1)
                ins.then_inc(ex_y, 1)

            def step(j, s):
                first = isinstance(j, int) and j == 0 and s == 0
                b, prev, b1 = j * 2 + s, j * 2 + s - 1, j * 2 + s + 1
                if not isinstance(b, int):
                    b, prev, b1 = pe.snap(b), pe.snap(prev), pe.snap(b1)
                freed = None if isinstance(prev, int) and prev == 0 else prev
                pe.wait_ge(ex_xTe, b1)
                pe.wait_ge(wgu_in[s], (j + 1) * 32)
                if not first:
                    pe.wait_ge(ex_s, b)
                product(2, wgate[s], ex_g)
                if not first:
                    aT(b, freed)
                product(3, wup[s], ex_u)
                xT(1 - s, (j + 1 + s) * 16)
                if not first:
                    down(1 - s, b, (j + s) * 16, freed)

            pe.wait_ge(idx_ok, 1)
            xT(0, 16)
            step(0, 0)
            step(0, 1)
            with pe.Fori(1, EXPERTS // 2) as j:
                for s in range(2):
                    step(j, s)
            nov = pe.value_load(nov_i[0:1, NOVER:NOVER + 1], min_val=0, max_val=NOVER)
            for b in range(0, NOVER, 2):
                with pe.If(nov > b):
                    for s in range(2):
                        step((EXPERTS + b) // 2, s)
            blocks, last, loaded = pe.snap(nov + EXPERTS), pe.snap(nov + (EXPERTS - 1)), pe.snap(nov * 8 + 16 * (EXPERTS // 2))
            aT(blocks, last)
            down(1, blocks, loaded, last)

        @block.vector
        def _(dve):
            n = [0]
            def link(ins):
                n[0] += 1
                ins.then_inc(dve_c, 1)
                dve.wait_ge(dve_c, n[0])

            def norm_pair(r):
                dve.wait_ge(ms_ok, 2 * r + 2)
                dve.tensor_scalar(msv[:, 2 * r:2 * r + 2], ms[:, 2 * r:2 * r + 2], 1.0 / D, RMS_EPS, ALU.mult, ALU.add)\
                   .then_inc(msv_ok, 1)
                dve.wait_ge(rstd_ok, r + 1)
                for i in (2 * r, 2 * r + 1):
                    dve.tensor_scalar(xt[:, i, :], xt[:, i, :], rstd[:, i:i + 1], None, ALU.mult).then_inc(xn_ok, 1)

            def hT_evac(i):
                dve.wait_ge(xT_ps, i + 1)
                if i == 0:
                    dve.wait_ge(par_in, 16 * PAR_N)
                for b in range(2):
                    dve.tensor_tensor(hT[:, 4 * b:4 * b + 4, i * P:(i + 1) * P],
                                      bank(2 * (i % 2) + b).rearrange("p (k n) -> p k n", k=4),
                                      bc(g1[:, 4 * b:4 * b + 4].unsqueeze(2), [P, 4, P]), ALU.mult).then_inc(hT_ok, 1)

            norm_pair(0)
            for r in range(1, 4):
                norm_pair(r)
                hT_evac(2 * r - 2)
                hT_evac(2 * r - 1)
            hT_evac(6)
            hT_evac(7)

            dve.wait_ge(par_in, 16 * PAR_N)
            for v in range(2):
                ins = dve.tensor_tensor_reduce(out=ctmp[:, 64 * v:64 * v + DK], in0=lamv[:, 2 * v, :], in1=lamv[:, 2 * v + 1, :],
                                               scale=1.0, scalar=0.0, op0=ALU.mult, op1=ALU.add, accum_out=lam[:, v:v + 1])
            ins.then_inc(lam_dot, 1)
            dve.wait_ge(lrow_ps, 1)
            dve.tensor_copy(sv[:, 2:4, :].rearrange("p n a -> p (n a)"), psum[:, 7, 0:16])
            c4 = psum[:, 7, 128:384].rearrange("p (r a h) -> p r a h", r=2, a=PAIRS)
            dve.tensor_copy(CAR[:, :, 0, :], c4[:, 0])
            link(dve.tensor_scalar(CAI[:, :, 0, :], c4[:, 1], -1.0, None, ALU.mult))
            dve.wait_ge(lam_exp, 1)
            link(dve.tensor_tensor(lam[:, 0:1], lam[:, 3:4], lam[:, 2:3], ALU.subtract))
            dve.tensor_scalar(lam[:, 1:2], lam[:, 0:1], LAM_INIT, None, ALU.subtract).then_inc(lam_ok, 1)
            dve.wait_ge(ssm_dt, 1)
            dve.tensor_tensor(sv[:, 4, :], sv[:, 2, :], sv[:, 1, :], ALU.mult)
            link(dve.tensor_tensor(sv[:, 9, :], sv[:, 3, :], sv[:, 1, :], ALU.mult))
            link(dve.tensor_scalar(sv[:, 10, :], sv[:, 9, :], 1.0 / (2.0 * math.pi), ROUND, ALU.mult, ALU.add))
            link(dve.tensor_scalar(sv[:, 10, :], sv[:, 10, :], ROUND, None, ALU.subtract))
            for c in TWO_PI:
                link(dve.scalar_tensor_tensor(sv[:, 9, :], sv[:, 10, :], -c, sv[:, 9, :], ALU.mult, ALU.add))
            dve.tensor_scalar(sv[:, 5, :], sv[:, 9, :], PI, -PI, ALU.min, ALU.max).then_inc(ssm_ang, 1)
            dve.tensor_tensor(sv[:, 11, :], sv[:, 2, :], sv[:, 2, :], ALU.mult)
            link(dve.tensor_tensor(sv[:, 12, :], sv[:, 3, :], sv[:, 3, :], ALU.mult))
            link(dve.tensor_tensor(sv[:, 11, :], sv[:, 11, :], sv[:, 12, :], ALU.add))
            link(dve.reciprocal(sv[:, 13, :], sv[:, 11, :]))
            dve.wait_ge(ssm_sin, 1)
            link(dve.scalar_tensor_tensor(sv[:, 14, :], sv[:, 8, :], -2.0, sv[:, 8, :], ALU.mult, ALU.mult))
            dve.scalar_tensor_tensor(PWR[:, 1, :], sv[:, 14, :], 1.0, sv[:, 6, :], ALU.add, ALU.mult)
            dve.tensor_tensor(PWI[:, 1, :], sv[:, 6, :], sv[:, 7, :], ALU.mult)
            dve.memset(PWR[:, 0, :], 1.0)
            link(dve.memset(PWI[:, 0, :], 0.0))
            link(dve.tensor_scalar(sv[:, 15, :], PWR[:, 1, :], 1.0, None, ALU.subtract))
            dve.tensor_tensor(sv[:, 16, :], sv[:, 15, :], sv[:, 2, :], ALU.mult)
            dve.tensor_tensor(sv[:, 17, :], PWI[:, 1, :], sv[:, 3, :], ALU.mult)
            dve.tensor_tensor(sv[:, 18, :], PWI[:, 1, :], sv[:, 2, :], ALU.mult)
            link(dve.tensor_tensor(sv[:, 19, :], sv[:, 15, :], sv[:, 3, :], ALU.mult))
            dve.tensor_tensor(sv[:, 20, :], sv[:, 16, :], sv[:, 17, :], ALU.add)
            link(dve.tensor_tensor(sv[:, 21, :], sv[:, 18, :], sv[:, 19, :], ALU.subtract))
            dve.tensor_tensor(sv[:, 22, :], sv[:, 20, :], sv[:, 13, :], ALU.mult)
            link(dve.tensor_tensor(sv[:, 23, :], sv[:, 21, :], sv[:, 13, :], ALU.mult))

            def cmul(outr, outi, ar, ai, br, bi, t1, t2, t3, t4, neg=False):
                dve.tensor_tensor(t1, ar, br, ALU.mult)
                dve.tensor_tensor(t2, ai, bi, ALU.mult)
                dve.tensor_tensor(t3, ar, bi, ALU.mult)
                link(dve.tensor_tensor(t4, ai, br, ALU.mult))
                dve.tensor_tensor(outr, t1, t2, ALU.add if neg else ALU.subtract)
                link(dve.tensor_tensor(outi, t3, t4, ALU.subtract if neg else ALU.add))

            tm = [ctmp[:, 64 * q:64 * q + 32] for q in range(4)]

            def small(q, k):
                return tm[q][:, 0:8 * k].rearrange("p (t a) -> p t a", a=PAIRS)

            for base in (1, 2, 4):
                w = [P, base, PAIRS]
                cmul(PWR[:, base + 1:2 * base + 1, :], PWI[:, base + 1:2 * base + 1, :],
                     bc(PWR[:, base:base + 1, :], w), bc(PWI[:, base:base + 1, :], w),
                     PWR[:, 1:base + 1, :], PWI[:, 1:base + 1, :], *[small(q, base) for q in range(4)])
            dve.tensor_copy(PDR[:, 0, :], PWR[:, 8, :])
            link(dve.tensor_copy(PDI[:, 0, :], PWI[:, 8, :]))
            for k in range(SCAN_STEPS - 1):
                cmul(PDR[:, k + 1:k + 2, :], PDI[:, k + 1:k + 2, :], PDR[:, k:k + 1, :], PDI[:, k:k + 1, :],
                     PDR[:, k:k + 1, :], PDI[:, k:k + 1, :], *[small(q, 1) for q in range(4)])
            w = [P, PAIRS, GCH]
            tb = [st4[:, 0:128].rearrange("p (a h) -> p a h", a=PAIRS) for st4 in TMP4]
            cmul(BBR, BBI, bc(sv[:, 22, :].unsqueeze(2), w), bc(sv[:, 23, :].unsqueeze(2), w), bre, bim, *tb)
            for i in range(CHUNK):
                dve.tensor_copy(RVR[:, i, :], PWR[:, CHUNK - 1 - i, :])
                ins = dve.tensor_copy(RVI[:, i, :], PWI[:, CHUNK - 1 - i, :])
            link(ins)
            w = [P, PAIRS, CHUNK, GCH]
            tv = [st4[:, 0:1024].rearrange("p (a i h) -> p a i h", a=PAIRS, i=CHUNK) for st4 in TMP4]
            cmul(VBR, VBI, bc(RVR.rearrange("p t a -> p a t").unsqueeze(3), w), bc(RVI.rearrange("p t a -> p a t").unsqueeze(3), w),
                 bc(BBR.unsqueeze(2), w), bc(BBI.unsqueeze(2), w), *tv)
            dve.tensor_copy(sv[:, 20, :], sv[:, 22, :]).then_inc(vb_ok, 1)
            cmul(CAR[:, :, 1:9, :], CAI[:, :, 1:9, :],
                 bc(PWR[:, 1:9, :].rearrange("p t a -> p a t").unsqueeze(3), w),
                 bc(PWI[:, 1:9, :].rearrange("p t a -> p a t").unsqueeze(3), w),
                 bc(CAR[:, :, 0:1, :], w), bc(CAI[:, :, 0:1, :], w), *tv, neg=True)
            dve.tensor_copy(sv[:, 21, :], sv[:, 22, :]).then_inc(ca_ok, 1)
            dve.wait_ge(set_in, 16 * SET_N)
            link(dve.tensor_scalar(nb31[:, :], b31[:, :], -1.0, None, ALU.mult))

            dve.wait_ge(unit_ev, LAST_UNIT[4] + 1)
            for c in range(2):
                dve.tensor_tensor(convh[:, c, :], convh[:, c, :], convo[:, c, :], ALU.mult).then_inc(h_ok, 1)
            dve.wait_ge(vin_ev, 4)
            dve.wait_ge(h_ok, 2)
            for j in range(TAPS - 1, -1, -1):
                s = TAPS - 1 - j
                for c in range(2):
                    acc = banks(2 - 2 * c, 2)
                    if s == 0:
                        ins = dve.tensor_scalar(acc, convh[:, c, :], convw[:, c, j:j + 1], None, ALU.mult)
                    else:
                        dve.wait_ge(tap_c, 2 * s - 1 + c)
                        ins = dve.scalar_tensor_tensor(acc[:, s:L], convh[:, c, 0:L - s], convw[:, c, j:j + 1],
                                                       acc[:, s:L], ALU.mult, ALU.add)
                    ins.then_inc(tap_c if s < TAPS - 1 else conv_ps, 1)
            dve.wait_ge(ud_ok, 1)
            for half in range(2):
                dve.wait_ge(y_ps, half + 1)
                for r in range(2):
                    src = bank(2 * r + half).rearrange("p (g j h) -> p j g h", g=4, j=CHUNK)
                    yv = yc[:, :, P * half:P * half + P].rearrange("p j (g r h) -> p r j g h", g=4, r=2)[:, r]
                    uv = uc[:, 8 * half:8 * half + 8].rearrange("p (g r) j h -> p r j g h", r=2)[:, r]
                    dve.tensor_tensor(yv, src, uv, ALU.add).then_inc(y_ev, 1)

            dve.wait_ge(band_ok, HEADS)

            def stats(k, m):
                h, i = ITEMS[k]
                nk = (i + 1) * P
                far = max(nk - 256, 0)
                sl = 2 * (k % 2) + m
                st_ = smx[:, k % 2, m, :]
                S = banks(2 * m, 2)
                dve.wait_ge(s_ps, 2 * k + m + 1)
                if k >= 2:
                    dve.wait_ge(pT_ps, k - 1)
                ins = dve.tensor_tensor_reduce(out=pexp[:, sl, far:nk], in0=S[:, far:nk], in1=band[:, h, 256 - (nk - far):256],
                                               scale=SCALE, scalar=-3e38, op0=ALU.add, op1=ALU.max, accum_out=st_[:, 0:1])
                if far:
                    link(dve.tensor_reduce(st_[:, 1:2], S[:, 0:far], AX.X, ALU.max))
                    link(dve.tensor_scalar(st_[:, 1:2], st_[:, 1:2], -SCALE, nb31[:, h:h + 1], ALU.mult, ALU.add))
                    link(dve.scalar_tensor_tensor(st_[:, 2:3], st_[:, 0:1], -1.0, st_[:, 1:2], ALU.mult, ALU.min))
                    dve.tensor_tensor(st_[:, 3:4], st_[:, 2:3], b31[:, h:h + 1], ALU.add).then_inc(nm_ok, 1)
                else:
                    link(ins)
                    dve.tensor_scalar(st_[:, 2:3], st_[:, 0:1], -1.0, None, ALU.mult).then_inc(nm_ok, 1)

            def combine(k):
                h, i = ITEMS[k]
                nk = (i + 1) * P
                far = nk > 256
                a, b = smx[:, k % 2, 0, :], smx[:, k % 2, 1, :]
                dve.wait_ge(e_ok, 2 * k + 2)
                if far:
                    dve.tensor_tensor(a[:, 4:5], a[:, 4:5], a[:, 5:6], ALU.add)
                    link(dve.tensor_tensor(b[:, 4:5], b[:, 4:5], b[:, 5:6], ALU.add))
                dve.reciprocal(a[:, 6:7], a[:, 4:5])
                link(dve.reciprocal(b[:, 6:7], b[:, 4:5]))
                dve.tensor_tensor(b[:, 7:8], b[:, 6:7], lam[:, 1:2], ALU.mult)
                p1, p2 = pexp[:, 2 * (k % 2), 0:nk], pexp[:, 2 * (k % 2) + 1, 0:nk]
                link(dve.tensor_scalar(p1, p1, a[:, 6:7], None, ALU.mult))
                dve.scalar_tensor_tensor(p1, p2, b[:, 7:8], p1, ALU.mult, ALU.add).then_inc(p_ok, 1)

            for k in range(ITERS + 2):
                if k < NI:
                    stats(k, 0)
                    stats(k, 1)
                if 1 <= k <= NI:
                    combine(k - 1)
                if k == 4:
                    dve.wait_ge(misc_ev, 4)
                    for i in range(NT):
                        ins = dve.bn_stats(lnst[:, i, :], convt[:, i, :])
                    link(ins)
                    for i in range(NT):
                        ins = dve.bn_aggr(lnmv[:, i, :], lnst[:, i, :])
                    link(ins)
                    dve.tensor_scalar(lnv[:, :], lnmv[:, :, 1], LN_EPS, None, ALU.add).then_inc(ln_var, 1)
                if k == 6:
                    dve.wait_ge(ln_rstd, 1)
                    for i in range(NT):
                        ins = dve.tensor_scalar(convt[:, i, :], convt[:, i, :], lnmv[:, i, 0:1], lnr[:, i:i + 1],
                                                ALU.subtract, ALU.mult)
                    ins.then_inc(ln_ok, 1)
                if 13 <= k < 17:
                    i = k - 13
                    c, half = i // 2, i % 2
                    dve.wait_ge(silu_t, i + 1)
                    link(dve.tensor_scalar(silu[:, i, :], silu[:, i, :], 0.5, 0.5, ALU.mult, ALU.add))
                    z = convo[:, c, 512 * half:512 * half + 512]
                    dve.tensor_tensor(z, z, silu[:, i, :], ALU.mult).then_inc(conv_ok, 1)
                if k == 19:
                    dve.wait_ge(misc_ev, 4 + 4 + 2 + 4)
                    gl = RG[:, 2048:4096]
                    link(dve.tensor_scalar(gl, gl, 0.5, 0.5, ALU.mult, ALU.add))
                    dve.tensor_tensor(RD[:, 6144:8192], RG[:, 4096:6144], gl, ALU.mult).then_inc(ssm_ok, 1)
                if k >= 10 and (k - 10) % NT == 0:
                    h = (k - 10) // NT
                    dve.wait_ge(head_ss, (h + 1) * NT)
                    dve.tensor_scalar(hssv[:, h, :], hss[:, h, :], 1.0 / DV, RMS_EPS, ALU.mult, ALU.add).then_inc(head_var, 1)

            for k in range(NT + 2):
                if k < NT:
                    dve.wait_ge(proj_ps, k + 1)
                    dve.wait_ge(xr_in, 16 * (k + 1))
                    if k == 0:
                        dve.wait_ge(ssm_ok, 1)
                    dve.tensor_tensor(x2[:, k, :], banks(2 * (k % 2), 2), xr[:, :], ALU.add).then_inc(x2_ok, 1)
                    dve.wait_ge(ms2_ok, k + 1)
                    dve.tensor_scalar(ms2v[:, k:k + 1], ms2[:, k:k + 1], 1.0 / D, RMS_EPS, ALU.mult, ALU.add).then_inc(ms2v_ok, 1)
                    dve.wait_ge(rstd2_ok, k + 1)
                    dve.tensor_scalar(mixT[:, :, k * P:(k + 1) * P], x2[:, k, :].rearrange("p (c n) -> p c n", c=KD),
                                      rstd2[:, k:k + 1], None, ALU.mult).then_inc(h2_ok, 1)
                if k >= 2:
                    dve.wait_ge(lg_ps, k - 1)
                    dve.tensor_tensor(logit[:, k - 2, :], psum[:, 4, 0:36], rbias[:, :], ALU.add).then_inc(lg_ok, 1)
                if 1 <= k <= NT:
                    dve.wait_ge(h2T_ps, k)
                    for b in range(2):
                        ins = dve.tensor_tensor(h2T[:, 4 * b:4 * b + 4, :], bank(4 + b).rearrange("p (k n) -> p k n", k=4),
                                                bc(g2k[:, 4 * b:4 * b + 4].unsqueeze(2), [P, 4, P]), ALU.mult)
                    ins.then_inc(h2T_ok, 1)

            dve.wait_ge(lg_ok, NT)
            dve.wait_ge(h2_out, 16 * NT)
            dve.wait_ge(const_ok, 4)
            T8 = [P, NT, 8]
            g8, mx8, e8, me8 = (rrv(x, 64).rearrange("p (t n) -> p t n", t=NT) for x in ("g8", "mx8", "e8", "me8"))
            gi8 = rrv("gi8", 64).bitcast(U32).rearrange("p (t n) -> p t n", t=NT)
            ei8 = rrv("ei8", 64).bitcast(U32).rearrange("p (t n) -> p t n", t=NT)
            gix = rrv("gix", 8)
            goh = rrv("goh", 32).rearrange("p (t n) -> p t n", t=NT)
            gsum, den, gp = rrv("gsum", 8), rrv("den", 8), rrv("gp", 8)
            gexp = rrv("gexp", 32).rearrange("p (t n) -> p t n", t=NT)
            gdif = rrv("gdif", 32).rearrange("p (t n) -> p t n", t=NT)
            edif, eexp = rrv("edif", 8), rrv("eexp", 8)
            gate = rrv("gate", 16).rearrange("p (r t) -> p r t", r=2)
            idx = rrv("idx", 16).rearrange("p (r t) -> p r t", r=2)
            rk, br_, ovs, blk, dst = (rrv(x, 16) for x in ("rk", "br_", "ovs", "blk", "dst"))
            tokm = rrv("tokm", 8)
            link(dve.memset(g8, -3e38))
            link(dve.tensor_copy(g8[:, :, 0:4], logit[:, :, 0:4]))
            for i in range(NT):
                ins = dve.max(mx8[:, i, :], g8[:, i, :])
            link(ins)
            for i in range(NT):
                ins = dve.max_index(gi8[:, i, :], mx8[:, i, :], g8[:, i, :])
            dve.tensor_tensor(gdif, logit[:, :, 0:4], bc(mx8[:, :, 0:1], [P, NT, 4]), ALU.subtract)
            link(dve.tensor_copy(tokm, tokf[:, :]))
            link(dve.tensor_copy(gix.unsqueeze(2), gi8[:, :, 0:1]))
            link(dve.tensor_tensor(goh, bc(gix.unsqueeze(2), [P, NT, 4]), bc(iotaf[:, 0:4].unsqueeze(1), [P, NT, 4]), ALU.is_equal))
            es4 = esel.rearrange("p (t g n) -> p t g n", t=NT, g=4)
            link(dve.tensor_tensor(es4, logit[:, :, 4:36].rearrange("p t (g n) -> p t g n", g=4),
                                   bc(goh.unsqueeze(3), [P, NT, 4, 8]), ALU.mult))
            link(dve.tensor_reduce(e8, es4.rearrange("p t g n -> p t n g"), AX.X, ALU.add))
            for i in range(NT):
                ins = dve.max(me8[:, i, :], e8[:, i, :])
            link(ins)
            for i in range(NT):
                dve.max_index(ei8[:, i, :], me8[:, i, :], e8[:, i, :])
            dve.tensor_tensor(edif.unsqueeze(2), me8[:, :, 1:2], me8[:, :, 0:1], ALU.subtract).then_inc(gd_ok, 1)
            link(dve.memset(dst, 0.0))
            for r in range(2):
                link(dve.tensor_copy(idx[:, r, :].unsqueeze(2), ei8[:, :, r:r + 1]))
                link(dve.scalar_tensor_tensor(idx[:, r, :], gix, float(EPG), idx[:, r, :], ALU.mult, ALU.add))
            idx16 = idx.rearrange("p r t -> p (r t)")
            link(dve.tensor_tensor(MM, bc(idx16.unsqueeze(2), [P, 16, 32]), bc(iotaf[:, 0:32].unsqueeze(1), [P, 16, 32]), ALU.is_equal))
            dve.tensor_tensor(mbf, MM[:, 0:8, :], MM[:, 8:16, :], ALU.add).then_inc(mm_ok, 1)
            dve.wait_ge(ge_ok, 1)
            dve.tensor_reduce(gsum, gexp, AX.X, ALU.add)
            link(dve.tensor_scalar(den, eexp, 1.0, None, ALU.add))
            link(dve.tensor_tensor(den, den, gsum, ALU.mult))
            link(dve.reciprocal(gate[:, 0, :], den))
            link(dve.tensor_tensor(gate[:, 1, :], gate[:, 0, :], eexp, ALU.mult))
            dve.wait_ge(rank_ps, 1)
            dve.tensor_copy(RK[:, :, :].rearrange("p t n -> p (t n)"), bank(0)[:, 0:256])
            cnt = ovt[:, 0:32]
            link(dve.tensor_copy(cnt, bank(1)[:, 0:32]))
            for r in range(2):
                dve.tensor_tensor(MP[:, 8 * r:8 * r + 8, :], MM[:, 8 * r:8 * r + 8, :], RK, ALU.mult)
            nvt = ovt[:, 64:64 + 224].rearrange("p (n j) -> p n j", j=7)
            link(dve.tensor_tensor(nvt, bc(cnt.unsqueeze(2), [P, 32, 7]), bc(thr[:, :].unsqueeze(1), [P, 32, 7]), ALU.is_gt))
            dve.tensor_reduce(rk, MP, AX.X, ALU.add)
            nov_e, ovend, ovstart = ovt[:, 32:64], ovt[:, 288:320], ovt[:, 320:352]
            link(dve.tensor_reduce(nov_e, nvt, AX.X, ALU.add))
            jt = ovt[:, 352:464].rearrange("p (n j) -> p n j", j=7)
            dve.tensor_tensor(jt, bc(rk.unsqueeze(2), [P, 16, 7]), bc(thr[:, :].unsqueeze(1), [P, 16, 7]), ALU.is_ge)
            link(dve.memset(ovt[:, 464:496], 1.0))
            link(dve.tensor_tensor_scan(ovend, ovt[:, 464:496], nov_e, 0.0, ALU.mult, ALU.add))
            dve.tensor_reduce(br_, jt, AX.X, ALU.add)
            link(dve.tensor_tensor(ovstart, ovend, nov_e, ALU.subtract))
            link(dve.tensor_tensor(MP, MM, bc(ovstart.unsqueeze(1), [P, 16, 32]), ALU.mult))
            dve.scalar_tensor_tensor(rk, br_, -float(P), rk, ALU.mult, ALU.add)
            link(dve.tensor_reduce(ovs, MP, AX.X, ALU.add))
            link(dve.tensor_tensor(blk, ovs, br_, ALU.add))
            link(dve.scalar_tensor_tensor(blk, blk, float(EXPERTS - 1), idx16, ALU.add, ALU.subtract))
            link(dve.scalar_tensor_tensor(blk, br_, 0.5, blk, ALU.is_gt, ALU.mult))
            link(dve.tensor_tensor(blk, blk, idx16, ALU.add))
            dve.tensor_tensor(slot1h, bc(rk.unsqueeze(2), [P, 16, P]), bc(iotaf[:, :].unsqueeze(1), [P, 16, P]), ALU.is_equal)
            dve.tensor_scalar(tokm, tokf[:, :], OOB, None, ALU.subtract)
            dve.tensor_scalar(dst[:, 0:8], tokf[:, :], 2.0, OOB, ALU.mult, ALU.subtract)
            dve.tensor_scalar(dst[:, 8:16], tokf[:, :], 2.0, OOB - 1.0, ALU.mult, ALU.subtract)
            link(dve.tensor_tensor(blk1h, bc(blk.unsqueeze(2), [P, 16, NBLK]), bc(iotaf[:, 0:NBLK].unsqueeze(1), [P, 16, NBLK]), ALU.is_equal))
            for r in range(2):
                dve.tensor_tensor(bval[:, 8 * r:8 * r + 8, :, 0], blk1h[:, 8 * r:8 * r + 8, :], bc(tokm.unsqueeze(2), [P, 8, NBLK]), ALU.mult)
            dve.tensor_tensor(bval[:, :, :, 1], blk1h, bc(dst.unsqueeze(2), [P, 16, NBLK]), ALU.mult)
            dve.tensor_tensor(bval[:, :, :, 2], blk1h, bc(gate.rearrange("p r t -> p (r t)").unsqueeze(2), [P, 16, NBLK]), ALU.mult)\
               .then_inc(tab_ok, 1)
            ovx = ovt[:, 0:16]
            ovc = MP.rearrange("p r n -> p (r n)").rearrange("p (b n) -> p b n", b=NOVER)
            ovn, ovs_ = ovt[:, 16:24], ovt[:, 24:25]
            evens = iotaf[:, 0:NOVER].rearrange("p (b two) -> p b two", two=2)[:, :, 0:1]
            dve.tensor_tensor(ovn.unsqueeze(2), bc(ovend[:, 31:32].unsqueeze(1), [P, NOVER // 2, 1]), evens, ALU.is_gt)
            link(dve.tensor_tensor(ovc, bc(ovend.unsqueeze(1), [P, NOVER, 32]), bc(iotaf[:, 0:NOVER].unsqueeze(2), [P, NOVER, 32]), ALU.is_le))
            link(dve.tensor_reduce(ovx[:, 0:NOVER], ovc, AX.X, ALU.add))
            link(dve.tensor_scalar(nov_i[:, 0:NOVER], ovx[:, 0:NOVER], float(EXPERTS - 1), None, ALU.min))
            link(dve.tensor_reduce(ovs_, ovn, AX.X, ALU.add))
            link(dve.tensor_scalar(nov_i[:, NOVER:NOVER + 1], ovs_, 2.0, None, ALU.mult))
            dve.wait_ge(tab_ps, 1)
            tab = bank(2)[:, 0:3 * NBLK].rearrange("p (n v) -> p v n", v=3)
            dve.tensor_scalar(tabi[:, :, :], tab[:, 0:2, :], OOB, None, ALU.add)
            dve.tensor_copy(tabg[:, :], tab[:, 2, :]).then_inc(idx_ok, 1)

            def xT_evac(v):
                dve.wait_ge(ex_xT, v)
                for b in range(2):
                    ins = dve.tensor_tensor(xgT[:, 4 * b:4 * b + 4, :], bank(b).rearrange("p (k n) -> p k n", k=4),
                                            bc(g2e[:, 4 * b:4 * b + 4].unsqueeze(2), [P, 4, P]), ALU.mult)
                ins.then_inc(ex_xTe, 1)

            def act_mul(v):
                dve.wait_ge(ex_u, v)
                dve.wait_ge(ex_s, v)
                dve.tensor_tensor(actb, bank(3), actb, ALU.mult).then_inc(ex_a, 1)

            def y_half(s, b, down, scat, done):
                g = tabg[:, b:b + 1] if isinstance(b, int) else tabg[:, bass.ds(b, 1)]
                dve.wait_ge(ex_y, down)
                if scat is not None:
                    dve.wait_ge(scat_out[s], scat)
                dve.tensor_scalar(yb[s][:, 512:1024], bank(6), g, None, ALU.mult).then_inc(done, 1)

            def step(j, s):
                first = isinstance(j, int) and j == 0 and s == 0
                b, prev, b1, b2 = j * 2 + s, j * 2 + s - 1, j * 2 + s + 1, j * 2 + s + 2
                scat = (j - 1 + s) * 16
                if not isinstance(b, int):
                    b, prev, b1, b2, scat = [dve.snap(v) for v in (b, prev, b1, b2, scat)]
                act_mul(b1)
                xT_evac(b2)
                if not first:
                    y_half(1 - s, prev, b, None if isinstance(scat, int) and scat == 0 else scat, ex_y1)

            dve.wait_ge(xg_z, 2)
            xT_evac(1)
            for j in range(2):
                for s in range(2):
                    step(j, s)
            with dve.Fori(2, EXPERTS // 2) as j:
                for s in range(2):
                    step(j, s)
            nov = dve.value_load(nov_i[0:1, NOVER:NOVER + 1], min_val=0, max_val=NOVER)
            for b in range(0, NOVER, 2):
                with dve.If(nov > b):
                    for s in range(2):
                        step((EXPERTS + b) // 2, s)
            blocks, last = dve.snap(nov + EXPERTS), dve.snap(nov + (EXPERTS - 1))
            scat = dve.snap(nov * 8 + 16 * (EXPERTS // 2 - 1))
            y_half(1, last, blocks, scat, tail_y)
            for i in range(NT + 1):
                if i < NT:
                    x3 = banks(2 * (i % 3), 2)
                    dve.wait_ge(ya_ps, i + 1)
                    dve.tensor_tensor(x3, x3, y2t[:, i % 4, 1, :], ALU.add).then_inc(fin_c, 1)
                    dve.wait_ge(fin_c, i + 1)
                    dve.tensor_tensor(x3, x3, x2[:, i, :], ALU.add).then_inc(x3_ok, 1)
                if i >= 1:
                    if i == 1:
                        dve.wait_ge(fg_in, 16)
                    dve.wait_ge(ms3_ok, i)
                    dve.tensor_scalar(ms3v[:, i - 1:i], ms3[:, i - 1:i], 1.0 / D, RMS_EPS, ALU.mult, ALU.add).then_inc(ms3v_ok, 1)
                    dve.wait_ge(rstd3_ok, i)
                    dve.scalar_tensor_tensor(x2[:, i - 1, :], banks(2 * ((i - 1) % 3), 2), rstd3[:, i - 1:i], fgb,
                                             ALU.mult, ALU.mult).then_inc(fin_ok, 1)


_INS = ["x", "rel_bias", "ln1_g", "w_in", "lam_q1", "lam_k1", "lam_q2", "lam_k2", "subln_g", "conv_w", "conv_b",
        "conv_ln_g", "conv_ln_b", "ssm_lam_re", "ssm_lam_im", "ssm_log_dt", "ssm_b_re", "ssm_b_im", "ssm_c_re",
        "ssm_c_im", "ssm_d", "ssm_glu_w", "ssm_glu_b", "w_out", "ln2_g", "group_router_w", "group_router_b",
        "expert_router_w", "expert_router_b", "w_gate", "w_up", "w_down", "final_g"]


def bucket_onehot():
    rel = 255 - np.arange(384)
    n = np.maximum(rel, 0)
    exact = BUCKETS // 2
    nf = np.maximum(n, 1).astype(np.float32)
    large = exact + (np.log(nf / np.float32(exact)) / np.float32(math.log(128 / exact))
                     * np.float32(BUCKETS - exact)).astype(np.int32)
    bucket = np.where(n < exact, n, np.minimum(large, BUCKETS - 1))
    return ((bucket[None, :] == np.arange(BUCKETS)[:, None]) & (rel >= 0)[None, :]).astype(np.float32)


def kernel(**inputs):
    import concourse.bacc as bacc
    from concourse.bass_utils import run_bass_kernel_spmd

    nc = bacc.Bacc("TRN2", target_bir_lowering=False, num_devices=1)
    arrays, t = {}, {}
    for name in _INS:
        arrays[f"in_{name}"] = np.ascontiguousarray(inputs[name])
    arrays["in_bucket_onehot"] = bucket_onehot()
    for key, a in arrays.items():
        t[key[3:]] = nc.dram_tensor(key, a.shape, mybir.dt.from_np(a.dtype), kind="ExternalInput").ap()
    t["out"] = nc.dram_tensor("out", (1, L, D), F32, kind="ExternalOutput").ap()
    build(nc, t)
    r = run_bass_kernel_spmd(nc, [arrays], core_ids=[0])
    return r.results[0]["out"]
```

```python
import math
from contextlib import ExitStack

import numpy as np

import concourse.bass as bass
import concourse.mybir as mybir
from concourse.mybir import ActivationFunctionType as ACT
from concourse.mybir import AluOpType as ALU
from concourse.mybir import AxisListType as AX

F32 = mybir.dt.float32
BF16 = mybir.dt.bfloat16
F32R = mybir.dt.float32r
I32 = mybir.dt.int32
U32 = mybir.dt.uint32

P = 128
D = 1024
L = 1024
KD = D // P
NT = L // P
HEADS, DK, DV = 4, 64, 128
CH = 256
TAPS = 31
GROUPS, GCH, STATES = 16, 16, 64
PAIRS = GROUPS // 2
CHUNK = 8
NC = L // CHUNK
SCAN_STEPS = int(math.log2(NC))
WCH = 256
BUCKETS = 32
EXPERTS, EGROUPS, EPG, FF = 32, 4, 8, 512
FK = FF // P
NOVER = 2 * L // P
NB = EXPERTS + NOVER
NBLK = NB + 2
OOB = float(1 << 20)
RMS_EPS, LN_EPS = 1e-6, 1e-5
SCALE = DK ** -0.5
LAM_INIT = 0.8 - 0.6 * math.exp(0.0)
NEG = -1e30
TWO_PI = (6.28125, 0.0019350051879882812, 3.019915981956753e-07)
ROUND = 12582912.0
PI = 3.1415925

CHUNKS = [(1024, "v"), (2048, "ssm"), (1280, "v"), (1792, "gate"), (1536, "a"),
          (0, "qk"), (256, "qk"), (512, "qk"), (768, "qk")]


def units():
    out = []
    for c, (_, kind) in enumerate(CHUNKS):
        if kind in ("ssm", "v"):
            out += [(c, kind, i) for i in range(NT)]
        else:
            out += [(c, kind, i) for i in range(4)]
    return out


UNITS = units()
LAST_UNIT = {c: max(n for n, u in enumerate(UNITS) if u[0] == c) for c in range(len(CHUNKS))}

MISC_AT = {}
for _n, _job in enumerate([("conv_to_tok", i) for i in range(4)] + [("ssm_to_ch", i) for i in range(4)]
                          + [("conv_to_ch", i) for i in range(4)] + [("head", 0), ("head", 1)]
                          + [("glu", i) for i in range(4)]):
    MISC_AT.setdefault(_n, []).append(_job)
for _n, _job in ((20, 2), (21, 3), (28, 4), (29, 5)):
    MISC_AT.setdefault(_n, []).append(("head", _job))
ITEMS = [(h, i) for h in range(HEADS) for i in reversed(range(NT))]
NI = len(ITEMS)
ITERS = NI + 2
MISC_AT[ITERS + 1] = [("head", 6), ("head", 7)]
MISC_ORDER = [j for n in sorted(MISC_AT) for j in MISC_AT[n]]


def build(nc, t):
    with ExitStack() as ctx:
        def sb(name, shape, dt=F32):
            return ctx.enter_context(nc.sbuf_tensor(name, shape, dt))

        def sem(name):
            return ctx.enter_context(nc.semaphore(name))

        x2_dram = nc.dram_tensor("x2_rows", [L, D], F32, kind="Internal").ap()
        band_rows = nc.dram_tensor("band_rows", [HEADS, P, 384], F32, kind="Internal").ap()
        toep_rows = nc.dram_tensor("toep_rows", [GROUPS, GCH, 2 * P], F32, kind="Internal").ap()
        h2_dram = nc.dram_tensor("h2_rows", [L, D], F32, kind="Internal").ap()
        y2_dram = nc.dram_tensor("y2_rows", [2 * L, D], F32, kind="Internal").ap()

        with nc.sbuf_tensor("RD", [P, 8192], F32) as RD, nc.sbuf_tensor("RF", [P, 8192], F32) as RF, \
                nc.sbuf_tensor("RG", [P, 8192], F32) as RG, nc.sbuf_tensor("band", [P, HEADS, 256], F32) as band, \
                nc.sbuf_tensor("xr", [P, 1024], F32) as xr:
            pass
        RD_head = sb("RD_head", [P, 4608])
        act_parts = sb("act_parts", [P, 1024], F32R)
        RD_tail = sb("RD_tail", [P, 2560])
        wd_parts = sb("wd_parts", [P, 8192], F32R)
        wg_parts = sb("wg_parts", [P, 8192], F32R)
        xT_lo = sb("xT_lo", [P, 1024], F32R)
        xT_hi = sb("xT_hi", [P, 1024], F32R)
        RAB = sb("RAB", [P, 16384])
        RA = RAB[:, 0:8192]
        RB = RAB[:, 8192:16384]
        RCE = sb("RCE", [P, 8192])
        RE = RCE[:, 0:4096]
        RC = RCE[:, 4096:8192]

        hT = RA[:, :].rearrange("p (k n) -> p k n", k=KD)
        xt = RB[:, :].rearrange("p (t n) -> p t n", t=NT)
        qkT = RB[:, :].rearrange("p (c n) -> p c n", c=8)
        vtok = RC[:, :].rearrange("p (t n) -> p t n", t=NT)
        mixT = RD[:, :].rearrange("p (k n) -> p k n", k=KD)
        win = RF[:, 0:6144].rearrange("p (s k n) -> p s k n", s=3, k=KD)
        wout = RF[:, :].rearrange("p (k n) -> p k n", k=KD)
        x2 = RG[:, :].rearrange("p (t n) -> p t n", t=NT)

        convh = RF[:, 6144:8192].rearrange("p (c n) -> p c n", c=2)
        convt = RF[:, 6144:8192].rearrange("p (t n) -> p t n", t=NT)
        convo = RD[:, 4096:6144].rearrange("p (c n) -> p c n", c=2)

        uc = RG[:, 0:2048].rearrange("p (g i h) -> p g i h", g=GROUPS, i=CHUNK)
        UT = RG[:, 2048:4096].rearrange("p (g c) -> p g c", g=GROUPS)
        XR = RG[:, 4096:5120].rearrange("p (a c) -> p a c", a=PAIRS)
        XI = RG[:, 5120:6144].rearrange("p (a c) -> p a c", a=PAIRS)
        yc = RG[:, 6144:8192].rearrange("p (j n) -> p j n", j=CHUNK)
        gT = RG[:, 4096:6144].rearrange("p (c n) -> p c n", c=2)
        glut = RG[:, 2048:4096].rearrange("p (c n) -> p c n", c=2)
        st = [RG[:, 6144:7168], RG[:, 7168:8192], RD[:, 6144:7168], RD[:, 7168:8192]]
        st = [s.rearrange("p (a c) -> p a c", a=PAIRS) for s in st]
        WinR = RE[:, 0:1024].rearrange("p (a s) -> p a s", a=PAIRS)
        WinI = RE[:, 1024:2048].rearrange("p (a s) -> p a s", a=PAIRS)
        TG = RE[:, 2048:4096].rearrange("p (g n) -> p g n", g=GROUPS)
        CAR = RD[:, 0:1152].rearrange("p (a t h) -> p a t h", a=PAIRS, t=9)
        CAI = RD[:, 1152:2304].rearrange("p (a t h) -> p a t h", a=PAIRS, t=9)
        VBR = RD[:, 6144:7168].rearrange("p (a i h) -> p a i h", a=PAIRS, i=CHUNK)
        VBI = RD[:, 7168:8192].rearrange("p (a i h) -> p a i h", a=PAIRS, i=CHUNK)
        s0 = 2304
        def scratch(n):
            nonlocal s0
            s0 += n
            assert s0 <= 4096
            return RD[:, s0 - n:s0]
        bre = scratch(128).rearrange("p (a h) -> p a h", a=PAIRS)
        bim = scratch(128).rearrange("p (a h) -> p a h", a=PAIRS)
        crow = scratch(256).rearrange("p (r s) -> p r s", r=2)
        BBR = scratch(128).rearrange("p (a h) -> p a h", a=PAIRS)
        BBI = scratch(128).rearrange("p (a h) -> p a h", a=PAIRS)
        PWR = scratch(72).rearrange("p (t a) -> p t a", a=PAIRS)
        PWI = scratch(72).rearrange("p (t a) -> p t a", a=PAIRS)
        RVR = scratch(64).rearrange("p (t a) -> p t a", a=PAIRS)
        RVI = scratch(64).rearrange("p (t a) -> p t a", a=PAIRS)
        sv = scratch(8 * 24).rearrange("p (n a) -> p n a", a=PAIRS)
        lrow = scratch(128)
        ctmp = scratch(256)
        lamv = RG[:, 6144:6400].rearrange("p (v n) -> p v n", v=4)
        onehot = RG[0:BUCKETS, 6400:6784]
        brow = RG[0:HEADS, 6784:7168]
        ksb = RG[:, 7168:8192].rearrange("p (q n) -> p q n", q=4)
        TMP4 = [RF[:, 6144:7168], RF[:, 7168:8192], RE[:, 2048:3072], RE[:, 3072:4096]]
        silu = RG[:, 0:2048].rearrange("p (i n) -> p i n", i=4)

        pexp = RE[:, :].rearrange("p (s n) -> p s n", s=4)
        xg = [RD[:, 0:1024], RD[:, 1024:2048]]
        xgT = RD[:, 2048:3072].rearrange("p (k n) -> p k n", k=KD)
        actb = RD[:, 4096:4608]
        actT_lo, actT_hi = act_parts[:, 0:512], act_parts[:, 512:1024]
        actT_last = RD[:, 6144 - 1024:6144 - 512]
        wg_hi, wg_lo = wg_parts[:, 0:4096], wg_parts[:, 4096:8192]
        wd_hi, wd_lo = wd_parts[:, 0:4096], wd_parts[:, 4096:8192]
        yb = [RD[:, 6144:7168], RD[:, 7168:8192]]
        wgate = [RA[:, 0:4096].rearrange("p (k n) -> p k n", k=KD), RB[:, 0:4096].rearrange("p (k n) -> p k n", k=KD)]
        wup = [RA[:, 4096:8192].rearrange("p (k n) -> p k n", k=KD), RB[:, 4096:8192].rearrange("p (k n) -> p k n", k=KD)]
        wdown = [RE[:, :].rearrange("p (k n) -> p k n", k=FK), RC[:, :].rearrange("p (k n) -> p k n", k=FK)]
        r0 = 0
        def route(n):
            nonlocal r0
            r0 += n
            assert r0 <= 8192
            return RD[:, r0 - n:r0]
        slot1h = route(2048).rearrange("p (r n) -> p r n", r=16)
        blk1h = route(16 * NBLK).rearrange("p (r n) -> p r n", r=16)
        bval = route(48 * NBLK).rearrange("p (r n v) -> p r n v", r=16, v=3)
        before0 = r0
        MM = route(512).rearrange("p (r n) -> p r n", r=16)
        MP = route(512).rearrange("p (r n) -> p r n", r=16)
        RK = route(256).rearrange("p (t n) -> p t n", t=NT)
        esel = route(256)
        rr = route(704)
        RR, _o = {}, 0
        for _name, _n in (("g8", 64), ("mx8", 64), ("e8", 64), ("me8", 64), ("gi8", 64), ("ei8", 64), ("gix", 8), ("goh", 32),
                          ("gsum", 8), ("den", 8), ("gexp", 32), ("gdif", 32), ("edif", 8), ("eexp", 8),
                          ("gate", 16), ("idx", 16), ("rk", 16), ("br_", 16), ("ovs", 16), ("blk", 16), ("dst", 16), ("tokm", 8)):
            RR[_name] = rr[:, _o:_o + _n]
            _o += _n
        assert _o <= 704

        def rrv(name, n=None):
            return RR[name]
        mbf = route(128).bitcast(BF16).rearrange("p (t n) -> p t n", t=NT)
        ovt = route(512)

        ident = sb("ident", [P, P])
        tri = sb("tri", [P, P], BF16)
        onesb = sb("onesb", [P, P], BF16)
        h2T = band[:, :, :].rearrange("p h n -> p (h n)").rearrange("p (k n) -> p k n", k=KD)
        pT = [xr[:, :].rearrange("p (k n) -> p k n", k=KD), RF[:, 5120:6144].rearrange("p (k n) -> p k n", k=KD)]
        g1 = sb("g1", [P, KD])
        g2k = sb("g2k", [P, KD])
        g2e = sb("g2e", [P, KD])
        rw = sb("rw", [P, KD, 36])
        rbias = sb("rbias", [P, 36])
        gluw = sb("gluw", [P, 2, CH])
        dbc = rw[:, :, :].rearrange("p k n -> p (k n)")[:, 0:CH]
        convw = sb("convw", [P, 2, TAPS])
        convb = sb("convb", [P, 2])
        lng = sb("lng", [P, 2])
        lnb = sb("lnb", [P, 2])
        glub = sb("glub", [P, 2])
        sg = sb("sg", [P, 1])
        b31 = sb("b31", [P, HEADS])
        relt = sb("relt", [BUCKETS, HEADS])
        nb31 = sb("nb31", [P, HEADS])
        lam = sb("lam", [P, 4])
        PDR = sb("PDR", [P, SCAN_STEPS, PAIRS])
        PDI = sb("PDI", [P, SCAN_STEPS, PAIRS])
        mhalf = sb("mhalf", [P, NT])
        ms = sb("ms", [P, NT])
        msv = sb("msv", [P, NT])
        rstd = sb("rstd", [P, NT])
        ms2 = sb("ms2", [P, NT])
        ms2v = sb("ms2v", [P, NT])
        rstd2 = sb("rstd2", [P, NT])
        ms3 = sb("ms3", [P, NT])
        ms3v = sb("ms3v", [P, NT])
        rstd3 = sb("rstd3", [P, NT])
        hss = sb("hss", [P, HEADS, NT])
        hssv = sb("hssv", [P, HEADS, NT])
        hrstd = sb("hrstd", [P, HEADS, NT])
        lnst = sb("lnst", [P, NT, 6])
        lnmv = sb("lnmv", [P, NT, 2])
        lnv = sb("lnv", [P, NT])
        lnr = sb("lnr", [P, NT])
        smx = sb("smx", [P, 2, 2, 8])
        logit = gluw[:, :, :].rearrange("p k n -> p (k n)")[:, 0:NT * 36].rearrange("p (t n) -> p t n", t=NT)
        iotai = RG[:, 0:128].bitcast(I32)
        iotaf = sb("iotaf", [P, P])
        thr = sb("thr", [P, 7])
        toki = RG[:, 128:136].bitcast(I32)
        tokf = sb("tokf", [P, NT])
        tabi = sb("tabi", [P, 2, NBLK], U32)
        tabg = sb("tabg", [P, NBLK])
        cur = sb("cur", [P, 1], U32)
        pdump = sb("pdump", [P, 4])
        nov_i = sb("nov_i", [P, 1], I32)
        ends = RD[:, 5632:5632 + EXPERTS].bitcast(I32)
        blkx = RD[:, 5760:5760 + 3 * (NB + 1)].bitcast(I32).rearrange("p (v n) -> p v n", v=3)

        psum = ctx.enter_context(nc.psum_tensor("psum", [P, 8, 512], F32))
        def bank(i):
            return psum[:, i, :]
        def banks(i, n):
            return psum[:, i:i + n, :].rearrange("p b n -> p (b n)")

        x_in = [sem(f"x_in{i}") for i in range(NT)]
        win_in = [sem(f"win_in{i}") for i in range(3)]
        par_in = sem("par_in")
        set_in = sem("set_in")
        const_ok = sem("const_ok")
        act_c = sem("act_c")
        dve_c = sem("dve_c")
        pool_c = sem("pool_c")
        ms_ok = sem("ms_ok")
        msv_ok = sem("msv_ok")
        rstd_ok = sem("rstd_ok")
        xn_ok = sem("xn_ok")
        g1_in = sem("g1_in")
        xT_ps = sem("xT_ps")
        hT_ok = sem("hT_ok")
        unit_ps = sem("unit_ps")
        unit_ev = sem("unit_ev")
        band_ps = sem("band_ps")
        band_row = sem("band_row")
        band_dram = sem("band_dram")
        band_in = sem("band_in")
        band_ok = sem("band_ok")
        lam_dot = sem("lam_dot")
        lam_exp = sem("lam_exp")
        lam_ok = sem("lam_ok")
        lrow_ps = sem("lrow_ps")
        ssm_dt = sem("ssm_dt")
        ssm_ang = sem("ssm_ang")
        ssm_sin = sem("ssm_sin")
        vb_ok = sem("vb_ok")
        ca_ok = sem("ca_ok")
        uT_ps = sem("uT_ps")
        uT_ev = sem("uT_ev")
        wi_ps = sem("wi_ps")
        wi_ev = sem("wi_ev")
        k_ps = sem("k_ps")
        k_ev = sem("k_ev")
        kz_ok = sem("kz_ok")
        toep_dram = sem("toep_dram")
        toep_in = sem("toep_in")
        vin_ps = sem("vin_ps")
        vin_ev = sem("vin_ev")
        scan_ok = sem("scan_ok")
        ud_ok = sem("ud_ok")
        y_ps = sem("y_ps")
        y_ev = sem("y_ev")
        gelu_ok = sem("gelu_ok")
        glu_half = sem("glu_half")
        ssm_ok = sem("ssm_ok")
        h_ok = sem("h_ok")
        tap_c = sem("tap_c")
        conv_ps = sem("conv_ps")
        conv_ev = sem("conv_ev")
        ln_var = sem("ln_var")
        ln_rstd = sem("ln_rstd")
        ln_ok = sem("ln_ok")
        silu_t = sem("silu_t")
        conv_ok = sem("conv_ok")
        s_ps = sem("s_ps")
        nm_ok = sem("nm_ok")
        e_ok = sem("e_ok")
        p_ok = sem("p_ok")
        pT_ps = sem("pT_ps")
        pT_ev = sem("pT_ev")
        o_ps = sem("o_ps")
        o_ev = sem("o_ev")
        misc_ps = sem("misc_ps")
        misc_ev = sem("misc_ev")
        head_ss = sem("head_ss")
        head_var = sem("head_var")
        head_rstd = sem("head_rstd")
        head_o = sem("head_o")
        rw_in = sem("rw_in")
        wout_in = [sem(f"wout_in{i}") for i in range(3)]
        xr_in = sem("xr_in")
        proj_ps = sem("proj_ps")
        x2_ok = sem("x2_ok")
        ms2_ok = sem("ms2_ok")
        ms2v_ok = sem("ms2v_ok")
        rstd2_ok = sem("rstd2_ok")
        h2_ok = sem("h2_ok")
        h2_out = sem("h2_out")
        h2T_ps = sem("h2T_ps")
        h2T_ok = sem("h2T_ok")
        lg_ps = sem("lg_ps")
        lg_ok = sem("lg_ok")
        gd_ok = sem("gd_ok")
        ge_ok = sem("ge_ok")
        mm_ok = sem("mm_ok")
        rank_ps = sem("rank_ps")
        tab_ok = sem("tab_ok")
        tab_ps = sem("tab_ps")
        idx_ok = sem("idx_ok")
        wgu_in = [sem(f"wgu_in{i}") for i in range(2)]
        wd_in = [sem(f"wd_in{i}") for i in range(2)]
        gather_in = [sem(f"gather_in{i}") for i in range(2)]
        cur_c = sem("cur_c")
        ex_xT = sem("ex_xT")
        ex_xTe = sem("ex_xTe")
        ex_g = sem("ex_g")
        ex_u = sem("ex_u")
        ex_s = sem("ex_s")
        ex_a = sem("ex_a")
        ex_aT = sem("ex_aT")
        ex_aTe = sem("ex_aTe")
        ex_y = sem("ex_y")
        ex_y0 = sem("ex_y0")
        ex_y1 = sem("ex_y1")
        ex_wh = sem("ex_wh")
        ex_wl = sem("ex_wl")
        ex_aTl = sem("ex_aTl")
        ex_gh = sem("ex_gh")
        ex_gl = sem("ex_gl")
        ex_xh = sem("ex_xh")
        ex_xl = sem("ex_xl")
        x2_out = sem("x2_out")
        x2_back = sem("x2_back")
        tail_y = sem("tail_y")
        scat_out = [sem(f"scat_out{i}") for i in range(2)]
        moe_done = sem("moe_done")
        fg_in = sem("fg_in")
        y2_in = [sem(f"y2_in{i}") for i in range(4)]
        ya_ps = sem("ya_ps")
        x3_ok = sem("x3_ok")
        ms3_ok = sem("ms3_ok")
        ms3v_ok = sem("ms3v_ok")
        rstd3_ok = sem("rstd3_ok")
        fin_ok = sem("fin_ok")
        fin_c = sem("fin_c")
        fin_out = sem("fin_out")

        fgb = band[:, :, :].rearrange("p h n -> p (h n)")
        y2t = RF[:, :].rearrange("p (s r n) -> p s r n", s=4, r=2)

        def bc(ap, shape):
            return ap.to_broadcast(shape)

        def vec(name, **kw):
            return t[name].rearrange("o (k p) -> (o p) k", **kw)

        par_loads = [
            (relt[:, :], t["rel_bias"]),
            (onehot, t["bucket_onehot"]),
            (lrow[0:8, :], t["ssm_lam_re"][0].rearrange("(a q) s -> a (q s)", q=2)),
            (lrow[8:16, :], t["ssm_lam_im"][0].rearrange("(a q) s -> a (q s)", q=2)),
            (sv[0:64, 0, :], t["ssm_log_dt"].rearrange("o (a q) -> q (o a)", q=2)[0:1, :].to_broadcast([64, PAIRS])),
            (sv[64:128, 0, :], t["ssm_log_dt"].rearrange("o (a q) -> q (o a)", q=2)[1:2, :].to_broadcast([64, PAIRS])),
            (bre, t["ssm_b_re"][0].rearrange("(a q) s h -> (q s) a h", q=2)),
            (bim, t["ssm_b_im"][0].rearrange("(a q) s h -> (q s) a h", q=2)),
        ]
        for r, name in enumerate(("ssm_c_re", "ssm_c_im")):
            for a in range(PAIRS):
                par_loads.append((crow[GCH * a:GCH * (a + 1), r, :].rearrange("h (q s) -> h q s", q=2),
                                  t[name][0, 2 * a:2 * a + 2].rearrange("q h s -> h q s")))
        for v, name in enumerate(("lam_q1", "lam_k1", "lam_q2", "lam_k2")):
            par_loads.append((lamv[:, v, :], t[name].to_broadcast([P, DK])))
        set_loads = [
            (b31[:, :], t["rel_bias"][BUCKETS - 1:BUCKETS, :].to_broadcast([P, HEADS])),
            (dbc[:, :], t["ssm_d"].to_broadcast([P, CH])),
            (convb[:, :], vec("conv_b", p=P)),
            (lng[:, :], vec("conv_ln_g", p=P)),
            (lnb[:, :], vec("conv_ln_b", p=P)),
            (glub[:, :], vec("ssm_glu_b", p=P)),
            (sg[:, :], vec("subln_g", p=P)),
            (gluw[:, :, :], t["ssm_glu_w"][0].rearrange("(k p) n -> p k n", p=P)),
            (g2k[:, :], vec("ln2_g", p=P)),
            (g2e[:, :], t["ln2_g"].rearrange("o (p k) -> (o p) k", p=P)),
            (rbias[:, 0:4], t["group_router_b"].to_broadcast([P, EGROUPS])),
            (rbias[:, 4:36], t["expert_router_b"].to_broadcast([P, EXPERTS])),
        ]
        for c in range(2):
            set_loads.append((convw[:, c, :], t["conv_w"][0].rearrange("j (c p) -> p c j", p=P)[:, c, :]))
        SET_N = len(set_loads)
        PAR_N = len(par_loads)

        block = ctx.enter_context(nc.Block())

        @block.sync
        def _(sp):
            def load_chunk(c):
                src = t["w_in"][0, :, CHUNKS[c][0]:CHUNKS[c][0] + WCH].rearrange("(k p) n -> p k n", p=P)
                if c >= 3:
                    sp.wait_ge(unit_ps, LAST_UNIT[c - 3] + 1)
                sp.dma_start(win[:, c % 3], src).then_inc(win_in[c % 3], 16)

            for i in range(NT):
                sp.dma_start(xt[:, i, :], t["x"][0, i * P:(i + 1) * P, :]).then_inc(x_in[i], 16)
                if i in (1, 3, 5):
                    load_chunk(i // 2)
            sp.wait_ge(band_row, 1)
            sp.dma_start(band_rows, bc(brow[:, :].unsqueeze(1), [HEADS, P, 384])).then_inc(band_dram, 16)
            sp.wait_ge(band_dram, 16)
            sp.dma_start(band[:, :, :], bass.AP(tensor=band_rows.tensor, offset=P - 1,
                                                ap=[[383, P], [384 * P, HEADS], [1, 256]])).then_inc(band_in, 16)
            sp.wait_ge(k_ev, 1)
            sp.wait_ge(kz_ok, 1)
            for r in range(4):
                sp.dma_start(toep_rows.rearrange("(q r) h n -> r h q n", r=4)[r], ksb[32 * r:32 * r + GCH])\
                  .then_inc(toep_dram, 16)
            sp.wait_ge(toep_dram, 64)
            for i in range(CHUNK):
                src = bass.AP(tensor=toep_rows.tensor, offset=P - GCH * i,
                              ap=[[2 * P, GCH], [2 * P * GCH, GROUPS], [1, P]])
                sp.dma_start(TG[GCH * i:GCH * (i + 1)], src).then_inc(toep_in, 16)
            for c in range(3, len(CHUNKS)):
                load_chunk(c)
            sp.wait_ge(unit_ps, len(UNITS))
            wo = t["w_out"][0].rearrange("(k p) n -> p k n", p=P)
            sp.dma_start(wout[:, 0:5], wo[:, 0:5]).then_inc(wout_in[0], 16)

            def load_gu(s, e):
                sp.dma_start(wgate[s], t["w_gate"][0, e].rearrange("(p k) n -> p k n", p=P)).then_inc(wgu_in[s], 16)
                sp.dma_start(wup[s], t["w_up"][0, e].rearrange("(p k) n -> p k n", p=P)).then_inc(wgu_in[s], 16)

            def load_d(s, e):
                sp.dma_start(wdown[s], t["w_down"][0, e].rearrange("(p k) n -> p k n", p=P)).then_inc(wd_in[s], 16)

            load_gu(0, 0)
            sp.wait_ge(conv_ok, 4)
            sp.wait_ge(silu_t, 4)
            sp.dma_start(wout[:, 6:8], wo[:, 6:8]).then_inc(wout_in[2], 16)
            sp.wait_ge(o_ps, NI)
            sp.dma_start(wout[:, 5:6], wo[:, 5:6]).then_inc(wout_in[1], 16)
            load_d(0, 0)
            load_gu(1, 1)
            load_d(1, 1)
            for i in range(NT):
                sp.wait_ge(x2_ok, i + 1)
                sp.dma_start(x2_dram[i * P:(i + 1) * P, :], x2[:, i, :]).then_inc(x2_out, 16)
            wg = t["w_gate"][0].rearrange("e (p k) n -> e p k n", p=P)
            wu = t["w_up"][0].rearrange("e (p k) n -> e p k n", p=P)
            wd = t["w_down"][0].rearrange("e (p k) n -> e p k n", p=P)

            def reload_gu(s, e, left):
                gone = sp.snap(left * 4)
                sp.wait_ge(ex_u, left)
                sp.dma_start(wup[s], wu[bass.ds(e, 1)].rearrange("e p k n -> (e p) k n")).then_inc(wgu_in[s], 16)
                sp.wait_ge(ex_gl, gone)
                sp.dma_start(wgate[s], wg[bass.ds(e, 1)].rearrange("e p k n -> (e p) k n")).then_inc(wgu_in[s], 16)

            def reload_d(s, e, left):
                sp.wait_ge(ex_wl, left * FK)
                sp.dma_start(wdown[s], wd[bass.ds(e, 1)].rearrange("e p k n -> (e p) k n")).then_inc(wd_in[s], 16)

            def blocks_to(e):
                at = slice(e, e + 1) if isinstance(e, int) else bass.ds(e, 1)
                return sp.value_load(ends[0:1, at], min_val=1, max_val=EXPERTS + NOVER)

            sp.wait_ge(idx_ok, 1)
            reload_gu(0, 2, blocks_to(0))
            with sp.Fori(1, EXPERTS // 2 - 1) as j:
                for s in range(2):
                    e, nxt = sp.snap(j * 2 + s), sp.snap(j * 2 + s + 1)
                    left, nxt_left = blocks_to(sp.snap(j * 2 + s - 2)), blocks_to(sp.snap(j * 2 + s - 1))
                    reload_gu(1 - s, nxt, nxt_left)
                    reload_d(s, e, sp.snap(left))
            left, nxt_left = blocks_to(EXPERTS - 4), blocks_to(EXPERTS - 3)
            reload_gu(1, EXPERTS - 1, nxt_left)
            reload_d(0, EXPERTS - 2, left)
            reload_d(1, EXPERTS - 1, nxt_left)
            nov = sp.value_load(nov_i[0:1, 0:1], min_val=0, max_val=NOVER)
            sp.wait_ge(ex_gl, sp.snap(nov * 4 + 4 * (EXPERTS + 1)))
            sp.dma_start(x2[:, :, :], x2_dram.rearrange("(i p) d -> p i d", p=P)).then_inc(x2_back, 16)
            sp.wait_ge(moe_done, 4)
            y2 = y2_dram.rearrange("(n r) d -> n (r d)", r=2)
            for i in range(NT):
                if i >= 4:
                    sp.wait_ge(x3_ok, i - 3)
                sp.dma_start(y2t[:, i % 4], y2[i * P:(i + 1) * P, :].rearrange("p (r d) -> p r d", r=2)).then_inc(y2_in[i % 4], 16)

        @block.gpsimd
        def _(pool):
            n = [0]
            def link(ins):
                n[0] += 1
                ins.then_inc(pool_c, 1)
                pool.wait_ge(pool_c, n[0])

            link(pool.memset(ident[:, :], 0.0))
            pool.affine_select(out=ident[:, :], in_=ident[:, :], compare_op=ALU.not_equal, fill=1.0, base=0,
                               pattern=[[-1, P]], channel_multiplier=1).then_inc(const_ok, 1)
            pool.memset(mhalf[:, :], -0.5).then_inc(const_ok, 1)
            for r in range(4):
                pool.wait_ge(msv_ok, r + 1)
                if r == 0:
                    pool.wait_ge(const_ok, 2)
                pool.tensor_tensor(rstd[:, 2 * r:2 * r + 2], msv[:, 2 * r:2 * r + 2], mhalf[:, 0:2], ALU.pow)\
                    .then_inc(rstd_ok, 1)
            pool.memset(ksb[:, :, 0:P], 0.0).then_inc(kz_ok, 1)
            link(pool.memset(onesb[:, :], 1.0))
            link(pool.memset(tri[:, :], 1.0))
            pool.affine_select(out=tri[:, :], in_=tri[:, :], compare_op=ALU.is_gt, fill=0.0, base=0,
                               pattern=[[1, P]], channel_multiplier=-1).then_inc(const_ok, 1)
            link(pool.iota(iotai[:, :], pattern=[[1, P]], base=0, channel_multiplier=0))
            link(pool.iota(toki[:, :], pattern=[[P, NT]], base=0, channel_multiplier=1))
            link(pool.tensor_copy(iotaf[:, :], iotai[:, :]))
            link(pool.tensor_copy(tokf[:, :], toki[:, :]))
            pool.tensor_scalar(thr[:, :], iotaf[:, 1:8], float(P), None, ALU.mult).then_inc(const_ok, 1)
            pool.wait_ge(band_in, 16)
            for h in range(HEADS):
                pool.affine_select(out=band[:, h, :], in_=band[:, h, :], compare_op=ALU.is_ge, fill=NEG / SCALE,
                                   base=P, pattern=[[-1, 256]], channel_multiplier=1).then_inc(band_ok, 1)
            pool.wait_ge(set_in, SET_N * 16)
            pool.wait_ge(uT_ps, 4)
            pool.tensor_tensor(uc, uc, bc(dbc.rearrange("p (g h) -> p g h", h=GCH).unsqueeze(2), [P, GROUPS, CHUNK, GCH]), ALU.mult).then_inc(ud_ok, 1)
            pool.wait_ge(vin_ev, 4)
            pool.wait_ge(toep_dram, 64)
            pool.wait_ge(band_dram, 16)
            for k in range(SCAN_STEPS):
                d = 1 << k
                w = [P, PAIRS, NC - d]
                pr = bc(PDR[:, k, :].unsqueeze(2), w)
                pi = bc(PDI[:, k, :].unsqueeze(2), w)
                a = [s[:, :, 0:NC - d] for s in st]
                xrs, xis = XR[:, :, 0:NC - d], XI[:, :, 0:NC - d]
                pool.tensor_tensor(a[0], xrs, pr, ALU.mult)
                pool.tensor_tensor(a[1], xis, pi, ALU.mult)
                pool.tensor_tensor(a[2], xrs, pi, ALU.mult)
                link(pool.tensor_tensor(a[3], xis, pr, ALU.mult))
                pool.tensor_tensor(a[0], a[0], a[1], ALU.subtract)
                link(pool.tensor_tensor(a[2], a[2], a[3], ALU.add))
                pool.tensor_tensor(XR[:, :, d:NC], XR[:, :, d:NC], a[0], ALU.add)
                ins = pool.tensor_tensor(XI[:, :, d:NC], XI[:, :, d:NC], a[2], ALU.add)
                if k < SCAN_STEPS - 1:
                    link(ins)
                else:
                    ins.then_inc(scan_ok, 1)
            pool.wait_ge(ln_var, 1)
            pool.tensor_tensor(lnr[:, :], lnv[:, :], mhalf[:, :], ALU.pow).then_inc(ln_rstd, 1)
            for h in range(HEADS):
                pool.wait_ge(head_var, h + 1)
                pool.tensor_tensor(hrstd[:, h, :], hssv[:, h, :], mhalf[:, :], ALU.pow).then_inc(head_rstd, 1)
                pool.wait_ge(head_rstd, h + 1)
                o = mixT[:, h, :].rearrange("p (i v) -> p i v", i=NT)
                pool.tensor_tensor(o, o, bc(hrstd[:, h, :].unsqueeze(2), [P, NT, DV]), ALU.mult).then_inc(head_o, 1)
            for i in range(NT):
                pool.wait_ge(ms2v_ok, i + 1)
                pool.tensor_tensor(rstd2[:, i:i + 1], ms2v[:, i:i + 1], mhalf[:, 0:1], ALU.pow).then_inc(rstd2_ok, 1)

            pool.wait_ge(tab_ps, 1)
            pool.wait_ge(h2_out, 16 * NT)

            def gather(b):
                pool.indirect_dma_start(xg[b % 2], None, h2_dram,
                                        bass.IndirectOffsetOnAxis(ap=tabi[:, 0, b:b + 1], axis=0),
                                        bounds_check=L - 1, oob_is_err=False).then_inc(gather_in[b % 2], 16)

            def scatter(rows, s):
                pool.indirect_dma_start(y2_dram, bass.IndirectOffsetOnAxis(ap=rows, axis=0),
                                        yb[s], None, bounds_check=2 * L - 1, oob_is_err=False).then_inc(scat_out[s], 16)

            def gate_low(b):
                slot = pool.value_load(blkx[0:1, 0, b:b + 1], min_val=0, max_val=1)
                base = pool.snap(slot * (2 * KD * FF))
                for q in (2, 3):
                    pool.wait_ge(ex_gh, 4 * b + q + 1)
                    pool.tensor_tensor(wg_lo[:, D * q:D * q + D], RAB[:, bass.ds(base + D * q, D)], wg_hi[:, D * q:D * q + D],
                                       ALU.subtract).then_inc(ex_gl, 1)

            def rows_low(b):
                pool.wait_ge(ex_xh, b + 1)
                pool.tensor_tensor(xT_lo[:, :], xgT.rearrange("p k n -> p (k n)"), xT_hi[:, :], ALU.subtract).then_inc(ex_xl, 1)

            def block_io(b):
                pool.wait_ge(ex_xT, b + 1)
                gather(b + 2)
                gate_low(b + 1)
                rows_low(b + 1)
                if b:
                    pool.wait_ge(ex_y0, b)
                    pool.wait_ge(ex_y1, b)
                    scatter(tabi[:, 1, b - 1:b], (b - 1) % 2)

            pool.wait_ge(idx_ok, 1)
            gather(0)
            gather(1)
            gate_low(0)
            rows_low(0)
            for b in range(EXPERTS):
                block_io(b)
            nov = pool.value_load(nov_i[0:1, 0:1], min_val=0, max_val=NOVER)
            for b in range(EXPERTS, EXPERTS + NOVER, 2):
                with pool.If(nov > b - EXPERTS):
                    block_io(b)
                    block_io(b + 1)
            pool.tensor_copy(cur[:, 0:1], tabi[:, 1, bass.ds(nov + (EXPERTS - 1), 1)]).then_inc(cur_c, 1)
            pool.wait_ge(tail_y, 2)
            pool.wait_ge(cur_c, 1)
            scatter(cur[:, 0:1], 1)
            scat_all = pool.snap(nov * 8 + 16 * (EXPERTS // 2))
            gath_all = pool.snap(nov * 8 + 16 * (EXPERTS // 2 + 1))
            for n, (done, val) in enumerate(((scat_out[0], scat_all), (scat_out[1], scat_all),
                                             (gather_in[0], gath_all), (gather_in[1], gath_all))):
                pool.wait_ge(done, val)
                pool.tensor_tensor(pdump[:, n:n + 1], mhalf[:, 0:1], mhalf[:, 0:1], ALU.add).then_inc(moe_done, 1)
            for i in range(NT + 1):
                if i < NT:
                    pool.wait_ge(ms3v_ok, i + 1)
                    pool.tensor_tensor(rstd3[:, i:i + 1], ms3v[:, i:i + 1], mhalf[:, 0:1], ALU.pow).then_inc(rstd3_ok, 1)
                if i:
                    pool.wait_ge(fin_ok, i)
                    pool.dma_start(t["out"][0, (i - 1) * P:i * P, :], x2[:, i - 1, :]).then_inc(fin_out, 16)
            pool.wait_ge(fin_out, 16 * NT)

        @block.scalar
        def _(act):
            n = [0]
            def link(ins):
                n[0] += 1
                ins.then_inc(act_c, 1)
                act.wait_ge(act_c, n[0])

            act.dma_start(g1[:, :], vec("ln1_g", p=P), allow_slow_non_contiguous=True).then_inc(g1_in, 16)
            for i in range(NT):
                for dst, src in par_loads[i::NT]:
                    act.dma_start(dst, src, allow_slow_non_contiguous=True).then_inc(par_in, 16)
                act.wait_ge(x_in[i], 16)
                if i:
                    act.wait_ge(ms_ok, i)
                act.activation(xr[:, :], xt[:, i, :], ACT.Square, accum_out=ms[:, i:i + 1]).then_inc(ms_ok, 1)
            for dst, src in set_loads:
                act.dma_start(dst, src, allow_slow_non_contiguous=True).then_inc(set_in, 16)
            def evac(u):
                _, kind, i = UNITS[u]
                src = bank(4 + u % 4)
                act.wait_ge(unit_ps, u + 1)
                if kind == "ssm":
                    act.activation(uc[:, :, i, :], src[:, 0:CH].rearrange("p (g h) -> p g h", h=GCH), ACT.Copy).then_inc(unit_ev, 1)
                elif kind == "v":
                    c0 = CHUNKS[UNITS[u][0]][0] - 1024
                    act.activation(vtok[:, i, c0:c0 + WCH], src[:, 0:WCH], ACT.Copy).then_inc(unit_ev, 1)
                elif kind == "gate":
                    act.activation(convo[:, i // 2, 512 * (i % 2):512 * (i % 2) + 512], src, ACT.Sigmoid).then_inc(unit_ev, 1)
                elif kind == "a":
                    act.activation(convh[:, i // 2, 512 * (i % 2):512 * (i % 2) + 512], src, ACT.Copy).then_inc(unit_ev, 1)
                else:
                    c = 2 * (UNITS[u][0] - 5) + i // 2
                    if u == LAST_UNIT[4] + 1:
                        act.wait_ge(xT_ps, NT)
                    act.activation(qkT[:, c, 512 * (i % 2):512 * (i % 2) + 512], src, ACT.Copy).then_inc(unit_ev, 1)

            for u in range(6):
                evac(u)
            act.wait_ge(band_ps, 1)
            act.activation(brow[:, :], psum[0:HEADS, 0, 0:384], ACT.Copy, scale=1.0 / SCALE).then_inc(band_row, 1)
            act.wait_ge(lam_dot, 1)
            act.activation(lam[:, 2:4], lam[:, 0:2], ACT.Exp).then_inc(lam_exp, 1)
            act.wait_ge(par_in, 16 * PAR_N)
            act.activation(sv[:, 1, :], sv[:, 0, :], ACT.Exp).then_inc(ssm_dt, 1)
            evac(6)
            evac(7)
            act.wait_ge(ssm_ang, 1)
            act.activation(sv[:, 6, :], sv[:, 4, :], ACT.Exp)
            act.activation(sv[:, 7, :], sv[:, 5, :], ACT.Sin)
            act.activation(sv[:, 8, :], sv[:, 5, :], ACT.Sin, scale=0.5).then_inc(ssm_sin, 1)

            act.wait_ge(const_ok, 4)
            for u in range(8, 16):
                evac(u)
            for i in range(4):
                act.wait_ge(uT_ps, i + 1)
                act.activation(UT[:, 4 * i:4 * i + 4, :].rearrange("p g c -> p (g c)"), bank(i), ACT.Copy).then_inc(uT_ev, 1)
            for i in range(4):
                act.wait_ge(wi_ps, i + 1)
                dst = (WinR, WinI)[i // 2]
                act.activation(dst[:, 4 * (i % 2):4 * (i % 2) + 4, :].rearrange("p a s -> p (a s)"), bank(i), ACT.Copy).then_inc(wi_ev, 1)
            act.wait_ge(k_ps, 1)
            act.wait_ge(kz_ok, 1)
            for r in range(4):
                ins = act.activation(ksb[32 * r:32 * r + GCH, :, P:2 * P],
                                     psum[32 * r:32 * r + GCH, 0, :].rearrange("p (q n) -> p q n", q=4), ACT.Copy)
            ins.then_inc(k_ev, 1)
            for u in range(16, LAST_UNIT[3] + 1):
                evac(u)
            act.memzero(XR[:, :, 0:1])
            act.memzero(XI[:, :, 0:1])
            for i in range(4):
                act.wait_ge(vin_ps, i + 1)
                dst = (XR, XI)[i // 2]
                act.activation(dst[:, 4 * (i % 2):4 * (i % 2) + 4, 1:NC],
                               bank(i % 2).rearrange("p (a c) -> p a c", a=4)[:, :, 0:NC - 1], ACT.Copy).then_inc(vin_ev, 1)
            for u in range(LAST_UNIT[3] + 1, len(UNITS)):
                evac(u)
            act.wait_ge(set_in, 16 * SET_N)
            for c in range(2):
                act.wait_ge(conv_ps, c + 1)
                act.activation(convo[:, c, :], banks(2 - 2 * c, 2), ACT.Identity, bias=convb[:, c:c + 1]).then_inc(conv_ev, 1)
            act.wait_ge(y_ev, 4)
            act.activation(RG[:, 6144:8192], RG[:, 6144:8192], ACT.Gelu_apprx_tanh).then_inc(gelu_ok, 1)

            act.dma_start(rw[:, :, 0:4], t["group_router_w"][0].rearrange("(k p) n -> p k n", p=P)).then_inc(rw_in, 16)
            act.dma_start(rw[:, :, 4:36], t["expert_router_w"][0].rearrange("(k p) n -> p k n", p=P)).then_inc(rw_in, 16)
            link(act.activation(sg[:, :], sg[:, :], ACT.Copy, scale=1.0 - LAM_INIT))
            nm = [0]

            def misc(job):
                kind, i = job
                nm[0] += 1
                act.wait_ge(misc_ps, nm[0])
                src = bank(7)
                if kind == "conv_to_tok":
                    ins = act.activation(convt[:, 2 * i:2 * i + 2, :].rearrange("p t n -> p (t n)"), src, ACT.Copy)
                elif kind == "ssm_to_ch":
                    c, jh = i // 2, i % 2
                    dst = gT[:, c, :].rearrange("p (n j) -> p j n", j=CHUNK)[:, 4 * jh:4 * jh + 4, :]
                    ins = act.activation(dst, src.rearrange("p (j n) -> p j n", j=4), ACT.Copy)
                elif kind == "conv_to_ch":
                    c, half = i // 2, i % 2
                    z = convo[:, c, 512 * half:512 * half + 512]
                    link(act.activation(z, src, ACT.Identity, bias=lnb[:, c:c + 1], scale=lng[:, c:c + 1]))
                    act.activation(silu[:, i, :], z, ACT.Tanh, scale=0.5).then_inc(silu_t, 1)
                    ins = None
                elif kind == "glu":
                    c, half = i // 2, i % 2
                    ins = act.activation(glut[:, c, 512 * half:512 * half + 512], src, ACT.Tanh,
                                         bias=glub[:, c:c + 1], scale=0.5)
                else:
                    h, half = i // 2, i % 2
                    ins = act.activation(mixT[:, h, 512 * half:512 * half + 512], src, ACT.Copy, scale=sg[:, 0:1])
                return ins

            link(act.activation(glub[:, :], glub[:, :], ACT.Copy, scale=0.5))

            def exps(k):
                h, i = ITEMS[k]
                nk = (i + 1) * P
                far = max(nk - 256, 0)
                for m in range(2):
                    act.wait_ge(nm_ok, 2 * k + m + 1)
                    sl = 2 * (k % 2) + m
                    st_ = smx[:, k % 2, m, :]
                    ins = act.activation(pexp[:, sl, far:nk], pexp[:, sl, far:nk], ACT.Exp,
                                         bias=st_[:, 2:3], accum_out=st_[:, 4:5])
                    if far:
                        ins = act.activation(pexp[:, sl, 0:far], banks(2 * m, 2)[:, 0:far], ACT.Exp,
                                             bias=st_[:, 3:4], scale=SCALE, accum_out=st_[:, 5:6])
                    ins.then_inc(e_ok, 1)

            def p_evac(k):
                h, i = ITEMS[k]
                act.wait_ge(pT_ps, k + 1)
                act.activation(pT[k % 2][:, 0:i + 1, :].rearrange("p k n -> p (k n)"),
                               banks(4, 2)[:, 0:(i + 1) * P], ACT.Copy).then_inc(pT_ev, 1)

            def o_evac(k):
                h, i = ITEMS[k]
                act.wait_ge(o_ps, k + 1)
                o = mixT[:, h, i * P:(i + 1) * P]
                act.activation(o, psum[:, 6, 0:P], ACT.Copy).then_inc(o_ev, 1)
                act.activation(psum[:, 6, P:2 * P], psum[:, 6, 0:P], ACT.Square, accum_out=hss[:, h, i:i + 1]).then_inc(head_ss, 1)

            for k in range(ITERS + 2):
                if k < NI:
                    exps(k)
                if 1 <= k <= NI:
                    p_evac(k - 1)
                if 2 <= k < NI + 2:
                    if k >= 3:
                        act.wait_ge(head_ss, k - 2)
                    o_evac(k - 2)
                for job in MISC_AT.get(k, []):
                    ins = misc(job)
                    if ins is not None:
                        ins.then_inc(misc_ev, 1)

            def reload(i):
                if i:
                    act.wait_ge(x2_ok, i)
                act.dma_start(xr[:, :], t["x"][0, i * P:(i + 1) * P, :]).then_inc(xr_in, 16)

            act.wait_ge(head_ss, NI)
            reload(0)
            for i in range(NT):
                act.wait_ge(x2_ok, i + 1)
                if i + 1 < NT:
                    reload(i + 1)
                if i:
                    act.wait_ge(ms2_ok, i)
                act.activation(banks(6, 2), x2[:, i, :], ACT.Square, accum_out=ms2[:, i:i + 1]).then_inc(ms2_ok, 1)
                act.wait_ge(h2_ok, i + 1)
                act.dma_start(h2_dram[i * P:(i + 1) * P, :].rearrange("p (k n) -> p k n", k=KD),
                              mixT[:, :, i * P:(i + 1) * P]).then_inc(h2_out, 16)
            act.wait_ge(gd_ok, 1)
            act.activation(rrv("gexp"), rrv("gdif"), ACT.Exp)
            act.activation(rrv("eexp"), rrv("edif"), ACT.Exp).then_inc(ge_ok, 1)

            def actT_evac(done):
                act.wait_ge(ex_aT, done)
                act.activation(actT_hi, bank(4), ACT.Copy).then_inc(ex_aTe, 1)

            def split_high(b, down):
                at = slice(b, b + 1) if isinstance(b, int) else bass.ds(b, 1)
                slot = act.value_load(blkx[0:1, 0, at], min_val=0, max_val=1)
                loads = [act.value_load(blkx[0:1, 1 + n, at], min_val=1, max_val=EXPERTS // 2) for n in range(2)]
                base = act.snap(slot * (FK * D))
                for n in range(2):
                    act.wait_ge(wd_in[n], act.snap(loads[n] * 16))
                if down is not None:
                    act.wait_ge(ex_y, down)
                for k in range(FK):
                    act.activation(wd_hi[:, D * k:D * k + D], RCE[:, bass.ds(base + D * k, D)], ACT.Copy).then_inc(ex_wh, 1)

            def gate_high(b, used):
                at = slice(b, b + 1) if isinstance(b, int) else bass.ds(b, 1)
                slot = act.value_load(blkx[0:1, 0, at], min_val=0, max_val=1)
                loads = [act.value_load(blkx[0:1, 1 + n, at], min_val=1, max_val=EXPERTS // 2) for n in range(2)]
                base = act.snap(slot * (2 * KD * FF))
                for n in range(2):
                    act.wait_ge(wgu_in[n], act.snap(loads[n] * 32))
                if used is not None:
                    act.wait_ge(ex_g, used)
                for q in range(4):
                    act.activation(wg_hi[:, D * q:D * q + D], RAB[:, bass.ds(base + D * q, D)], ACT.Copy).then_inc(ex_gh, 1)

            def rows_high(done):
                act.wait_ge(ex_xTe, done)
                act.activation(xT_hi[:, :], xgT.rearrange("p k n -> p (k n)"), ACT.Copy).then_inc(ex_xh, 1)

            def silu_gate(done):
                act.wait_ge(ex_g, done)
                act.activation(actb, bank(2), ACT.Silu).then_inc(ex_s, 1)

            def y_half(s, b, down, scat, done):
                gate = tabg[:, b:b + 1] if isinstance(b, int) else tabg[:, bass.ds(b, 1)]
                act.wait_ge(ex_y, down)
                if scat is not None:
                    act.wait_ge(scat_out[s], scat)
                act.activation(yb[s][:, 0:512], bank(5), ACT.Copy, scale=gate).then_inc(done, 1)

            def step(j, s):
                b, prev, b1, b2 = j * 2 + s, j * 2 + s - 1, j * 2 + s + 1, j * 2 + s + 2
                scat = (j - 1 + s) * 16
                if not isinstance(b, int):
                    b, prev, b1, b2, scat = [act.snap(v) for v in (b, prev, b1, b2, scat)]
                split_high(prev, None if isinstance(prev, int) and prev == 0 else prev)
                actT_evac(b)
                silu_gate(b1)
                gate_high(b1, b1)
                rows_high(b2)
                y_half(1 - s, prev, b, None if isinstance(scat, int) and scat == 0 else scat, ex_y0)

            act.wait_ge(idx_ok, 1)
            act.wait_ge(x2_out, 16 * NT)
            gate_high(0, None)
            rows_high(1)
            silu_gate(1)
            gate_high(1, 1)
            rows_high(2)
            step(0, 1)
            step(1, 0)
            step(1, 1)
            with act.Fori(2, EXPERTS // 2) as j:
                for s in range(2):
                    step(j, s)
            nov = act.value_load(nov_i[0:1, 0:1], min_val=0, max_val=NOVER)
            for b in range(0, NOVER, 2):
                with act.If(nov > b):
                    for s in range(2):
                        step((EXPERTS + b) // 2, s)
            blocks, last = act.snap(nov + EXPERTS), act.snap(nov + (EXPERTS - 1))
            scat = act.snap(nov * 8 + 16 * (EXPERTS // 2 - 1))
            act.wait_ge(ex_aT, blocks)
            act.activation(actT_last, bank(4), ACT.Copy).then_inc(ex_aTe, 1)
            y_half(1, last, blocks, scat, tail_y)
            act.wait_ge(moe_done, 4)
            act.dma_start(fgb, t["final_g"].rearrange("(o d) -> o d", o=1).to_broadcast([P, D])).then_inc(fg_in, 16)
            for i in range(NT + 1):
                if i < NT:
                    act.wait_ge(y2_in[i % 4], 16 * (i // 4 + 1))
                    if i >= 3:
                        act.wait_ge(fin_ok, i - 2)
                    act.activation(banks(2 * (i % 3), 2), y2t[:, i % 4, 0, :], ACT.Copy).then_inc(ya_ps, 1)
                if i >= 1:
                    act.wait_ge(x3_ok, i)
                    if i >= 2:
                        act.wait_ge(ms3_ok, i - 1)
                    act.activation(banks(6, 2), banks(2 * ((i - 1) % 3), 2), ACT.Square,
                                   accum_out=ms3[:, i - 1:i]).then_inc(ms3_ok, 1)

        @block.tensor
        def _(pe):
            pe.wait_ge(const_ok, 1)
            chunk_seen = [-1]

            def unit(u):
                c, kind, i = UNITS[u]
                if chunk_seen[0] != c:
                    chunk_seen[0] = c
                    pe.wait_ge(win_in[c % 3], 16 * (c // 3 + 1))
                if u < NT:
                    pe.wait_ge(hT_ok, 2 * (u + 1))
                if u >= 4:
                    pe.wait_ge(unit_ev, u - 3)
                w = win[:, c % 3]
                for k in range(KD):
                    first, last = k == 0, k == KD - 1
                    if kind == "ssm":
                        ins = pe.matmul(bank(4 + u % 4)[:, 0:WCH], hT[:, k, i:L:CHUNK], w[:, k, :], start=first, stop=last)
                    elif kind == "v":
                        ins = pe.matmul(bank(4 + u % 4)[:, 0:WCH], hT[:, k, i * P:(i + 1) * P], w[:, k, :], start=first, stop=last)
                    else:
                        ct, half = i // 2, i % 2
                        ins = pe.matmul(bank(4 + u % 4), w[:, k, ct * P:(ct + 1) * P],
                                        hT[:, k, 512 * half:512 * half + 512], start=first, stop=last)
                ins.then_inc(unit_ps, 1)

            for i in range(NT):
                pe.wait_ge(xn_ok, i + 1)
                if i >= 2:
                    pe.wait_ge(hT_ok, 2 * (i - 1))
                for k in range(KD):
                    ins = pe.transpose(psum[:, 2 * (i % 2) + k // 4, P * (k % 4):P * (k % 4) + P],
                                       xt[:, i, k * P:(k + 1) * P], ident[:, :])
                ins.then_inc(xT_ps, 1)
                if i >= 2:
                    unit(i - 2)
            pe.wait_ge(hT_ok, 2 * (NT - 1))
            pe.wait_ge(par_in, 16 * PAR_N)
            pe.matmul(psum[0:HEADS, 0, 0:384], relt[:, :], onehot, start=True, stop=True).then_inc(band_ps, 1)
            pe.transpose(psum[:, 1, 0:16], lrow[0:16, :], ident[0:16, 0:16])
            pe.transpose(psum[:, 1, 128:256], crow[:, 0, :], ident[:, :])
            pe.transpose(psum[:, 1, 256:384], crow[:, 1, :], ident[:, :]).then_inc(lrow_ps, 1)
            for u in range(NT - 2, 16):
                unit(u)
            pe.wait_ge(unit_ev, 16)
            for g in range(GROUPS):
                ins = pe.transpose(psum[:, g // 4, P * (g % 4):P * (g % 4) + P],
                                   uc[:, g].rearrange("p i h -> p (i h)"), ident[:, :])
                if g % 4 == 3:
                    ins.then_inc(uT_ps, 1)
            pe.wait_ge(vb_ok, 1)
            for r, vb in enumerate((VBR, VBI)):
                for a in range(PAIRS):
                    b = 2 * r + a // 4
                    if a % 4 == 0:
                        pe.wait_ge(uT_ev, b + 1)
                    ins = pe.transpose(psum[:, b, P * (a % 4):P * (a % 4) + P],
                                       vb[:, a].rearrange("p i h -> p (i h)"), ident[:, :])
                    if a % 4 == 3:
                        ins.then_inc(wi_ps, 1)
            pe.wait_ge(ca_ok, 1)
            pe.wait_ge(wi_ev, 1)
            for g in range(GROUPS):
                a, q = g // 2, STATES * (g % 2)
                out = psum[32 * (g % 4):32 * (g % 4) + GCH, 0, P * (g // 4):P * (g // 4) + P]
                pe.matmul(out, BBR[q:q + STATES, a, :], CAR[q:q + STATES, a, 0:CHUNK, :].rearrange("p t h -> p (t h)"),
                          start=True, stop=False)
                ins = pe.matmul(out, BBI[q:q + STATES, a, :], CAI[q:q + STATES, a, 0:CHUNK, :].rearrange("p t h -> p (t h)"),
                                start=False, stop=True)
            ins.then_inc(k_ps, 1)
            for u in range(16, LAST_UNIT[3] + 1):
                unit(u)
            pe.wait_ge(k_ev, 1)
            pe.wait_ge(wi_ev, 4)
            for r, win_ in enumerate((WinR, WinI)):
                for a in range(PAIRS):
                    b = a // 4
                    if r == 1 and a % 4 == 0:
                        pe.wait_ge(vin_ev, b + 1)
                    for q in range(2):
                        ins = pe.matmul(psum[STATES * q:STATES * (q + 1), b, P * (a % 4):P * (a % 4) + P],
                                        win_[:, a, STATES * q:STATES * (q + 1)], UT[:, 2 * a + q, :], start=True, stop=True)
                    if a % 4 == 3:
                        ins.then_inc(vin_ps, 1)
            for u in range(LAST_UNIT[3] + 1, len(UNITS)):
                unit(u)
            pe.wait_ge(scan_ok, 1)
            pe.wait_ge(toep_in, 16 * CHUNK)
            pe.wait_ge(conv_ev, 2)
            for g in range(GROUPS):
                a, q = g // 2, STATES * (g % 2)
                b, c = 2 * (g % 2) + g // 8, (g // 2) % 4
                out = psum[:, b, P * c:P * c + P]
                pe.matmul(out, XR[q:q + STATES, a, :], CAR[q:q + STATES, a, 1:CHUNK + 1, :].rearrange("p t h -> p (t h)"),
                          start=True, stop=False)
                pe.matmul(out, XI[q:q + STATES, a, :], CAI[q:q + STATES, a, 1:CHUNK + 1, :].rearrange("p t h -> p (t h)"),
                          start=False, stop=False)
                ins = pe.matmul(out, UT[:, g, :], TG[:, g, :], start=False, stop=True)
                if g % 8 == 7:
                    ins.then_inc(y_ps, 1)

            nm = [0]

            def misc(job):
                kind, i = job
                if nm[0] and MISC_ORDER[nm[0] - 1][0] != "conv_to_ch":
                    pe.wait_ge(misc_ev, sum(1 for j in MISC_ORDER[:nm[0]] if j[0] != "conv_to_ch"))
                elif nm[0]:
                    pe.wait_ge(silu_t, sum(1 for j in MISC_ORDER[:nm[0]] if j[0] == "conv_to_ch"))
                nm[0] += 1
                if kind == "conv_to_tok":
                    for k in range(4):
                        tt, c = 2 * i + k // 2, k % 2
                        ins = pe.transpose(psum[:, 7, P * k:P * k + P], convo[:, c, tt * P:(tt + 1) * P], ident[:, :])
                elif kind == "ssm_to_ch":
                    pe.wait_ge(gelu_ok, 1)
                    c, jh = i // 2, i % 2
                    for k in range(4):
                        ins = pe.transpose(psum[:, 7, P * k:P * k + P], yc[:, 4 * jh + k, c * P:(c + 1) * P], ident[:, :])
                elif kind == "conv_to_ch":
                    pe.wait_ge(ln_ok, 1)
                    c, half = i // 2, i % 2
                    for k in range(4):
                        ins = pe.transpose(psum[:, 7, P * k:P * k + P], convt[:, 4 * half + k, c * P:(c + 1) * P], ident[:, :])
                elif kind == "glu":
                    c, half = i // 2, i % 2
                    for k in range(2):
                        ins = pe.matmul(bank(7), gluw[:, k, c * P:(c + 1) * P], gT[:, k, 512 * half:512 * half + 512],
                                        start=k == 0, stop=k == 1)
                else:
                    h, half = i // 2, i % 2
                    pe.wait_ge(head_o, h + 1)
                    for k in range(4):
                        ins = pe.transpose(psum[:, 7, P * k:P * k + P],
                                           mixT[:, h, (4 * half + k) * P:(4 * half + k + 1) * P], ident[:, :])
                ins.then_inc(misc_ps, 1)

            pe.wait_ge(set_in, 16 * SET_N)
            pe.wait_ge(unit_ev, len(UNITS))
            pe.wait_ge(y_ev, 4)
            def scores(k, m):
                h, i = ITEMS[k]
                q = DK * (h % 2)
                nk = (i + 1) * P
                if k:
                    pe.wait_ge(e_ok, 2 * (k - 1) + m + 1)
                for b in range(0, nk, 512):
                    w = min(512, nk - b)
                    ins = pe.matmul(psum[:, 2 * m + b // 512, 0:w],
                                    qkT[q:q + DK, 2 * m + h // 2, i * P:(i + 1) * P],
                                    qkT[q:q + DK, 4 + 2 * m + h // 2, b:b + w], start=True, stop=True)
                ins.then_inc(s_ps, 1)

            def turn(k):
                i = ITEMS[k][1]
                pe.wait_ge(p_ok, k + 1)
                if k >= 1:
                    pe.wait_ge(pT_ev, k)
                for c in range(i + 1):
                    ins = pe.transpose(psum[:, 4 + c // 4, P * (c % 4):P * (c % 4) + P],
                                       pexp[:, 2 * (k % 2), c * P:(c + 1) * P], ident[:, :])
                ins.then_inc(pT_ps, 1)

            def times_v(k):
                h, i = ITEMS[k]
                pe.wait_ge(pT_ev, k + 1)
                if k >= 1:
                    pe.wait_ge(head_ss, k)
                for c in range(i + 1):
                    ins = pe.matmul(psum[:, 6, 0:P], pT[k % 2][:, c, :], vtok[:, c, h * DV:(h + 1) * DV],
                                    start=c == 0, stop=c == i)
                ins.then_inc(o_ps, 1)

            for k in range(ITERS + 2):
                if k < NI:
                    scores(k, 0)
                if k < NI:
                    scores(k, 1)
                if 2 <= k < NI + 2:
                    times_v(k - 2)
                if 1 <= k <= NI:
                    turn(k - 1)
                for job in MISC_AT.get(k, []):
                    misc(job)

            for s in range(3):
                pe.wait_ge(wout_in[s], 16)
            pe.wait_ge(rw_in, 32)
            pe.wait_ge(misc_ev, sum(1 for j in MISC_ORDER if j[0] != "conv_to_ch"))
            pe.wait_ge(conv_ok, 4)
            pe.wait_ge(ssm_ok, 1)
            def half_product(k, half):
                for c in range(KD):
                    ins = pe.matmul(bank(2 * (k % 2) + half), mixT[:, c, k * P:(k + 1) * P],
                                    wout[:, c, 512 * half:512 * half + 512], start=c == 0, stop=c == KD - 1)
                return ins

            for k in range(NT + 2):
                if k < NT:
                    if k >= 2:
                        pe.wait_ge(x2_ok, k - 1)
                    half_product(k, 0)
                if k >= 2:
                    pe.wait_ge(h2T_ok, k - 1)
                    if k >= 3:
                        pe.wait_ge(lg_ok, k - 2)
                    for c in range(KD):
                        ins = pe.matmul(psum[:, 4, 0:36], h2T[:, c, :], rw[:, c, :], start=c == 0, stop=c == KD - 1)
                    ins.then_inc(lg_ps, 1)
                if 1 <= k <= NT:
                    pe.wait_ge(h2_ok, k)
                    for c in range(4):
                        pe.transpose(psum[:, 5, P * c:P * c + P], mixT[:, 4 + c, (k - 1) * P:k * P], ident[:, :])
                    if k >= 2:
                        pe.wait_ge(lg_ok, k - 1)
                    for c in range(4):
                        ins = pe.transpose(psum[:, 4, P * c:P * c + P], mixT[:, c, (k - 1) * P:k * P], ident[:, :])
                    ins.then_inc(h2T_ps, 1)
                if k < NT:
                    half_product(k, 1).then_inc(proj_ps, 1)

            pe.wait_ge(mm_ok, 1)
            pe.wait_ge(const_ok, 3)
            pe.matmul(bank(0)[:, 0:256], tri[:, :], mbf[:, :, :].rearrange("p t n -> p (t n)"), start=True, stop=False)
            for s in range(1, NT):
                pe.matmul(bank(0)[:, 32 * s:256], onesb[:, :], mbf[:, 0:NT - s, :].rearrange("p t n -> p (t n)"),
                          start=False, stop=s == NT - 1)
            for i in range(NT):
                ins = pe.matmul(bank(1)[:, 0:32], onesb[:, :], mbf[:, i, :], start=i == 0, stop=i == NT - 1)
            ins.then_inc(rank_ps, 1)
            for r in range(16):
                if r % 8 == 0:
                    pe.wait_ge(tab_ok, r // 8 + 1)
                ins = pe.matmul(bank(2)[:, 0:3 * NBLK], slot1h[:, r, :], bval[:, r].rearrange("p n v -> p (n v)"),
                                start=r == 0, stop=r == 15)
            ins.then_inc(tab_ps, 1)

            def xT(s, got):
                pe.wait_ge(gather_in[s], got)
                for k in range(KD):
                    ins = pe.transpose(psum[:, k // 4, P * (k % 4):P * (k % 4) + P],
                                       xg[s].rearrange("p (n k) -> p k n", k=KD)[:, k, :], ident[:, :])
                ins.then_inc(ex_xT, 1)

            def block_weights(b):
                at = slice(b, b + 1) if isinstance(b, int) else bass.ds(b, 1)
                slot = pe.value_load(blkx[0:1, 0, at], min_val=0, max_val=1)
                return slot, [pe.value_load(blkx[0:1, 1 + n, at], min_val=1, max_val=EXPERTS // 2) for n in range(2)]

            def up_product(base):
                for k in range(KD):
                    ins = pe.matmul(bank(3), xgT[:, k, :], RAB[:, bass.ds(base + FF * k, FF)], start=k == 0, stop=k == KD - 1)
                ins.then_inc(ex_u, 1)

            def gate_product():
                for k in range(KD):
                    hi, lo = xT_hi[:, P * k:P * k + P], xT_lo[:, P * k:P * k + P]
                    cols = slice(FF * k, FF * k + FF)
                    pe.matmul(bank(2), hi, wg_hi[:, cols], start=k == 0, stop=False)
                    pe.matmul(bank(2), hi, wg_lo[:, cols], start=False, stop=False)
                    ins = pe.matmul(bank(2), lo, wg_hi[:, cols], start=False, stop=k == KD - 1)
                ins.then_inc(ex_g, 1)

            def aT(a, freed):
                pe.wait_ge(ex_a, a)
                if freed is not None:
                    pe.wait_ge(ex_aTl, freed)
                for k in range(FK):
                    ins = pe.transpose(psum[:, 4, P * k:P * k + P],
                                       actb.rearrange("p (n k) -> p k n", k=FK)[:, k, :], ident[:, :])
                ins.then_inc(ex_aT, 1)

            def down(b1, freed):
                pe.wait_ge(ex_aTe, b1)
                pe.wait_ge(ex_aTl, b1)
                pe.wait_ge(ex_wl, b1 * FK if isinstance(b1, int) else pe.snap(b1 * FK))
                if freed is not None:
                    pe.wait_ge(ex_y0, freed)
                    pe.wait_ge(ex_y1, freed)
                for half in range(2):
                    for k in range(FK):
                        hi, lo = actT_hi[:, P * k:P * k + P], actT_lo[:, P * k:P * k + P]
                        cols = slice(D * k + 512 * half, D * k + 512 * half + 512)
                        pe.matmul(bank(5 + half), hi, wd_hi[:, cols], start=k == 0, stop=False)
                        pe.matmul(bank(5 + half), hi, wd_lo[:, cols], start=False, stop=False)
                        ins = pe.matmul(bank(5 + half), lo, wd_hi[:, cols], start=False, stop=k == FK - 1)
                ins.then_inc(ex_y, 1)

            def step(j, s):
                first = isinstance(j, int) and j == 0 and s == 0
                b, prev, b1 = j * 2 + s, j * 2 + s - 1, j * 2 + s + 1
                if not isinstance(b, int):
                    b, prev, b1 = pe.snap(b), pe.snap(prev), pe.snap(b1)
                freed = None if isinstance(prev, int) and prev == 0 else prev
                slot, loads = block_weights(b)
                up = pe.snap(slot * (2 * KD * FF) + KD * FF)
                parts = b1 * 4 if isinstance(b1, int) else pe.snap(b1 * 4)
                for n in range(2):
                    pe.wait_ge(wgu_in[n], pe.snap(loads[n] * 32))
                pe.wait_ge(ex_xTe, b1)
                if not first:
                    pe.wait_ge(ex_a, b)
                up_product(up)
                if not first:
                    aT(b, freed)
                    pe.wait_ge(ex_s, b)
                pe.wait_ge(ex_xl, b1)
                pe.wait_ge(ex_gl, parts)
                gate_product()
                xT(1 - s, (j + 1 + s) * 16)
                if not first:
                    down(b, freed)

            pe.wait_ge(idx_ok, 1)
            xT(0, 16)
            step(0, 0)
            step(0, 1)
            with pe.Fori(1, EXPERTS // 2) as j:
                for s in range(2):
                    step(j, s)
            nov = pe.value_load(nov_i[0:1, 0:1], min_val=0, max_val=NOVER)
            for b in range(0, NOVER, 2):
                with pe.If(nov > b):
                    for s in range(2):
                        step((EXPERTS + b) // 2, s)
            blocks, last = pe.snap(nov + EXPERTS), pe.snap(nov + (EXPERTS - 1))
            slot, loads = block_weights(last)
            base = pe.snap(slot * (FK * D))
            aT(blocks, last)
            for n in range(2):
                pe.wait_ge(wd_in[n], pe.snap(loads[n] * 16))
            pe.wait_ge(ex_aTe, blocks)
            pe.wait_ge(ex_y0, last)
            pe.wait_ge(ex_y1, last)
            for half in range(2):
                for k in range(FK):
                    ins = pe.matmul(bank(5 + half), actT_last[:, P * k:P * k + P],
                                    RCE[:, bass.ds(base + (D * k + 512 * half), 512)], start=k == 0, stop=k == FK - 1)
            ins.then_inc(ex_y, 1)

        @block.vector
        def _(dve):
            n = [0]
            def link(ins):
                n[0] += 1
                ins.then_inc(dve_c, 1)
                dve.wait_ge(dve_c, n[0])

            def norm_pair(r):
                dve.wait_ge(ms_ok, 2 * r + 2)
                dve.tensor_scalar(msv[:, 2 * r:2 * r + 2], ms[:, 2 * r:2 * r + 2], 1.0 / D, RMS_EPS, ALU.mult, ALU.add)\
                   .then_inc(msv_ok, 1)
                dve.wait_ge(rstd_ok, r + 1)
                for i in (2 * r, 2 * r + 1):
                    dve.tensor_scalar(xt[:, i, :], xt[:, i, :], rstd[:, i:i + 1], None, ALU.mult).then_inc(xn_ok, 1)

            def hT_evac(i):
                dve.wait_ge(xT_ps, i + 1)
                if i == 0:
                    dve.wait_ge(g1_in, 16)
                for b in range(2):
                    dve.tensor_tensor(hT[:, 4 * b:4 * b + 4, i * P:(i + 1) * P],
                                      bank(2 * (i % 2) + b).rearrange("p (k n) -> p k n", k=4),
                                      bc(g1[:, 4 * b:4 * b + 4].unsqueeze(2), [P, 4, P]), ALU.mult).then_inc(hT_ok, 1)

            norm_pair(0)
            for r in range(1, 4):
                norm_pair(r)
                hT_evac(2 * r - 2)
                hT_evac(2 * r - 1)
            hT_evac(6)
            hT_evac(7)

            dve.wait_ge(par_in, 16 * PAR_N)
            for v in range(2):
                ins = dve.tensor_tensor_reduce(out=ctmp[:, 64 * v:64 * v + DK], in0=lamv[:, 2 * v, :], in1=lamv[:, 2 * v + 1, :],
                                               scale=1.0, scalar=0.0, op0=ALU.mult, op1=ALU.add, accum_out=lam[:, v:v + 1])
            ins.then_inc(lam_dot, 1)
            dve.wait_ge(lrow_ps, 1)
            dve.tensor_copy(sv[:, 2:4, :].rearrange("p n a -> p (n a)"), psum[:, 1, 0:16])
            c4 = psum[:, 1, 128:384].rearrange("p (r a h) -> p r a h", r=2, a=PAIRS)
            dve.tensor_copy(CAR[:, :, 0, :], c4[:, 0])
            link(dve.tensor_scalar(CAI[:, :, 0, :], c4[:, 1], -1.0, None, ALU.mult))
            dve.wait_ge(lam_exp, 1)
            link(dve.tensor_tensor(lam[:, 0:1], lam[:, 3:4], lam[:, 2:3], ALU.subtract))
            dve.tensor_scalar(lam[:, 1:2], lam[:, 0:1], LAM_INIT, None, ALU.subtract).then_inc(lam_ok, 1)
            dve.wait_ge(ssm_dt, 1)
            dve.tensor_tensor(sv[:, 4, :], sv[:, 2, :], sv[:, 1, :], ALU.mult)
            link(dve.tensor_tensor(sv[:, 9, :], sv[:, 3, :], sv[:, 1, :], ALU.mult))
            link(dve.tensor_scalar(sv[:, 10, :], sv[:, 9, :], 1.0 / (2.0 * math.pi), ROUND, ALU.mult, ALU.add))
            link(dve.tensor_scalar(sv[:, 10, :], sv[:, 10, :], ROUND, None, ALU.subtract))
            for c in TWO_PI:
                link(dve.scalar_tensor_tensor(sv[:, 9, :], sv[:, 10, :], -c, sv[:, 9, :], ALU.mult, ALU.add))
            dve.tensor_scalar(sv[:, 5, :], sv[:, 9, :], PI, -PI, ALU.min, ALU.max).then_inc(ssm_ang, 1)
            dve.tensor_tensor(sv[:, 11, :], sv[:, 2, :], sv[:, 2, :], ALU.mult)
            link(dve.tensor_tensor(sv[:, 12, :], sv[:, 3, :], sv[:, 3, :], ALU.mult))
            link(dve.tensor_tensor(sv[:, 11, :], sv[:, 11, :], sv[:, 12, :], ALU.add))
            link(dve.reciprocal(sv[:, 13, :], sv[:, 11, :]))
            dve.wait_ge(ssm_sin, 1)
            link(dve.scalar_tensor_tensor(sv[:, 14, :], sv[:, 8, :], -2.0, sv[:, 8, :], ALU.mult, ALU.mult))
            dve.scalar_tensor_tensor(PWR[:, 1, :], sv[:, 14, :], 1.0, sv[:, 6, :], ALU.add, ALU.mult)
            dve.tensor_tensor(PWI[:, 1, :], sv[:, 6, :], sv[:, 7, :], ALU.mult)
            dve.memset(PWR[:, 0, :], 1.0)
            link(dve.memset(PWI[:, 0, :], 0.0))
            link(dve.tensor_scalar(sv[:, 15, :], PWR[:, 1, :], 1.0, None, ALU.subtract))
            dve.tensor_tensor(sv[:, 16, :], sv[:, 15, :], sv[:, 2, :], ALU.mult)
            dve.tensor_tensor(sv[:, 17, :], PWI[:, 1, :], sv[:, 3, :], ALU.mult)
            dve.tensor_tensor(sv[:, 18, :], PWI[:, 1, :], sv[:, 2, :], ALU.mult)
            link(dve.tensor_tensor(sv[:, 19, :], sv[:, 15, :], sv[:, 3, :], ALU.mult))
            dve.tensor_tensor(sv[:, 20, :], sv[:, 16, :], sv[:, 17, :], ALU.add)
            link(dve.tensor_tensor(sv[:, 21, :], sv[:, 18, :], sv[:, 19, :], ALU.subtract))
            dve.tensor_tensor(sv[:, 22, :], sv[:, 20, :], sv[:, 13, :], ALU.mult)
            link(dve.tensor_tensor(sv[:, 23, :], sv[:, 21, :], sv[:, 13, :], ALU.mult))

            def cmul(outr, outi, ar, ai, br, bi, t1, t2, t3, t4, neg=False):
                dve.tensor_tensor(t1, ar, br, ALU.mult)
                dve.tensor_tensor(t2, ai, bi, ALU.mult)
                dve.tensor_tensor(t3, ar, bi, ALU.mult)
                link(dve.tensor_tensor(t4, ai, br, ALU.mult))
                dve.tensor_tensor(outr, t1, t2, ALU.add if neg else ALU.subtract)
                link(dve.tensor_tensor(outi, t3, t4, ALU.subtract if neg else ALU.add))

            tm = [ctmp[:, 64 * q:64 * q + 32] for q in range(4)]

            def small(q, k):
                return tm[q][:, 0:8 * k].rearrange("p (t a) -> p t a", a=PAIRS)

            for base in (1, 2, 4):
                w = [P, base, PAIRS]
                cmul(PWR[:, base + 1:2 * base + 1, :], PWI[:, base + 1:2 * base + 1, :],
                     bc(PWR[:, base:base + 1, :], w), bc(PWI[:, base:base + 1, :], w),
                     PWR[:, 1:base + 1, :], PWI[:, 1:base + 1, :], *[small(q, base) for q in range(4)])
            dve.tensor_copy(PDR[:, 0, :], PWR[:, 8, :])
            link(dve.tensor_copy(PDI[:, 0, :], PWI[:, 8, :]))
            for k in range(SCAN_STEPS - 1):
                cmul(PDR[:, k + 1:k + 2, :], PDI[:, k + 1:k + 2, :], PDR[:, k:k + 1, :], PDI[:, k:k + 1, :],
                     PDR[:, k:k + 1, :], PDI[:, k:k + 1, :], *[small(q, 1) for q in range(4)])
            w = [P, PAIRS, GCH]
            tb = [st4[:, 0:128].rearrange("p (a h) -> p a h", a=PAIRS) for st4 in TMP4]
            cmul(BBR, BBI, bc(sv[:, 22, :].unsqueeze(2), w), bc(sv[:, 23, :].unsqueeze(2), w), bre, bim, *tb)
            for i in range(CHUNK):
                dve.tensor_copy(RVR[:, i, :], PWR[:, CHUNK - 1 - i, :])
                ins = dve.tensor_copy(RVI[:, i, :], PWI[:, CHUNK - 1 - i, :])
            link(ins)
            w = [P, PAIRS, CHUNK, GCH]
            tv = [st4[:, 0:1024].rearrange("p (a i h) -> p a i h", a=PAIRS, i=CHUNK) for st4 in TMP4]
            cmul(VBR, VBI, bc(RVR.rearrange("p t a -> p a t").unsqueeze(3), w), bc(RVI.rearrange("p t a -> p a t").unsqueeze(3), w),
                 bc(BBR.unsqueeze(2), w), bc(BBI.unsqueeze(2), w), *tv)
            dve.tensor_copy(sv[:, 20, :], sv[:, 22, :]).then_inc(vb_ok, 1)
            cmul(CAR[:, :, 1:9, :], CAI[:, :, 1:9, :],
                 bc(PWR[:, 1:9, :].rearrange("p t a -> p a t").unsqueeze(3), w),
                 bc(PWI[:, 1:9, :].rearrange("p t a -> p a t").unsqueeze(3), w),
                 bc(CAR[:, :, 0:1, :], w), bc(CAI[:, :, 0:1, :], w), *tv, neg=True)
            dve.tensor_copy(sv[:, 21, :], sv[:, 22, :]).then_inc(ca_ok, 1)
            dve.wait_ge(set_in, 16 * SET_N)
            link(dve.tensor_scalar(nb31[:, :], b31[:, :], -1.0, None, ALU.mult))

            dve.wait_ge(unit_ev, LAST_UNIT[4] + 1)
            for c in range(2):
                dve.tensor_tensor(convh[:, c, :], convh[:, c, :], convo[:, c, :], ALU.mult).then_inc(h_ok, 1)
            dve.wait_ge(vin_ev, 4)
            dve.wait_ge(h_ok, 2)
            for j in range(TAPS - 1, -1, -1):
                s = TAPS - 1 - j
                for c in range(2):
                    acc = banks(2 - 2 * c, 2)
                    if s == 0:
                        ins = dve.tensor_scalar(acc, convh[:, c, :], convw[:, c, j:j + 1], None, ALU.mult)
                    else:
                        dve.wait_ge(tap_c, 2 * s - 1 + c)
                        ins = dve.scalar_tensor_tensor(acc[:, s:L], convh[:, c, 0:L - s], convw[:, c, j:j + 1],
                                                       acc[:, s:L], ALU.mult, ALU.add)
                    ins.then_inc(tap_c if s < TAPS - 1 else conv_ps, 1)
            dve.wait_ge(ud_ok, 1)
            for half in range(2):
                dve.wait_ge(y_ps, half + 1)
                for r in range(2):
                    src = bank(2 * r + half).rearrange("p (g j h) -> p j g h", g=4, j=CHUNK)
                    yv = yc[:, :, P * half:P * half + P].rearrange("p j (g r h) -> p r j g h", g=4, r=2)[:, r]
                    uv = uc[:, 8 * half:8 * half + 8].rearrange("p (g r) j h -> p r j g h", r=2)[:, r]
                    dve.tensor_tensor(yv, src, uv, ALU.add).then_inc(y_ev, 1)

            dve.wait_ge(band_ok, HEADS)

            def stats(k, m):
                h, i = ITEMS[k]
                nk = (i + 1) * P
                far = max(nk - 256, 0)
                sl = 2 * (k % 2) + m
                st_ = smx[:, k % 2, m, :]
                S = banks(2 * m, 2)
                dve.wait_ge(s_ps, 2 * k + m + 1)
                if k >= 2:
                    dve.wait_ge(pT_ps, k - 1)
                ins = dve.tensor_tensor_reduce(out=pexp[:, sl, far:nk], in0=S[:, far:nk], in1=band[:, h, 256 - (nk - far):256],
                                               scale=SCALE, scalar=-3e38, op0=ALU.add, op1=ALU.max, accum_out=st_[:, 0:1])
                if far:
                    link(dve.tensor_reduce(st_[:, 1:2], S[:, 0:far], AX.X, ALU.max))
                    link(dve.tensor_scalar(st_[:, 1:2], st_[:, 1:2], -SCALE, nb31[:, h:h + 1], ALU.mult, ALU.add))
                    link(dve.scalar_tensor_tensor(st_[:, 2:3], st_[:, 0:1], -1.0, st_[:, 1:2], ALU.mult, ALU.min))
                    dve.tensor_tensor(st_[:, 3:4], st_[:, 2:3], b31[:, h:h + 1], ALU.add).then_inc(nm_ok, 1)
                else:
                    link(ins)
                    dve.tensor_scalar(st_[:, 2:3], st_[:, 0:1], -1.0, None, ALU.mult).then_inc(nm_ok, 1)

            def combine(k):
                h, i = ITEMS[k]
                nk = (i + 1) * P
                far = nk > 256
                a, b = smx[:, k % 2, 0, :], smx[:, k % 2, 1, :]
                dve.wait_ge(e_ok, 2 * k + 2)
                if far:
                    dve.tensor_tensor(a[:, 4:5], a[:, 4:5], a[:, 5:6], ALU.add)
                    link(dve.tensor_tensor(b[:, 4:5], b[:, 4:5], b[:, 5:6], ALU.add))
                dve.reciprocal(a[:, 6:7], a[:, 4:5])
                link(dve.reciprocal(b[:, 6:7], b[:, 4:5]))
                dve.tensor_tensor(b[:, 7:8], b[:, 6:7], lam[:, 1:2], ALU.mult)
                p1, p2 = pexp[:, 2 * (k % 2), 0:nk], pexp[:, 2 * (k % 2) + 1, 0:nk]
                link(dve.tensor_scalar(p1, p1, a[:, 6:7], None, ALU.mult))
                dve.scalar_tensor_tensor(p1, p2, b[:, 7:8], p1, ALU.mult, ALU.add).then_inc(p_ok, 1)

            for k in range(ITERS + 2):
                if 1 <= k <= NI:
                    combine(k - 1)
                if k < NI:
                    stats(k, 0)
                    stats(k, 1)
                if k == 4:
                    dve.wait_ge(misc_ev, 4)
                    for i in range(NT):
                        ins = dve.bn_stats(lnst[:, i, :], convt[:, i, :])
                    link(ins)
                    for i in range(NT):
                        ins = dve.bn_aggr(lnmv[:, i, :], lnst[:, i, :])
                    link(ins)
                    dve.tensor_scalar(lnv[:, :], lnmv[:, :, 1], LN_EPS, None, ALU.add).then_inc(ln_var, 1)
                if k == 6:
                    dve.wait_ge(ln_rstd, 1)
                    for i in range(NT):
                        ins = dve.tensor_scalar(convt[:, i, :], convt[:, i, :], lnmv[:, i, 0:1], lnr[:, i:i + 1],
                                                ALU.subtract, ALU.mult)
                    ins.then_inc(ln_ok, 1)
                if 13 <= k < 17:
                    i = k - 13
                    c, half = i // 2, i % 2
                    dve.wait_ge(silu_t, i + 1)
                    link(dve.tensor_scalar(silu[:, i, :], silu[:, i, :], 0.5, 0.5, ALU.mult, ALU.add))
                    z = convo[:, c, 512 * half:512 * half + 512]
                    dve.tensor_tensor(z, z, silu[:, i, :], ALU.mult).then_inc(conv_ok, 1)
                if k == 19:
                    dve.wait_ge(misc_ev, 4 + 4 + 2 + 4)
                    gl = RG[:, 2048:4096]
                    link(dve.tensor_scalar(gl, gl, 0.5, 0.5, ALU.mult, ALU.add))
                    dve.tensor_tensor(RD[:, 6144:8192], RG[:, 4096:6144], gl, ALU.mult).then_inc(ssm_ok, 1)
                if k >= 10 and (k - 10) % NT == 0:
                    h = (k - 10) // NT
                    dve.wait_ge(head_ss, (h + 1) * NT)
                    dve.tensor_scalar(hssv[:, h, :], hss[:, h, :], 1.0 / DV, RMS_EPS, ALU.mult, ALU.add).then_inc(head_var, 1)

            for k in range(NT + 2):
                if k >= 2:
                    dve.wait_ge(lg_ps, k - 1)
                    dve.tensor_tensor(logit[:, k - 2, :], psum[:, 4, 0:36], rbias[:, :], ALU.add).then_inc(lg_ok, 1)
                if 1 <= k <= NT:
                    dve.wait_ge(h2T_ps, k)
                    for b in range(2):
                        ins = dve.tensor_tensor(h2T[:, 4 * b:4 * b + 4, :], bank(4 + b).rearrange("p (k n) -> p k n", k=4),
                                                bc(g2k[:, 4 * b:4 * b + 4].unsqueeze(2), [P, 4, P]), ALU.mult)
                    ins.then_inc(h2T_ok, 1)
                if k < NT:
                    dve.wait_ge(proj_ps, k + 1)
                    dve.wait_ge(xr_in, 16 * (k + 1))
                    if k == 0:
                        dve.wait_ge(ssm_ok, 1)
                    dve.tensor_tensor(x2[:, k, :], banks(2 * (k % 2), 2), xr[:, :], ALU.add).then_inc(x2_ok, 1)
                    dve.wait_ge(ms2_ok, k + 1)
                    dve.tensor_scalar(ms2v[:, k:k + 1], ms2[:, k:k + 1], 1.0 / D, RMS_EPS, ALU.mult, ALU.add).then_inc(ms2v_ok, 1)
                    dve.wait_ge(rstd2_ok, k + 1)
                    dve.tensor_scalar(mixT[:, :, k * P:(k + 1) * P], x2[:, k, :].rearrange("p (c n) -> p c n", c=KD),
                                      rstd2[:, k:k + 1], None, ALU.mult).then_inc(h2_ok, 1)

            dve.wait_ge(lg_ok, NT)
            dve.wait_ge(h2_out, 16 * NT)
            dve.wait_ge(const_ok, 4)
            g8, mx8, e8, me8 = (rrv(x, 64).rearrange("p (t n) -> p t n", t=NT) for x in ("g8", "mx8", "e8", "me8"))
            gi8 = rrv("gi8").bitcast(U32).rearrange("p (t n) -> p t n", t=NT)
            ei8 = rrv("ei8").bitcast(U32).rearrange("p (t n) -> p t n", t=NT)
            gix = rrv("gix")
            goh = rrv("goh").rearrange("p (t n) -> p t n", t=NT)
            gsum, den = rrv("gsum"), rrv("den")
            gexp = rrv("gexp").rearrange("p (t n) -> p t n", t=NT)
            gdif = rrv("gdif").rearrange("p (t n) -> p t n", t=NT)
            edif, eexp = rrv("edif"), rrv("eexp")
            gate = rrv("gate").rearrange("p (r t) -> p r t", r=2)
            idx = rrv("idx").rearrange("p (r t) -> p r t", r=2)
            rk, br_, ovs, blk, dst = (rrv(x, 16) for x in ("rk", "br_", "ovs", "blk", "dst"))
            tokm = rrv("tokm")
            link(dve.memset(g8, -3e38))
            link(dve.tensor_copy(g8[:, :, 0:4], logit[:, :, 0:4]))
            for i in range(NT):
                ins = dve.max(mx8[:, i, :], g8[:, i, :])
            link(ins)
            for i in range(NT):
                ins = dve.max_index(gi8[:, i, :], mx8[:, i, :], g8[:, i, :])
            dve.tensor_tensor(gdif, logit[:, :, 0:4], bc(mx8[:, :, 0:1], [P, NT, 4]), ALU.subtract)
            link(dve.tensor_copy(tokm, tokf[:, :]))
            link(dve.tensor_copy(gix.unsqueeze(2), gi8[:, :, 0:1]))
            link(dve.tensor_tensor(goh, bc(gix.unsqueeze(2), [P, NT, 4]), bc(iotaf[:, 0:4].unsqueeze(1), [P, NT, 4]), ALU.is_equal))
            es4 = esel.rearrange("p (t g n) -> p t g n", t=NT, g=4)
            link(dve.tensor_tensor(es4, logit[:, :, 4:36].rearrange("p t (g n) -> p t g n", g=4),
                                   bc(goh.unsqueeze(3), [P, NT, 4, 8]), ALU.mult))
            link(dve.tensor_reduce(e8, es4.rearrange("p t g n -> p t n g"), AX.X, ALU.add))
            for i in range(NT):
                ins = dve.max(me8[:, i, :], e8[:, i, :])
            link(ins)
            for i in range(NT):
                dve.max_index(ei8[:, i, :], me8[:, i, :], e8[:, i, :])
            dve.tensor_tensor(edif.unsqueeze(2), me8[:, :, 1:2], me8[:, :, 0:1], ALU.subtract).then_inc(gd_ok, 1)
            link(dve.memset(dst, 0.0))
            for r in range(2):
                link(dve.tensor_copy(idx[:, r, :].unsqueeze(2), ei8[:, :, r:r + 1]))
                link(dve.scalar_tensor_tensor(idx[:, r, :], gix, float(EPG), idx[:, r, :], ALU.mult, ALU.add))
            idx16 = idx.rearrange("p r t -> p (r t)")
            link(dve.tensor_tensor(MM, bc(idx16.unsqueeze(2), [P, 16, 32]), bc(iotaf[:, 0:32].unsqueeze(1), [P, 16, 32]), ALU.is_equal))
            dve.tensor_tensor(mbf, MM[:, 0:8, :], MM[:, 8:16, :], ALU.add).then_inc(mm_ok, 1)
            dve.wait_ge(ge_ok, 1)
            dve.tensor_reduce(gsum, gexp, AX.X, ALU.add)
            link(dve.tensor_scalar(den, eexp, 1.0, None, ALU.add))
            link(dve.tensor_tensor(den, den, gsum, ALU.mult))
            link(dve.reciprocal(gate[:, 0, :], den))
            link(dve.tensor_tensor(gate[:, 1, :], gate[:, 0, :], eexp, ALU.mult))
            dve.wait_ge(rank_ps, 1)
            dve.tensor_copy(RK[:, :, :].rearrange("p t n -> p (t n)"), bank(0)[:, 0:256])
            cnt = ovt[:, 0:32]
            link(dve.tensor_copy(cnt, bank(1)[:, 0:32]))
            for r in range(2):
                dve.tensor_tensor(MP[:, 8 * r:8 * r + 8, :], MM[:, 8 * r:8 * r + 8, :], RK, ALU.mult)
            nvt = ovt[:, 64:64 + 224].rearrange("p (n j) -> p n j", j=7)
            link(dve.tensor_tensor(nvt, bc(cnt.unsqueeze(2), [P, 32, 7]), bc(thr[:, :].unsqueeze(1), [P, 32, 7]), ALU.is_gt))
            dve.tensor_reduce(rk, MP, AX.X, ALU.add)
            nov_e, ovend, ovstart = ovt[:, 32:64], ovt[:, 288:320], ovt[:, 320:352]
            link(dve.tensor_reduce(nov_e, nvt, AX.X, ALU.add))
            jt = ovt[:, 352:464].rearrange("p (n j) -> p n j", j=7)
            dve.tensor_tensor(jt, bc(rk.unsqueeze(2), [P, 16, 7]), bc(thr[:, :].unsqueeze(1), [P, 16, 7]), ALU.is_ge)
            link(dve.memset(ovt[:, 464:496], 1.0))
            link(dve.tensor_tensor_scan(ovend, ovt[:, 464:496], nov_e, 0.0, ALU.mult, ALU.add))
            dve.tensor_reduce(br_, jt, AX.X, ALU.add)
            link(dve.tensor_tensor(ovstart, ovend, nov_e, ALU.subtract))
            link(dve.tensor_tensor(MP, MM, bc(ovstart.unsqueeze(1), [P, 16, 32]), ALU.mult))
            dve.scalar_tensor_tensor(rk, br_, -float(P), rk, ALU.mult, ALU.add)
            link(dve.tensor_reduce(ovs, MP, AX.X, ALU.add))
            link(dve.tensor_tensor(blk, ovs, br_, ALU.add))
            link(dve.tensor_tensor(blk, blk, idx16, ALU.add))
            dve.tensor_scalar(tokm, tokf[:, :], OOB, None, ALU.subtract)
            dve.tensor_scalar(dst[:, 0:8], tokf[:, :], 2.0, OOB, ALU.mult, ALU.subtract)
            link(dve.tensor_scalar(dst[:, 8:16], tokf[:, :], 2.0, OOB - 1.0, ALU.mult, ALU.subtract))
            gates = gate.rearrange("p r t -> p (r t)")
            for r in range(2):
                c = slice(8 * r, 8 * r + 8)
                dve.tensor_tensor(slot1h[:, c], bc(rk[:, c].unsqueeze(2), [P, 8, P]), bc(iotaf[:, :].unsqueeze(1), [P, 8, P]), ALU.is_equal)
                link(dve.tensor_tensor(blk1h[:, c], bc(blk[:, c].unsqueeze(2), [P, 8, NBLK]), bc(iotaf[:, 0:NBLK].unsqueeze(1), [P, 8, NBLK]), ALU.is_equal))
                dve.tensor_tensor(bval[:, c, :, 0], blk1h[:, c], bc(tokm.unsqueeze(2), [P, 8, NBLK]), ALU.mult)
                dve.tensor_tensor(bval[:, c, :, 1], blk1h[:, c], bc(dst[:, c].unsqueeze(2), [P, 8, NBLK]), ALU.mult)
                dve.tensor_tensor(bval[:, c, :, 2], blk1h[:, c], bc(gates[:, c].unsqueeze(2), [P, 8, NBLK]), ALU.mult).then_inc(tab_ok, 1)
            endf = ovt[:, 192:224]
            link(dve.scalar_tensor_tensor(endf, ovend, 1.0, iotaf[:, 0:EXPERTS], ALU.add, ALU.add))
            novh, novs = ovt[:, 16:24], ovt[:, 24:25]
            evens = iotaf[:, 0:NOVER].rearrange("p (b two) -> p b two", two=2)[:, :, 0:1]
            link(dve.tensor_tensor(novh.unsqueeze(2), bc(ovend[:, 31:32].unsqueeze(1), [P, NOVER // 2, 1]), evens, ALU.is_gt))
            link(dve.tensor_reduce(novs, novh, AX.X, ALU.add))
            dve.tensor_scalar(nov_i[:, :], novs, 2.0, None, ALU.mult)
            eo = ovt[:, 64:64 + 2 * (NB + 1)].rearrange("p (b two) -> p b two", two=2)
            before = RD[:, before0:before0 + (NB + 1) * EXPERTS].rearrange("p (b n) -> p b n", b=NB + 1)
            link(dve.tensor_tensor(before, bc(endf.unsqueeze(1), [P, NB + 1, EXPERTS]), bc(iotaf[:, 0:NB + 1].unsqueeze(2), [P, NB + 1, EXPERTS]), ALU.is_le))
            link(dve.tensor_reduce(eo, before.rearrange("p b (n two) -> p b two n", two=2), AX.X, ALU.add))
            link(dve.tensor_scalar(eo[:, :, 1], eo[:, :, 1], float(EXPERTS // 2 - 1), None, ALU.min))
            dve.tensor_copy(ends[:, :], endf)
            dve.tensor_tensor(blkx[:, 0, :], eo[:, :, 0], eo[:, :, 1], ALU.subtract)
            dve.tensor_scalar(blkx[:, 1, :], eo[:, :, 1], 1.0, None, ALU.add)
            dve.tensor_scalar(blkx[:, 2, :], eo[:, :, 0], 1.0, None, ALU.max)
            dve.wait_ge(tab_ps, 1)
            tab = bank(2)[:, 0:3 * NBLK].rearrange("p (n v) -> p v n", v=3)
            dve.tensor_scalar(tabi[:, :, :], tab[:, 0:2, :], OOB, None, ALU.add)
            dve.tensor_copy(tabg[:, :], tab[:, 2, :]).then_inc(idx_ok, 1)

            def xT_evac(v):
                dve.wait_ge(ex_xT, v)
                for b in range(2):
                    ins = dve.tensor_tensor(xgT[:, 4 * b:4 * b + 4, :], bank(b).rearrange("p (k n) -> p k n", k=4),
                                            bc(g2e[:, 4 * b:4 * b + 4].unsqueeze(2), [P, 4, P]), ALU.mult)
                ins.then_inc(ex_xTe, 1)

            def act_mul(v):
                dve.wait_ge(ex_u, v)
                dve.wait_ge(ex_s, v)
                dve.tensor_tensor(actb, bank(3), actb, ALU.mult).then_inc(ex_a, 1)

            def gate_low(b):
                at = slice(b, b + 1) if isinstance(b, int) else bass.ds(b, 1)
                slot = dve.value_load(blkx[0:1, 0, at], min_val=0, max_val=1)
                base = dve.snap(slot * (2 * KD * FF))
                for q in range(2):
                    dve.wait_ge(ex_gh, 4 * b + q + 1 if isinstance(b, int) else dve.snap(b * 4 + (q + 1)))
                    dve.tensor_tensor(wg_lo[:, D * q:D * q + D], RAB[:, bass.ds(base + D * q, D)], wg_hi[:, D * q:D * q + D],
                                      ALU.subtract).then_inc(ex_gl, 1)

            def split_low(b, b1):
                at = slice(b, b + 1) if isinstance(b, int) else bass.ds(b, 1)
                slot = dve.value_load(blkx[0:1, 0, at], min_val=0, max_val=1)
                base = dve.snap(slot * (FK * D))
                first = isinstance(b, int) and b == 0
                for k in range(FK):
                    dve.wait_ge(ex_wh, k + 1 if first else (b * FK + k + 1 if isinstance(b, int) else dve.snap(b * FK + (k + 1))))
                    dve.tensor_tensor(wd_lo[:, D * k:D * k + D], RCE[:, bass.ds(base + D * k, D)], wd_hi[:, D * k:D * k + D],
                                      ALU.subtract).then_inc(ex_wl, 1)
                dve.wait_ge(ex_aTe, b1)
                dve.tensor_tensor(actT_lo, bank(4), actT_hi, ALU.subtract).then_inc(ex_aTl, 1)

            def y_half(s, b, down, scat, done):
                g = tabg[:, b:b + 1] if isinstance(b, int) else tabg[:, bass.ds(b, 1)]
                dve.wait_ge(ex_y, down)
                if scat is not None:
                    dve.wait_ge(scat_out[s], scat)
                dve.tensor_scalar(yb[s][:, 512:1024], bank(6), g, None, ALU.mult).then_inc(done, 1)

            def step(j, s):
                first = isinstance(j, int) and j == 0 and s == 0
                b, prev, b1, b2 = j * 2 + s, j * 2 + s - 1, j * 2 + s + 1, j * 2 + s + 2
                scat = (j - 1 + s) * 16
                if not isinstance(b, int):
                    b, prev, b1, b2, scat = [dve.snap(v) for v in (b, prev, b1, b2, scat)]
                if not first:
                    split_low(prev, b)
                act_mul(b1)
                xT_evac(b2)
                gate_low(b1)
                if not first:
                    y_half(1 - s, prev, b, None if isinstance(scat, int) and scat == 0 else scat, ex_y1)

            xT_evac(1)
            gate_low(0)
            for j in range(2):
                for s in range(2):
                    step(j, s)
            with dve.Fori(2, EXPERTS // 2) as j:
                for s in range(2):
                    step(j, s)
            nov = dve.value_load(nov_i[0:1, 0:1], min_val=0, max_val=NOVER)
            for b in range(0, NOVER, 2):
                with dve.If(nov > b):
                    for s in range(2):
                        step((EXPERTS + b) // 2, s)
            blocks, last = dve.snap(nov + EXPERTS), dve.snap(nov + (EXPERTS - 1))
            scat = dve.snap(nov * 8 + 16 * (EXPERTS // 2 - 1))
            y_half(1, last, blocks, scat, tail_y)
            dve.wait_ge(x2_back, 16)
            for i in range(NT + 1):
                if i < NT:
                    x3 = banks(2 * (i % 3), 2)
                    dve.wait_ge(ya_ps, i + 1)
                    dve.tensor_tensor(x3, x3, y2t[:, i % 4, 1, :], ALU.add).then_inc(fin_c, 1)
                    dve.wait_ge(fin_c, i + 1)
                    dve.tensor_tensor(x3, x3, x2[:, i, :], ALU.add).then_inc(x3_ok, 1)
                if i >= 1:
                    if i == 1:
                        dve.wait_ge(fg_in, 16)
                    dve.wait_ge(ms3_ok, i)
                    dve.tensor_scalar(ms3v[:, i - 1:i], ms3[:, i - 1:i], 1.0 / D, RMS_EPS, ALU.mult, ALU.add).then_inc(ms3v_ok, 1)
                    dve.wait_ge(rstd3_ok, i)
                    dve.scalar_tensor_tensor(x2[:, i - 1, :], banks(2 * ((i - 1) % 3), 2), rstd3[:, i - 1:i], fgb,
                                             ALU.mult, ALU.mult).then_inc(fin_ok, 1)


_INS = ["x", "rel_bias", "ln1_g", "w_in", "lam_q1", "lam_k1", "lam_q2", "lam_k2", "subln_g", "conv_w", "conv_b",
        "conv_ln_g", "conv_ln_b", "ssm_lam_re", "ssm_lam_im", "ssm_log_dt", "ssm_b_re", "ssm_b_im", "ssm_c_re",
        "ssm_c_im", "ssm_d", "ssm_glu_w", "ssm_glu_b", "w_out", "ln2_g", "group_router_w", "group_router_b",
        "expert_router_w", "expert_router_b", "w_gate", "w_up", "w_down", "final_g"]


def bucket_onehot():
    rel = 255 - np.arange(384)
    n = np.maximum(rel, 0)
    exact = BUCKETS // 2
    nf = np.maximum(n, 1).astype(np.float32)
    large = exact + (np.log(nf / np.float32(exact)) / np.float32(math.log(128 / exact))
                     * np.float32(BUCKETS - exact)).astype(np.int32)
    bucket = np.where(n < exact, n, np.minimum(large, BUCKETS - 1))
    return ((bucket[None, :] == np.arange(BUCKETS)[:, None]) & (rel >= 0)[None, :]).astype(np.float32)


def kernel(**inputs):
    import concourse.bacc as bacc
    from concourse.bass_utils import run_bass_kernel_spmd

    nc = bacc.Bacc("TRN2", target_bir_lowering=False, num_devices=1)
    arrays, t = {}, {}
    for name in _INS:
        arrays[f"in_{name}"] = np.ascontiguousarray(inputs[name])
    arrays["in_bucket_onehot"] = bucket_onehot()
    for key, a in arrays.items():
        t[key[3:]] = nc.dram_tensor(key, a.shape, mybir.dt.from_np(a.dtype), kind="ExternalInput").ap()
    t["out"] = nc.dram_tensor("out", (1, L, D), F32, kind="ExternalOutput").ap()
    build(nc, t)
    r = run_bass_kernel_spmd(nc, [arrays], core_ids=[0])
    return r.results[0]["out"]
```
